# Optimizing a Trainium2 kernel written in Bass

```python
import jax, jax.numpy as jnp
from jax import lax
import numpy as np
import math
import jax
import jax.numpy as jnp

D_MODEL = 1024
BATCH = 1
SEQ = 256
DEPTH = 2

N_MIXERS = 3
HEAD_DIM = 64
EPS = 1e-6
NEG_INF = -1e30

A_HEADS = D_MODEL // HEAD_DIM
A_WINDOWS = (128, 512, 2048)
A_DILATIONS = (1, 4, 16)
A_GROUPS = len(A_WINDOWS)
ROPE_THETA = 500000.0
ROPE_DIMS = HEAD_DIM // 4

B_CONV_WIDTH = 3

C_Q_HEADS = D_MODEL // HEAD_DIM
C_KV_HEADS = 4
C_THETA = 10000.0
Q_BLOCK = 128
GRID_W = 64

D_FF = 4 * D_MODEL

N_A = len(range(0, DEPTH, N_MIXERS))
N_B = len(range(1, DEPTH, N_MIXERS))
N_C = len(range(2, DEPTH, N_MIXERS))


def rms_norm(x, g):
    xf = x.astype(jnp.float32)
    y = xf * lax.rsqrt(jnp.mean(xf * xf, axis=-1, keepdims=True) + EPS)
    return (y * g.astype(jnp.float32)).astype(x.dtype)

def rope_angles(pos, dim, theta):
    inv = theta ** (-jnp.arange(0, dim, 2, dtype=jnp.float32) / dim)
    ang = pos.astype(jnp.float32)[:, None] * inv[None, :]
    return jnp.cos(ang), jnp.sin(ang)

def apply_rope(x, cos, sin):
    half = x.shape[-1] // 2
    xf = x.astype(jnp.float32)
    x1, x2 = xf[..., :half], xf[..., half:]
    c, s = cos[:, None, :], sin[:, None, :]
    return jnp.concatenate([x1 * c - x2 * s, x2 * c + x1 * s], axis=-1).astype(x.dtype)

def partial_rope(x, cos, sin):
    return jnp.concatenate([apply_rope(x[..., :ROPE_DIMS], cos, sin), x[..., ROPE_DIMS:]], axis=-1)

def dilated_group(q, k, v, dilation, radius):
    B, S, H, Dh = q.shape
    L = S // dilation
    nb = -(-L // radius)
    Lp = nb * radius

    def split(t):
        t = jnp.moveaxis(t.reshape(B, L, dilation, H, Dh), 2, 1)
        return jnp.pad(t, ((0, 0), (0, 0), (0, Lp - L), (0, 0), (0, 0)))

    def band(t):
        tp = jnp.pad(t, ((0, 0), (0, 0), (radius, radius), (0, 0), (0, 0)))
        tb = tp.reshape(B, dilation, nb + 2, radius, H, Dh)
        return jnp.concatenate([tb[:, :, :-2], tb[:, :, 1:-1], tb[:, :, 2:]], axis=3)

    qb = split(q).reshape(B, dilation, nb, radius, H, Dh)
    kb = band(split(k))
    vb = band(split(v))

    q_idx = jnp.arange(Lp).reshape(nb, radius)
    k_idx = jnp.arange(nb)[:, None] * radius - radius + jnp.arange(3 * radius)[None, :]
    mask = ((jnp.abs(q_idx[:, :, None] - k_idx[:, None, :]) <= radius)
            & (k_idx[:, None, :] >= 0) & (k_idx[:, None, :] < L))

    s = jnp.einsum('bdnqhe,bdnkhe->bdnqhk', qb, kb).astype(jnp.float32) * (HEAD_DIM ** -0.5)
    s = jnp.where(mask[None, None, :, :, None, :], s, NEG_INF)
    mx = jnp.max(s, axis=-1)
    p = jnp.exp(s - mx[..., None])
    den = jnp.sum(p, axis=-1)
    num = jnp.einsum('bdnqhk,bdnkhe->bdnqhe', p, vb.astype(jnp.float32))

    def unsplit(t):
        rest = t.shape[4:]
        t = t.reshape((B, dilation, Lp) + rest)[:, :, :L]
        return jnp.moveaxis(t, 1, 2).reshape((B, S) + rest)

    return unsplit(num), unsplit(den), unsplit(mx)

def mixer_a(h, w_qkv, q_gain, k_gain, w_o, cos, sin):
    B, S, _ = h.shape
    qkv = (h @ w_qkv).reshape(B, S, A_GROUPS, 3, A_HEADS, HEAD_DIM)
    nums, dens, mxs = [], [], []
    for g in range(A_GROUPS):
        dil = A_DILATIONS[g]
        radius = A_WINDOWS[g] // (2 * dil)
        q = partial_rope(rms_norm(qkv[:, :, g, 0], q_gain[g]), cos, sin)
        k = partial_rope(rms_norm(qkv[:, :, g, 1], k_gain[g]), cos, sin)
        v = qkv[:, :, g, 2]
        num, den, mx = dilated_group(q, k, v, dil, radius)
        nums.append(num); dens.append(den); mxs.append(mx)
    mx = jnp.stack(mxs, 0)
    wts = jnp.exp(mx - jnp.max(mx, axis=0, keepdims=True))
    num = jnp.sum(wts[..., None] * jnp.stack(nums, 0), axis=0)
    den = jnp.sum(wts * jnp.stack(dens, 0), axis=0)
    o = (num / den[..., None]).astype(h.dtype).reshape(B, S, D_MODEL)
    return o @ w_o

def mixer_b(h, w_in, conv_w, w_out):
    b_gate, c_gate, xt = jnp.split(h @ w_in, 3, axis=-1)
    u = c_gate * xt
    y = lax.conv_general_dilated(u, conv_w[:, None, :].astype(u.dtype), window_strides=(1,),
                                 padding=((1, 1),), dimension_numbers=('NWC', 'WIO', 'NWC'),
                                 feature_group_count=D_MODEL)
    return (b_gate * y) @ w_out

def axial_rope(x, cos_r, sin_r, cos_c, sin_c):
    half = HEAD_DIM // 2
    return jnp.concatenate([apply_rope(x[..., :half], cos_r, sin_r),
                            apply_rope(x[..., half:], cos_c, sin_c)], axis=-1)

def mixer_c(h, w_qkv, q_gain, k_gain, w_o):
    B, S, _ = h.shape
    rows = S // GRID_W
    row_id = jnp.repeat(jnp.arange(rows), GRID_W)
    col_id = jnp.tile(jnp.arange(GRID_W), rows)
    cos_r, sin_r = rope_angles(row_id, HEAD_DIM // 2, C_THETA)
    cos_c, sin_c = rope_angles(col_id, HEAD_DIM // 2, C_THETA)

    qkv = h @ w_qkv
    nq, nk = C_Q_HEADS * HEAD_DIM, C_KV_HEADS * HEAD_DIM
    q = qkv[..., :nq].reshape(B, S, C_Q_HEADS, HEAD_DIM)
    k = qkv[..., nq:nq + nk].reshape(B, S, C_KV_HEADS, HEAD_DIM)
    v = qkv[..., nq + nk:].reshape(B, S, C_KV_HEADS, HEAD_DIM)
    q = axial_rope(rms_norm(q, q_gain), cos_r, sin_r, cos_c, sin_c)
    k = axial_rope(rms_norm(k, k_gain), cos_r, sin_r, cos_c, sin_c)

    grp = C_Q_HEADS // C_KV_HEADS
    nblk = S // Q_BLOCK
    qb = jnp.moveaxis(q.reshape(B, nblk, Q_BLOCK, C_KV_HEADS, grp, HEAD_DIM), 1, 0)

    def attend(qblk):
        s = jnp.einsum('bqhgd,bkhd->bhgqk', qblk, k).astype(jnp.float32) * (HEAD_DIM ** -0.5)
        p = jax.nn.softmax(s, axis=-1)
        return jnp.einsum('bhgqk,bkhd->bqhgd', p.astype(v.dtype), v)

    o = lax.map(attend, qb)
    o = jnp.moveaxis(o, 0, 1).reshape(B, S, D_MODEL)
    return o @ w_o

def mlp_sq_relu(h, w1, w2):
    return jnp.square(jax.nn.relu(h @ w1)) @ w2

def first_inputs(seed: int = 0) -> dict:
    key = jax.random.key(seed)
    ks = jax.random.split(key, 20)
    D, Dh = D_MODEL, HEAD_DIM
    nrm = lambda k, shape, fan_in: jax.random.normal(k, shape, jnp.float32) * (fan_in ** -0.5)
    gain = lambda k, shape: 1.0 + 0.02 * jax.random.normal(k, shape, jnp.float32)
    c_cols = (C_Q_HEADS + 2 * C_KV_HEADS) * Dh
    return {
        "x": jax.random.normal(ks[0], (BATCH, SEQ, D), jnp.float32),
        "norm1": gain(ks[1], (DEPTH, D)),
        "norm2": gain(ks[2], (DEPTH, D)),
        "a_wqkv": nrm(ks[3], (N_A, D, A_GROUPS * 3 * D), D),
        "a_q_gain": gain(ks[4], (N_A, A_GROUPS, Dh)),
        "a_k_gain": gain(ks[5], (N_A, A_GROUPS, Dh)),
        "a_wo": nrm(ks[6], (N_A, D, D), D),
        "b_win": nrm(ks[7], (N_B, D, 3 * D), D),
        "b_conv": nrm(ks[8], (N_B, B_CONV_WIDTH, D), B_CONV_WIDTH),
        "b_wout": nrm(ks[9], (N_B, D, D), D),
        "c_wqkv": nrm(ks[10], (N_C, D, c_cols), D),
        "c_q_gain": gain(ks[11], (N_C, Dh)),
        "c_k_gain": gain(ks[12], (N_C, Dh)),
        "c_wo": nrm(ks[13], (N_C, D, D), D),
        "mlp_w1": nrm(ks[14], (DEPTH, D, D_FF), D),
        "mlp_w2": nrm(ks[15], (DEPTH, D_FF, D), D_FF),
    }

def first_block(x, norm1, norm2, a_wqkv, a_q_gain, a_k_gain, a_wo, b_win, b_conv, b_wout,
              c_wqkv, c_q_gain, c_k_gain, c_wo, mlp_w1, mlp_w2):
    S = x.shape[1]
    cos, sin = rope_angles(jnp.arange(S), ROPE_DIMS, ROPE_THETA)
    h = x
    for i in range(DEPTH):
        kind, j = i % N_MIXERS, i // N_MIXERS
        y = rms_norm(h, norm1[i])
        if kind == 0:
            y = mixer_a(y, a_wqkv[j], a_q_gain[j], a_k_gain[j], a_wo[j], cos, sin)
        elif kind == 1:
            y = mixer_b(y, b_win[j], b_conv[j], b_wout[j])
        else:
            y = mixer_c(y, c_wqkv[j], c_q_gain[j], c_k_gain[j], c_wo[j])
        h = h + y
        h = h + mlp_sq_relu(rms_norm(h, norm2[i]), mlp_w1[i], mlp_w2[i])
    return h


CHUNK = 64
RET_HEADS = 4
RET_DK = 64
RET_DV = 64
RET_THETA = 10000.0
DIFF_HEADS = 4
DIFF_DK = 64
DIFF_DV = 2 * DIFF_DK
ROPE_DIMS_2 = DIFF_DK // 4
GLA_HEADS = 4
GLA_DK = 32
GLA_DV = 64
GLA_RANK = 16
GLA_TAU = 16.0
RET_W = RET_HEADS * RET_DV
DIFF_W = DIFF_HEADS * DIFF_DV
GLA_W = GLA_HEADS * GLA_DV
MIX_WIDTH = RET_W + DIFF_W + GLA_W
IN_SPLITS = (RET_HEADS * RET_DK, RET_HEADS * RET_DK, RET_W, RET_W,
             DIFF_HEADS * 2 * DIFF_DK, DIFF_HEADS * 2 * DIFF_DK, DIFF_W,
             GLA_HEADS * GLA_DK, GLA_HEADS * GLA_DK, GLA_W, GLA_RANK, GLA_W)
IN_WIDTH = sum(IN_SPLITS)
N_EXPERTS = 32
N_GROUPS = 8
EXPERTS_PER_GROUP = N_EXPERTS // N_GROUPS
TOP_K = 2
GROUP_SCORE_K = 2
D_EXPERT = 512
MOE_BLOCK = 256


def rms_norm_2(x, g):
    x32 = x.astype(jnp.float32)
    y = x32 * lax.rsqrt(jnp.mean(x32 * x32, axis=-1, keepdims=True) + EPS)
    return (y * g.astype(jnp.float32)).astype(x.dtype)

def split_cols(p, sizes):
    idx = np.cumsum(np.array(sizes))[:-1].tolist()
    return jnp.split(p, idx, axis=-1)

def apply_rotary(x, positions, theta, rot_dims):
    half = rot_dims // 2
    inv_freq = 1.0 / (theta ** (jnp.arange(half, dtype=jnp.float32) / half))
    ang = positions.astype(jnp.float32)[..., None] * inv_freq
    cos = jnp.cos(ang)[:, :, None, :]
    sin = jnp.sin(ang)[:, :, None, :]
    xr = x[..., :rot_dims].astype(jnp.float32)
    x1, x2 = xr[..., :half], xr[..., half:]
    rot = jnp.concatenate([x1 * cos - x2 * sin, x1 * sin + x2 * cos], axis=-1).astype(x.dtype)
    return jnp.concatenate([rot, x[..., rot_dims:]], axis=-1)

def retention(q, k, v, positions):
    B_, S_, H, dk = q.shape
    dv = v.shape[-1]
    n_c = S_ // CHUNK
    q = apply_rotary(q, positions, RET_THETA, dk)
    k = apply_rotary(k, positions, RET_THETA, dk) * (dk ** -0.5)
    log_g = jnp.log(1.0 - 2.0 ** (-5.0 - jnp.arange(H, dtype=jnp.float32)))
    j = jnp.arange(CHUNK, dtype=jnp.float32)
    intra_decay = jnp.exp(log_g[:, None, None] * jnp.abs(j[:, None] - j[None, :]))
    q_decay = jnp.exp(log_g[:, None] * (j + 1.0))
    k_decay = jnp.exp(log_g[:, None] * (CHUNK - 1.0 - j))
    chunk_decay = jnp.exp(log_g * CHUNK)
    qc = q.reshape(B_, n_c, CHUNK, H, dk)
    kc = k.reshape(B_, n_c, CHUNK, H, dk)
    vc = v.reshape(B_, n_c, CHUNK, H, dv)
    scores = jnp.einsum('bnthd,bnshd->bnhts', qc, kc) * intra_decay
    intra = jnp.einsum('bnhts,bnshe->bnthe', scores, vc)
    kv = jnp.einsum('bnshd,hs,bnshe->bnhde', kc, k_decay, vc)

    def step(state, kv_i):
        return state * chunk_decay[None, :, None, None] + kv_i, state

    init = jnp.zeros((B_, H, dk, dv), kv.dtype)
    _, prev = lax.scan(step, init, jnp.moveaxis(kv, 1, 0))
    prev = jnp.moveaxis(prev, 0, 1)
    cross = jnp.einsum('bnthd,ht,bnhde->bnthe', qc, q_decay, prev)
    return (intra + cross).reshape(B_, S_, H, dv)

def diff_attention(q, k, v, positions, q_g, k_g, lq1, lk1, lq2, lk2, sub_g, lam_init):
    B_, S_, H, _, dk = q.shape
    dv = v.shape[-1]
    q = rms_norm_2(q, q_g)
    k = rms_norm_2(k, k_g)
    q = apply_rotary(q.reshape(B_, S_, 2 * H, dk), positions, ROPE_THETA, ROPE_DIMS_2)
    q = q.reshape(B_, S_, H, 2, dk) * (dk ** -0.5)
    k = apply_rotary(k.reshape(B_, S_, 2 * H, dk), positions, ROPE_THETA, ROPE_DIMS_2)
    k = k.reshape(B_, S_, H, 2, dk)
    lam = (jnp.exp(jnp.sum((lq1 * lk1).astype(jnp.float32)))
           - jnp.exp(jnp.sum((lq2 * lk2).astype(jnp.float32))) + lam_init)
    n_q = S_ // Q_BLOCK
    key_chunk = jnp.arange(S_) // CHUNK
    qb = jnp.swapaxes(q.reshape(B_, n_q, Q_BLOCK, H, 2, dk), 0, 1)

    def block(args):
        qi, bi = args
        s = jnp.einsum('bqhcd,bkhcd->bhcqk', qi, k).astype(jnp.float32)
        q_chunk = (bi * Q_BLOCK + jnp.arange(Q_BLOCK)) // CHUNK
        mask = key_chunk[None, :] <= q_chunk[:, None]
        p = jax.nn.softmax(jnp.where(mask, s, -jnp.inf), axis=-1)
        a = p[:, :, 0] - lam * p[:, :, 1]
        return jnp.einsum('bhqk,bkhe->bqhe', a.astype(v.dtype), v)

    o = lax.map(block, (qb, jnp.arange(n_q)))
    o = jnp.swapaxes(o, 0, 1).reshape(B_, S_, H, dv)
    return rms_norm_2(o, sub_g) * (1.0 - lam_init)

def gated_linear_attention(q, k, v, log_a):
    B_, S_, H, dk = q.shape
    dv = v.shape[-1]
    n_c = S_ // CHUNK
    q = q * (dk ** -0.5)
    to_chunks = lambda t: jnp.swapaxes(t.reshape(B_, n_c, CHUNK, H, t.shape[-1]), 0, 1)

    def step(state, inp):
        qi, ki, vi, la = inp
        g = jnp.cumsum(la.astype(jnp.float32), axis=1)
        dmat = jnp.exp(-jnp.abs(g[:, :, None] - g[:, None, :]))
        a = jnp.einsum('bthd,bshd,btshd->bhts', qi, ki, dmat)
        o = (jnp.einsum('bhts,bshe->bthe', a, vi)
             + jnp.einsum('bthd,bhde->bthe', qi * jnp.exp(g), state))
        g_last = g[:, -1]
        k_dec = ki * jnp.exp(g_last[:, None] - g)
        state = jnp.exp(g_last)[..., None] * state + jnp.einsum('bshd,bshe->bhde', k_dec, vi)
        return state, o

    init = jnp.zeros((B_, H, dk, dv), jnp.float32)
    _, o = lax.scan(step, init, (to_chunks(q), to_chunks(k), to_chunks(v), to_chunks(log_a)))
    return jnp.swapaxes(o, 0, 1).reshape(B_, S_, H, dv)

def route(h, router_w, router_b):
    t = h.shape[0]
    scores = jax.nn.sigmoid((h @ router_w).astype(jnp.float32))
    biased = scores + router_b.astype(jnp.float32)
    grp = biased.reshape(t, N_GROUPS, EXPERTS_PER_GROUP)
    group_score = jnp.sum(lax.top_k(grp, GROUP_SCORE_K)[0], axis=-1)
    g_sel = jnp.argmax(group_score, axis=-1)
    in_group = (jnp.arange(N_EXPERTS) // EXPERTS_PER_GROUP)[None, :] == g_sel[:, None]
    _, idx = lax.top_k(jnp.where(in_group, biased, -jnp.inf), TOP_K)
    w = jnp.take_along_axis(scores, idx, axis=-1)
    return idx, w / jnp.sum(w, axis=-1, keepdims=True)

def moe(h, idx, gates, w_gate, w_up, w_down):
    t, d = h.shape
    n_a = t * TOP_K
    e_flat = idx.reshape(n_a)
    tok_flat = jnp.repeat(jnp.arange(t, dtype=jnp.int32), TOP_K)
    g_flat = gates.reshape(n_a)
    order = jnp.argsort(e_flat)
    e_s, tok_s, g_s = e_flat[order], tok_flat[order], g_flat[order]
    counts = jnp.bincount(e_flat, length=N_EXPERTS)
    starts = jnp.cumsum(counts) - counts
    padded = ((counts + MOE_BLOCK - 1) // MOE_BLOCK) * MOE_BLOCK
    pad_ends = jnp.cumsum(padded)
    pad_starts = pad_ends - padded
    dest = pad_starts[e_s] + jnp.arange(n_a) - starts[e_s]
    n_blocks = -(-n_a // MOE_BLOCK) + N_EXPERTS
    p_len = n_blocks * MOE_BLOCK
    tok_buf = jnp.full((p_len,), t, jnp.int32).at[dest].set(tok_s)
    gate_buf = jnp.zeros((p_len,), g_s.dtype).at[dest].set(g_s)
    block_expert = jnp.minimum(
        jnp.searchsorted(pad_ends, jnp.arange(n_blocks) * MOE_BLOCK, side='right'), N_EXPERTS - 1)
    h_pad = jnp.concatenate([h, jnp.zeros((1, d), h.dtype)], axis=0)

    def expert_block(args):
        toks, gts, e = args
        xb = h_pad[toks]
        u = jax.nn.silu(xb @ w_gate[e]) * (xb @ w_up[e])
        return (u @ w_down[e]) * gts[:, None].astype(xb.dtype)

    y = lax.map(expert_block, (tok_buf.reshape(n_blocks, MOE_BLOCK),
                               gate_buf.reshape(n_blocks, MOE_BLOCK), block_expert))
    out = jnp.zeros((t + 1, d), y.dtype).at[tok_buf].add(y.reshape(p_len, d))
    return out[:t]

def second_inputs(seed: int = 0) -> dict:
    key = jax.random.key(seed)
    ks = jax.random.split(key, 26)
    f32 = jnp.float32
    nrm = lambda k, shape, s: jax.random.normal(k, shape, f32) * s
    gain = lambda k, shape: 1.0 + 0.02 * jax.random.normal(k, shape, f32)
    x = jax.random.normal(ks[0], (BATCH, SEQ, D_MODEL), f32)
    c = jax.random.normal(ks[1], (BATCH, D_MODEL), f32)
    offsets = jax.random.randint(ks[2], (BATCH, 1), 0, 1024) * CHUNK
    positions = (offsets + jnp.arange(SEQ, dtype=jnp.int32)[None, :]).astype(jnp.int32)
    return {
        "x": x,
        "c": c,
        "positions": positions,
        "w_mod": nrm(ks[3], (DEPTH, D_MODEL, 6 * D_MODEL), 0.01),
        "b_mod": nrm(ks[4], (DEPTH, 6 * D_MODEL), 0.02),
        "norm1_g": gain(ks[5], (DEPTH, D_MODEL)),
        "norm2_g": gain(ks[6], (DEPTH, D_MODEL)),
        "w_in": nrm(ks[7], (DEPTH, D_MODEL, IN_WIDTH), D_MODEL ** -0.5),
        "ret_norm_g": gain(ks[8], (DEPTH, RET_DV)),
        "diff_q_g": gain(ks[9], (DEPTH, DIFF_DK)),
        "diff_k_g": gain(ks[10], (DEPTH, DIFF_DK)),
        "lam_q1": nrm(ks[11], (DEPTH, DIFF_DK), 0.1),
        "lam_k1": nrm(ks[12], (DEPTH, DIFF_DK), 0.1),
        "lam_q2": nrm(ks[13], (DEPTH, DIFF_DK), 0.1),
        "lam_k2": nrm(ks[14], (DEPTH, DIFF_DK), 0.1),
        "diff_sub_g": gain(ks[15], (DEPTH, DIFF_DV)),
        "gla_w_a2": nrm(ks[16], (DEPTH, GLA_RANK, GLA_HEADS * GLA_DK), GLA_RANK ** -0.5),
        "gla_b_a": nrm(ks[17], (DEPTH, GLA_HEADS * GLA_DK), 0.1),
        "gla_norm_g": gain(ks[18], (DEPTH, GLA_DV)),
        "w_out": nrm(ks[19], (DEPTH, MIX_WIDTH, D_MODEL), MIX_WIDTH ** -0.5),
        "router_w": nrm(ks[20], (D_MODEL, N_EXPERTS), D_MODEL ** -0.5),
        "router_b": nrm(ks[21], (N_EXPERTS,), 0.01),
        "w_gate": nrm(ks[22], (DEPTH, N_EXPERTS, D_MODEL, D_EXPERT), D_MODEL ** -0.5),
        "w_up": nrm(ks[23], (DEPTH, N_EXPERTS, D_MODEL, D_EXPERT), D_MODEL ** -0.5),
        "w_down": nrm(ks[24], (DEPTH, N_EXPERTS, D_EXPERT, D_MODEL), D_EXPERT ** -0.5),
    }

def second_block(x, c, positions, w_mod, b_mod, norm1_g, norm2_g, w_in, ret_norm_g,
              diff_q_g, diff_k_g, lam_q1, lam_k1, lam_q2, lam_k2, diff_sub_g,
              gla_w_a2, gla_b_a, gla_norm_g, w_out, router_w, router_b,
              w_gate, w_up, w_down):
    B_, S_, D = x.shape
    heads = lambda t, n: t.reshape(B_, S_, n, -1)
    c_act = jax.nn.silu(c)
    for l in range(DEPTH):
        lam_init = 0.8 - 0.6 * math.exp(-0.3 * l)
        mod = c_act @ w_mod[l] + b_mod[l]
        sh1, sc1, gt1, sh2, sc2, gt2 = jnp.split(mod[:, None, :], 6, axis=-1)
        h = rms_norm_2(x, norm1_g[l]) * (1.0 + sc1) + sh1
        (rq, rk, rv, rg, dq, dk_, dv_, gq, gk, gv, ga, gr) = split_cols(h @ w_in[l], IN_SPLITS)
        out_r = rms_norm_2(retention(heads(rq, RET_HEADS), heads(rk, RET_HEADS),
                                   heads(rv, RET_HEADS), positions),
                         ret_norm_g[l]) * jax.nn.silu(heads(rg, RET_HEADS))
        out_d = diff_attention(dq.reshape(B_, S_, DIFF_HEADS, 2, DIFF_DK),
                               dk_.reshape(B_, S_, DIFF_HEADS, 2, DIFF_DK),
                               heads(dv_, DIFF_HEADS), positions, diff_q_g[l], diff_k_g[l],
                               lam_q1[l], lam_k1[l], lam_q2[l], lam_k2[l], diff_sub_g[l],
                               lam_init)
        log_a = jax.nn.log_sigmoid((ga @ gla_w_a2[l] + gla_b_a[l]).astype(jnp.float32)) / GLA_TAU
        out_g = rms_norm_2(gated_linear_attention(heads(gq, GLA_HEADS), heads(gk, GLA_HEADS),
                                                heads(gv, GLA_HEADS), heads(log_a, GLA_HEADS)),
                         gla_norm_g[l]) * jax.nn.silu(heads(gr, GLA_HEADS))
        mixed = jnp.concatenate([out_r.reshape(B_, S_, RET_W), out_d.reshape(B_, S_, DIFF_W),
                                 out_g.reshape(B_, S_, GLA_W)], axis=-1)
        x = x + gt1 * (mixed @ w_out[l])
        h2 = (rms_norm_2(x, norm2_g[l]) * (1.0 + sc2) + sh2).reshape(B_ * S_, D)
        idx, gates = route(h2, router_w, router_b)
        y = moe(h2, idx, gates, w_gate[l], w_up[l], w_down[l]).reshape(B_, S_, D)
        x = x + gt2 * y
    return x


def setup_inputs(seed=0):
    out = dict(first_inputs(seed))
    for name, value in second_inputs(seed + 1).items():
        if name != "x":
            out[name + "_2"] = value
    return out


def reference(
    x, norm1, norm2, a_wqkv, a_q_gain, a_k_gain, a_wo, b_win, b_conv, b_wout, c_wqkv, c_q_gain,
    c_k_gain, c_wo, mlp_w1, mlp_w2, c_2, positions_2, w_mod_2, b_mod_2, norm1_g_2, norm2_g_2,
    w_in_2, ret_norm_g_2, diff_q_g_2, diff_k_g_2, lam_q1_2, lam_k1_2, lam_q2_2, lam_k2_2,
    diff_sub_g_2, gla_w_a2_2, gla_b_a_2, gla_norm_g_2, w_out_2, router_w_2, router_b_2,
    w_gate_2, w_up_2, w_down_2,
):
    x = first_block(
        x, norm1, norm2, a_wqkv, a_q_gain, a_k_gain, a_wo, b_win, b_conv, b_wout, c_wqkv,
        c_q_gain, c_k_gain, c_wo, mlp_w1, mlp_w2,
    )
    return second_block(
        x, c_2, positions_2, w_mod_2, b_mod_2, norm1_g_2, norm2_g_2, w_in_2, ret_norm_g_2,
        diff_q_g_2, diff_k_g_2, lam_q1_2, lam_k1_2, lam_q2_2, lam_k2_2, diff_sub_g_2,
        gla_w_a2_2, gla_b_a_2, gla_norm_g_2, w_out_2, router_w_2, router_b_2, w_gate_2, w_up_2,
        w_down_2,
    )


_drawn_inputs = setup_inputs


def setup_inputs(seed=0):
    import zlib

    import numpy as np

    out = dict(_drawn_inputs(seed))
    spreads = {}
    factors = {'a_q_gain': 8.0,
     'a_k_gain': 7.592,
     'b_mod_2': 3.085,
     'norm1_g_2': 8.0,
     'norm2_g_2': 5.285,
     'ret_norm_g_2': 8.0,
     'diff_q_g_2': 8.0,
     'diff_k_g_2': 8.0,
     'lam_q1_2': 6.822,
     'lam_k1_2': 6.44,
     'lam_q2_2': 8.0,
     'lam_k2_2': 6.76,
     'diff_sub_g_2': 8.0,
     'gla_w_a2_2': 4.485,
     'gla_b_a_2': 8.0,
     'gla_norm_g_2': 8.0,
     'router_b_2': 3.325}
    for name, (base, spread) in spreads.items():
        noise = np.random.default_rng([zlib.crc32(name.encode()), seed]).standard_normal(out[name].shape)
        drawn = base * np.exp(spread * noise) if base else spread * noise
        out[name] = jnp.asarray(drawn.astype(out[name].dtype))
    for name, factor in factors.items():
        out[name] = (out[name] * factor).astype(out[name].dtype)
    return out
```

```python
from contextlib import ExitStack

import numpy as np

import concourse.bass as bass
from concourse import mybir

F32 = mybir.dt.float32
I32 = mybir.dt.int32
ALU = mybir.AluOpType
ACT = mybir.ActivationFunctionType
AX = mybir.AxisListType.X

P = 128
D = 1024
KD = D // P
S = 256
NT = S // P
EPS = 1e-6
SLOTS = 6
SLAB = 4096
HEADS = 16
DH = 64
GROUPS_A = 3
DILATIONS = (1, 4, 16)
RADIUS = 64
FF = 4096
NF = FF // 512
CHUNK = 64
DEPTH = 2
E = 32
EG = 4
NG = E // EG
FE = 512
SB = 64
BLOCKS = (2 * S - E) // SB + E
PAIRS = BLOCKS // 2
IN_WIDTH = 3344
NEG = -1e30
SCALE = DH ** -0.5
QK_SCALE = SCALE * DH
GLA_HEADS, GLA_DK = 4, 32
LAM_INIT = [0.8 - 0.6 * float(np.exp(-0.3 * l)) for l in range(DEPTH)]

A_QKV = 0
A_WO = A_QKV + 6 * GROUPS_A
MLP0 = A_WO + 2
B_WIN = MLP0 + 2 * NF
B_WOUT = B_WIN + 6
MLP1 = B_WOUT + 2
MOD = MLP1 + 2 * NF
WIN = MOD + 12
WOUT = WIN + 7
MOE = WOUT + 2
TURNS = (12 + 7 + 2 + 3 * BLOCKS) // SLOTS
assert TURNS * SLOTS == 12 + 7 + 2 + 3 * BLOCKS and BLOCKS % 2 == 1

COMMON = {"ident": 128, "ones": 128, "bd64": 128, "rot16": 128}
CONST_A = {"cos_a": S, "sin_a": S, "mask_a": NT * 512}
CONST_2 = {"rot64": 128, "tri": 128, "before": 128, "bdmask": 256, "hsel": 4, "inv_r": 1, "inv_d": 1,
           "decay": 4 * NT * S, "mask_d": NT * S, "iota64": SB, "iota32": 32, "iota8": 8,
           "iotab": BLOCKS, "slot0": 1}
PARAM_1 = {"norm1": 2 * KD, "norm2": 2 * KD, "gain_a": 2 * GROUPS_A, "conv": 3 * KD}
PARAM_2 = {"bmod": 48, "norm1": KD, "norm2": KD, "gain_r": 1, "gain_q": 1, "gain_k": 1, "gain_d": 1,
           "gain_g": 1, "one_minus_lam": 1, "neg_lam": 1, "lam": 4 * DH, "wa2": 128, "ba": 128}
PARAM_R = {"router": KD * E, "router_b": E, "c": KD}


def columns(table):
    at, out = 0, {}
    for name, n in table.items():
        out[name] = (at, at + n)
        at += n
    return out, at


def round_bits(x, bits):
    m, e = np.frexp(x)
    return float(np.ldexp(np.round(m * 2 ** bits), e - bits))


TWO_PI = 2 * np.pi
PI_1 = round_bits(TWO_PI, 8)
PI_2 = round_bits(TWO_PI - PI_1, 8)
PI_3 = TWO_PI - PI_1 - PI_2
MAGIC = 1.5 * 2.0 ** 23


VEC_STEPS = 363
ACT_STEPS = 18


class Ring:

    def __init__(self, slots, landed, done, skip=0):
        self.slots, self.landed, self.done, self.skip = slots, landed, done, skip

    def tile(self, n):
        return self.slots[:, n % SLOTS, :]

    def wait_landed(self, eng, n, turns=0):
        eng.wait_ge(self.landed[n % SLOTS], (turns + (n // SLOTS + 1 - self.skip)) * 16)

    def wait_done(self, eng, n, turns=0):
        eng.wait_ge(self.done, turns * SLOTS + (n + 1 - SLOTS * max(self.skip - 1, 0)))


class Steps:

    def __init__(self, eng, sem):
        self.eng, self.sem, self.n, self.turns = eng, sem, 0, 0

    def inc(self, ins):
        ins.then_inc(self.sem, 1)
        self.n += 1

    def settle(self):
        self.eng.wait_ge(self.sem, self.turns + self.n)

    def step(self, ins):
        self.inc(ins)
        self.settle()

    def loop(self, i, per):
        outer, start = self.turns, self.n
        self.turns = outer + i * per

        def end(times):
            assert self.n - start == per, (self.n - start, per)
            self.turns, self.n = outer, start + per * times
        return end


def program(nc, x_d, xp_d, common_d, const_a_d, const_2_d, param_1_d, param_2_d, param_r_d, pos_d,
            a_wqkv, a_wo, b_win, b_wout, mlp_w1, mlp_w2, w_mod, w_in, w_out, w_gate, w_up, w_down,
            out_d, first=True, second=True, stop=99):
    ctx = ExitStack()
    enter = ctx.enter_context

    def sb(name, n, dt=F32):
        return enter(nc.sbuf_tensor(name, [P, n], dt))[:, :]

    def sem(name):
        return enter(nc.semaphore(name))

    ring_sb = enter(nc.sbuf_tensor("ring", [P, SLOTS, SLAB], F32))
    xT = sb("xT", KD * S)
    hT = sb("hT", KD * S)
    tmp = sb("tmp", 2048)
    rstd = sb("rstd", S)
    small = sb("small", 64)
    com_c, com_n = columns(COMMON)
    common = sb("common", com_n)
    p1_c, p1_n = columns(PARAM_1)
    param_1 = sb("param_1", p1_n)
    ARENA = 21504
    arena = sb("arena", ARENA)
    x3 = xT.rearrange("p (k t) -> p k t", k=KD)
    h3 = hT.rearrange("p (k t) -> p k t", k=KD)
    tmp_a, tmp_b = tmp[:, 0:1024], tmp[:, 1024:2048]

    def com(name):
        a, b = com_c[name]
        return common[:, a:b]

    def par1(name):
        a, b = p1_c[name]
        return param_1[:, a:b]

    def carve():
        at = [0]

        def take(n):
            at[0] += n
            assert at[0] <= ARENA, at
            return arena[:, at[0] - n:at[0]]
        return take

    take = carve()
    qk = take(GROUPS_A * 2 * KD * S).rearrange("p (g w k t) -> p g w k t", g=GROUPS_A, w=2, k=KD)
    vA = take(GROUPS_A * NT * D).rearrange("p (g r f) -> p g r f", g=GROUPS_A, r=NT)
    xp = vA[:, :, :, :].rearrange("p g r f -> p (g r f)")[:, 0:KD * S].rearrange("p (k t) -> p k t", k=KD)
    ca_c, ca_n = columns(CONST_A)
    const_a = take(ca_n)
    heads_now = take(GROUPS_A * 2 * S).rearrange("p (g w t) -> p g w t", g=GROUPS_A, w=2)
    o_rows = rstd[:, 0:P]
    att_s = [tmp[:, 0:512], tmp[:, 512:1024]]
    att_t = tmp[:, 1024:1536].rearrange("p (j q) -> p j q", j=4)
    o_bank = (3, 4, 5, 7)
    cos_a = const_a[:, ca_c["cos_a"][0]:ca_c["cos_a"][1]]
    sin_a = const_a[:, ca_c["sin_a"][0]:ca_c["sin_a"][1]]
    mask_a = const_a[:, ca_c["mask_a"][0]:ca_c["mask_a"][1]].rearrange("p (r n) -> p r n", r=NT)

    take = carve()
    act3 = [take(1024) for _ in range(3)]
    conv_u = take(1024).rearrange("p (k t) -> p k t", k=4)
    conv_y = take(1024).rearrange("p (k t) -> p k t", k=4)
    mixB = take(KD * S).rearrange("p (k t) -> p k t", k=KD)

    take = carve()
    c2_c, c2_n = columns(CONST_2)
    const_2 = take(c2_n)
    p2_c, p2_n = columns(PARAM_2)
    param_2 = take(p2_n)
    pr_c, pr_n = columns(PARAM_R)
    param_r = take(pr_n)
    tables = take(4 * S).rearrange("p (n t) -> p n t", n=4)
    md = take(48)
    gains = take(2 * KD)
    zeros = take(P)
    base2 = c2_n + p2_n + pr_n + 4 * S + 48 + 2 * KD + P

    def carve2():
        at = [base2]

        def take(n):
            at[0] += n
            assert at[0] <= ARENA, (at, ARENA)
            return arena[:, at[0] - n:at[0]]
        return take
    take = carve2()
    rqk = take(4 * S).rearrange("p (k t) -> p k t", k=4)
    gates = take(4 * S).rearrange("p (k t) -> p k t", k=4)
    dqk = take(8 * S).rearrange("p (k t) -> p k t", k=8)
    rv = take(NT * 256).rearrange("p (r f) -> p r f", r=NT)
    dv = take(NT * 512).rearrange("p (r f) -> p r f", r=NT)
    gv = take(4 * 256).rearrange("p (c f) -> p c f", c=4)
    gqk = take(2 * S).rearrange("p (k t) -> p k t", k=2)
    ga = take(S)
    gT, eg, qe, kd = take(S), take(S), take(S), take(S)
    qsel = take(4 * S).rearrange("p (t h) -> p t h", h=4)
    a_gla = rqk.rearrange("p k t -> p (k t)")
    state = take(256)
    kvm = take(256)
    pair_d = [take(2048).rearrange("p (t s) -> p t s", t=32) for _ in range(2)]
    kdt = rv.rearrange("p r f -> p (r f)").rearrange("p (c f) -> p c f", c=4)
    la = take(NT * P).rearrange("p (r f) -> p r f", r=NT)
    scratch = pair_d[0].rearrange("p t s -> p (t s)")
    scratch_b = pair_d[1].rearrange("p t s -> p (t s)")
    aT = [take(512).rearrange("p (r t) -> p r t", r=NT) for _ in range(2)]
    att_d = aT
    aTd = [kdt.rearrange("p c f -> p (c f)"), a_gla[:, 0:512]]
    aTd = [a.rearrange("p (r t) -> p r t", r=NT) for a in aTd]
    take = carve2()
    h2tok = take(NT * D).rearrange("p (r f) -> p r f", r=NT)
    sel = [take(NT * SB).rearrange("p (r s) -> p r s", r=NT) for _ in range(2)]
    selT = take(S)
    selT_b = take(S)
    xg = [take(KD * SB).rearrange("p (k s) -> p k s", k=KD) for _ in range(2)]
    eb, sg, ue = take(256), take(256), take(256)
    ysb = take(D)
    dbc = take(4 * S).rearrange("p (j t) -> p j t", j=4)
    route = take(1400)
    ends, passed = take(BLOCKS * E), take(BLOCKS)
    diag = take(8 * P).rearrange("p (r j t) -> p r j t", r=NT, j=4)
    btab = enter(nc.sbuf_tensor("block_experts", [P, BLOCKS], I32))

    def con2(name):
        a, b = c2_c[name]
        return const_2[:, a:b]

    def par2(name):
        a, b = p2_c[name]
        return param_2[:, a:b]

    def parr(name):
        a, b = pr_c[name]
        return param_r[:, a:b]

    decay = con2("decay").rearrange("p (h r t) -> p h r t", h=4, r=NT)
    mask_d = con2("mask_d").rearrange("p (r t) -> p r t", r=NT)
    router = parr("router").rearrange("p (k e) -> p k e", k=KD)

    ps = enter(nc.psum_tensor("ps", [P, 8, 512], F32))

    def bank(b, n=1):
        return ps[:, b:b + n, :].rearrange("p b n -> p (b n)")

    def chunks(b, n):
        return bank(b, (n + 1) // 2)[:, 0:n * S].rearrange("p (k t) -> p k t", k=n)

    landed = [sem(f"slab_landed_{i}") for i in range(SLOTS)]
    slab_done = sem("slab_done")
    skip = 0 if first else MOD // SLOTS
    ring = Ring(ring_sb, landed, slab_done, skip)
    consts_in, x_in, xp_in, const2_in, pos_in, param2_in, out_sent = [
        sem(n) for n in ("consts_in", "x_in", "xp_in", "const2_in", "pos_in", "param2_in", "out_sent")]
    vec_step, act_step = sem("vec_step"), sem("act_step")
    held = sem("held")
    x_squared, x_summed, x_root, h_ready, x_ready = [
        sem(n) for n in ("x_squared", "x_summed", "x_root", "h_ready", "x_ready")]
    q_squared, q_summed, q_normed, q_root, q_turned, q_ready, v_ready = [
        sem(n) for n in ("q_squared", "q_summed", "q_normed", "q_root", "q_turned", "q_ready", "v_ready")]
    heads_staged, scored, masked, max_ready, prob_ready, prob_turned, prob_copied, pv_done, o_scaled, \
        o_turned, o_copied = [sem("a_" + n) for n in (
            "heads_staged", "scored", "masked", "max_ready", "prob_ready", "prob_turned", "prob_copied",
            "pv_done", "o_scaled", "o_turned", "o_copied")]
    relu_ready, act_ready = sem("relu_ready"), sem("act_ready")
    c_copied, u_ready, y_ready = sem("c_copied"), sem("u_ready"), sem("y_ready")
    tables_ready, angle_ready, sin_ready, c_exp = [
        sem(n) for n in ("tables_ready", "angle_ready", "sin_ready", "c_exp")]
    win_copied, dq_squared, qk_product, qk_root, qk_ready = [
        sem(n) for n in ("win_copied", "dq_squared", "qk_product", "qk_root", "qk_ready")]
    gate_exp, gate_ready, lam_exp, lam_ready = [sem(n) for n in ("gate_exp", "gate_ready", "lam_exp", "lam_ready")]
    r_scored, r_decayed, r_used = [sem(n) for n in ("r_scored", "r_decayed", "r_used")]
    d_scored, d_max, d_exp, d_diff, d_turned, d_copied, d_out = [
        sem("d_" + n) for n in ("scored", "max", "exp", "diff", "turned", "copied", "out")]
    o_squared, o_summed, o_root, mix_ready = [
        sem(n) for n in ("o_squared", "o_summed", "o_root", "mix_ready")]
    g_logit, g_log, g_la, g_cum, g_exps, g_keys, g_keysT, g_keysC, g_diff, g_dexp, g_dk, g_pair, \
        g_acopy, g_kv, g_state, g_out = [sem("g_" + n) for n in (
            "logit", "log", "la", "cum", "exps", "keys", "keysT", "keysC", "diff", "dexp", "dk",
            "pair", "acopy", "kv", "state", "out")]
    t_logits, t_exp, t_rows, t_rows_copied, t_mask, t_ranks, t_table, t_diag, t_spread, t_spread_copied, \
        t_cleared = [sem("t_" + n) for n in (
            "logits", "exp", "rows", "rows_copied", "mask", "ranks", "table", "diag", "spread",
            "spread_copied", "cleared")]
    sel_ready, gathered, xg_ready, gate_e, ue_ready, y_copied_a, y_copied_v, selT_ready, scattered = [
        sem("e_" + n) for n in ("sel_ready", "gathered", "xg_ready", "gate_e", "ue_ready", "y_copied_a",
                                "y_copied_v", "selT_ready", "scattered")]

    def cols_of(w, n0, cols=512):
        return w[:, n0:n0 + cols].rearrange("(k p) n -> p k n", p=P)

    def rows_of(w, r0):
        return w[r0:r0 + 512, :].rearrange("(k p) n -> p k n", p=P)

    def wcols(n, cols=512):
        return ring.tile(n)[:, 0:KD * cols].rearrange("p (k n) -> p k n", k=KD)

    def wrows(n):
        return ring.tile(n).rearrange("p (k n) -> p k n", k=4)

    block = enter(nc.Block())
    MIN_X = 4 if first else 0

    @block.sync
    def _(sp):
        def load(n, dst, src, turns=0):
            if n >= SLOTS:
                sp.wait_ge(slab_done, turns * SLOTS + (n - SLOTS * (1 + max(skip - 1, 0)) + 1))
            sp.dma_start(dst, src).then_inc(landed[n % SLOTS], 16)

        def load_cols(n, w, n0, cols=512, turns=0):
            load(n, wcols(n, cols), cols_of(w, n0, cols), turns)

        def load_rows(n, w, r0, turns=0):
            load(n, wrows(n), rows_of(w, r0), turns)

        def mlp(n, w1, w2):
            load_cols(n, w1, 0)
            for j in range(1, NF):
                load_cols(n + 2 * j - 1, w1, 512 * j)
                load_rows(n + 2 * j, w2, 512 * (j - 1))
            load_rows(n + 2 * NF - 1, w2, 512 * (NF - 1))

        if first:
            for g in range(GROUPS_A):
                for s in range(6):
                    load_cols(A_QKV + 6 * g + s, a_wqkv[0], (6 * g + s) * 512)
            for s in range(2):
                load_cols(A_WO + s, a_wo[0], 512 * s)
            mlp(MLP0, mlp_w1[0], mlp_w2[0])
            for s in range(2):
                for j, part in enumerate((1, 2, 0)):
                    load_cols(B_WIN + 3 * s + j, b_win[0], part * D + 512 * s)
            for s in range(2):
                load_cols(B_WOUT + s, b_wout[0], 512 * s)
            mlp(MLP1, mlp_w1[1], mlp_w2[1])
        if second:
            wm = w_mod.rearrange("l (k p) (j n) -> l p k j n", p=P, n=512)
            wi = w_in.rearrange("l (k p) n -> l p k n", p=P)
            wo = w_out.rearrange("l (k p) n -> l p k n", p=P)
            wg = w_gate.rearrange("l e (k p) f -> (l e) p k f", p=P)
            wu = w_up.rearrange("l e (k p) f -> (l e) p k f", p=P)
            wd = w_down.rearrange("l e (k p) n -> (l e) p k n", p=P)

            def pick(w, i):
                return w[bass.ds(i, 1)].rearrange("o p k n -> p (o k) n")

            with sp.Fori(0, DEPTH) as lay:
                with sp.Fori(0, 2) as i:
                    for s in range(6):
                        src = wm[bass.ds(lay, 1), :, :, bass.ds(i * 6 + s, 1), :].rearrange("o p k q n -> p (o k) (q n)")
                        load(MOD + s, wcols(MOD + s), src, lay * TURNS + i)
                for s in range(7):
                    cols = min(512, IN_WIDTH - 512 * s)
                    src = wi[bass.ds(lay, 1), :, :, 512 * s:512 * s + cols].rearrange("o p k n -> p (o k) n")
                    load(WIN + s, wcols(WIN + s, cols), src, lay * TURNS)
                for s in range(2):
                    src = wo[bass.ds(lay, 1), :, :, 512 * s:512 * s + 512].rearrange("o p k n -> p (o k) n")
                    load(WOUT + s, wcols(WOUT + s), src, lay * TURNS)
                sp.wait_ge(t_table, lay + 1)
                sp.sem_inc(held, 1)

                def expert(n, b, turns):
                    e = sp.value_load(btab[0:1, b:b + 1] if isinstance(b, int) else btab[0:1, bass.ds(b, 1)],
                                      min_val=0, max_val=E - 1)
                    e = sp.snap(e + lay * E, min_val=0, max_val=DEPTH * E - 1)
                    load(n, wcols(n), pick(wg, e), turns)
                    load(n + 1, wcols(n + 1), pick(wu, e), turns)
                    load(n + 2, wrows(n + 2), pick(wd, e), turns)

                with sp.Fori(0, PAIRS) as i:
                    for h in range(2):
                        expert(MOE + 3 * h, sp.snap(i * 2 + h), lay * TURNS + i)
                expert(MOE + 6 * PAIRS, BLOCKS - 1, lay * TURNS)
        sp.wait_ge(x_ready, MIN_X + (2 * DEPTH if second else 0))
        sp.dma_start(out_d, xT).then_inc(out_sent, 16)
        sp.wait_ge(out_sent, 16)

    @block.scalar
    def _(act):
        sc = nc.scalar
        own = Steps(act, act_step)
        act.dma_start(common[:, :], common_d).then_inc(consts_in, 16)
        act.dma_start(param_1[:, :], param_1_d).then_inc(consts_in, 16)
        act.dma_start(xT, x_d).then_inc(x_in, 16)
        if first:
            act.dma_start(xp.rearrange("p k t -> p (k t)"), xp_d).then_inc(xp_in, 16)
            act.dma_start(const_a[:, :], const_a_d).then_inc(consts_in, 16)

        def root(dst, src, scale, eps, ready):
            own.step(sc.activation(dst, src, ACT.Ln, bias=eps, scale=scale))
            sc.activation(dst, dst, ACT.Exp, scale=-0.5).then_inc(ready, 1)

        def square_x(n, src):
            if isinstance(n, int) and n == 0:
                act.wait_ge(xp_in if first else x_in, 16)
            else:
                act.wait_ge(x_ready, n)
            sc.activation(tmp, src, ACT.Square).then_inc(x_squared, 1)
            act.wait_ge(x_summed, n + 1)
            root(rstd, bank(7)[:, 0:S], 1.0 / D, EPS, x_root)

        def mlp(l, n):
            def relu(j, slab, turns=0, i=0):
                ring.wait_done(act, slab, turns)
                act.wait_ge(act_ready, i + 8 * l + j)
                sc.activation(tmp_a, bank(4, 2), ACT.Relu).then_inc(relu_ready, 1)
            relu(0, n)
            relu(1, n + 1)
            with act.Fori(0, 2) as i:
                for jj in range(3):
                    relu(2 + jj, n + 3 + 2 * jj, i, i * 3)

        if first:
            square_x(0, xp.rearrange("p k t -> p (k t)"))
            with act.Fori(0, GROUPS_A) as g:
                close = own.loop(g, 4)
                for s in range(4):
                    ring.wait_done(act, A_QKV + s, g)
                    act.wait_ge(q_summed, g * 4 + s)
                    sc.activation(tmp_a, bank(2 * (s % 2), 2), ACT.Square).then_inc(q_squared, 1)
                    act.wait_ge(q_summed, g * 4 + (s + 1))
                    act.wait_ge(q_ready, g * 4 + max(s - 1, 0))
                    root(tmp_b, bank(4, 2), 1.0, DH * EPS, q_root)
                close(GROUPS_A)
                for s in range(2):
                    ring.wait_done(act, A_QKV + 4 + s, g)
                    dst = vA[:, bass.ds(g, 1), :, 512 * s:512 * s + 512].rearrange("p g r f -> p (g r) f")
                    sc.activation(dst, bank(2 * s, 2).rearrange("p (r f) -> p r f", r=NT),
                                  ACT.Copy).then_inc(v_ready, 1)
            act.wait_ge(q_ready, 4 * GROUPS_A)
            with act.Fori(0, KD) as c:
                act.wait_ge(scored, c * 4)
                src = qk[:, :, :, bass.ds(c, 1), :].rearrange("p g w c t -> p (g w c) t")
                sc.activation(heads_now.rearrange("p g w t -> p (g w) t"), src, ACT.Copy).then_inc(heads_staged, 1)

                def o_copy(r):
                    act.wait_ge(o_turned, c * 2 + (r + 1))
                    dst = h3[:, bass.ds(c, 1), r * P:(r + 1) * P].rearrange("p c t -> p (c t)")
                    sc.activation(dst, bank(6)[:, 0:P], ACT.Copy).then_inc(o_copied, 1)
                for u in range(4):
                    act.wait_ge(max_ready, c * 4 + (u + 1))
                    sc.activation(att_s[u % 2], att_s[u % 2], ACT.Exp, bias=small[:, 2 + u % 2:3 + u % 2],
                                  scale=QK_SCALE, accum_out=small[:, 4 + u % 2:5 + u % 2]).then_inc(prob_ready, 1)
                    act.wait_ge(prob_turned, c * 4 + (u + 1))
                    act.wait_ge(pv_done, c * 4 + u)
                    sc.activation(att_t.rearrange("p j q -> p (j q)"), bank(2), ACT.Copy).then_inc(prob_copied, 1)
                    if u == 2:
                        o_copy(0)
                o_copy(1)
            square_x(1, xT)
            mlp(0, MLP0)
            square_x(2, xT)
            for s in range(2):
                ring.wait_done(act, B_WIN + 3 * s)
                if s:
                    act.wait_ge(u_ready, s)
                sc.activation(tmp_a, bank(0, 2), ACT.Copy).then_inc(c_copied, 1)
            square_x(3, xT)
            mlp(1, MLP1)

        if second:
            if first:
                act.wait_ge(x_ready, 4)
            act.dma_start(const_2[:, :], const_2_d).then_inc(const2_in, 16)
            act.dma_start(param_r[:, :], param_r_d).then_inc(const2_in, 16)
            pos_i = scratch[:, 0:S].bitcast(I32)
            act.dma_start(pos_i, pos_d).then_inc(pos_in, 16)
            for n in range(4):
                act.wait_ge(angle_ready, n + 1)
                sc.activation(tables[:, n, :], scratch[:, (2 + n) * S:(3 + n) * S], ACT.Sin).then_inc(sin_ready, 1)
            act.wait_ge(const2_in, 32)
            sc.activation(small[:, 16:24], parr("c"), ACT.Exp, scale=-1.0).then_inc(c_exp, 1)
            with act.Fori(0, DEPTH) as lay:
                close = own.loop(lay, ACT_STEPS)
                act.wait_ge(x_ready, lay * 2 + MIN_X)
                act.dma_start(param_2[:, :], param_2_d[bass.ds(lay, 1)].rearrange("o p n -> p (o n)")
                              ).then_inc(param2_in, 16)
                act.wait_ge(x_in, 16)
                square_x(lay * 2 + MIN_X, xT)
                act.wait_ge(lam_ready, lay * 2 + 1)
                sc.activation(small[:, 26:28], small[:, 24:26], ACT.Exp).then_inc(lam_exp, 1)
                pair = (0, 3)

                def slab(s):
                    ring.wait_done(act, WIN + s, lay * TURNS)
                    return pair[s % 2]

                def qk_roots(w):
                    act.wait_ge(qk_product, lay * 5 + (2 + 2 * w))
                    act.wait_ge(qk_ready, lay * 5 + (1 + 2 * w))
                    root(tmp_b, bank(6, 2), 1.0, DH * EPS, qk_root)
                b = slab(0)
                sc.activation(rqk, chunks(b, 4), ACT.Copy).then_inc(win_copied, 1)
                b = slab(1)
                sc.activation(rv, bank(b).rearrange("p (r f) -> p r f", r=NT), ACT.Copy)
                sc.activation(gates[:, 0:2, :], chunks(b + 1, 2), ACT.Copy).then_inc(win_copied, 1)
                b = slab(2)
                sc.activation(tmp_a, bank(b, 2), ACT.Square).then_inc(dq_squared, 1)
                sc.activation(dqk[:, 0:4, :], chunks(b, 4), ACT.Copy).then_inc(win_copied, 1)
                b = slab(3)
                sc.activation(scratch_b[:, 0:1024], bank(b, 2), ACT.Square).then_inc(dq_squared, 1)
                sc.activation(dqk[:, 4:8, :], chunks(b, 4), ACT.Copy).then_inc(win_copied, 1)
                qk_roots(0)
                b = slab(4)
                sc.activation(dv, bank(b, 2).rearrange("p (r f) -> p r f", r=NT), ACT.Copy).then_inc(win_copied, 1)
                b = slab(5)
                sc.activation(gqk[:, 0, :], chunks(b, 2)[:, 0, :], ACT.Copy, scale=GLA_DK ** -0.5)
                sc.activation(gqk[:, 1, :], chunks(b, 2)[:, 1, :], ACT.Copy)
                sc.activation(gv[0:64].rearrange("p c f -> p (c f)"), bank(b + 1, 2)[0:64], ACT.Copy).then_inc(win_copied, 1)
                qk_roots(1)
                b = slab(6)
                sc.activation(ga[0:16, :], bank(b)[0:16, 0:S], ACT.Copy)
                sc.activation(gates[:, 2:4, :], chunks(b + 1, 2), ACT.Copy).then_inc(win_copied, 1)
                act.wait_ge(win_copied, lay * 7 + 7)
                sc.activation(scratch[:, 0:1024], gates.rearrange("p k t -> p (k t)"), ACT.Exp, scale=-1.0
                              ).then_inc(gate_exp, 1)

                def square_o(n, width, b, sums, dim, ready):
                    act.wait_ge(*ready)
                    act.wait_ge(qk_ready, lay * 5 + 5)
                    if n:
                        act.wait_ge(o_summed, lay * 3 + n)
                    sc.activation(tmp_a[:, 0:width], bank(b, width // 512), ACT.Square).then_inc(o_squared, 1)
                    act.wait_ge(o_summed, lay * 3 + (n + 1))
                    act.wait_ge(mix_ready, lay * 3 + n)
                    root(tmp_b[:, 0:width], bank(sums, width // 512), 1.0 / dim, EPS, o_root)
                square_o(0, 512, 2, 3, DH, (r_used, lay * 4 + 4))
                def d_copy(u):
                    h, r = u // 2, u % 2
                    act.wait_ge(d_turned, lay * 8 + (u + 1))
                    if h >= 2:
                        act.wait_ge(d_out, lay * 4 + (h - 1))
                    src = bank(6 + u % 2)[:, 0:S].rearrange("p (k q) -> p k q", k=NT)
                    sc.activation(aTd[h % 2][:, :, r * P:(r + 1) * P], src, ACT.Copy).then_inc(d_copied, 1)
                for u in range(8):
                    act.wait_ge(d_max, lay * 8 + (u + 1))
                    for w in range(2):
                        e = sc.activation(att_d[u % 2][:, w, :], att_d[u % 2][:, w, :], ACT.Exp,
                                          bias=small[:, 32 + 2 * (u % 2) + w:33 + 2 * (u % 2) + w],
                                          scale=QK_SCALE,
                                          accum_out=small[:, 36 + 2 * (u % 2) + w:37 + 2 * (u % 2) + w])
                    e.then_inc(d_exp, 1)
                    if u:
                        d_copy(u - 1)
                d_copy(7)
                square_o(1, 1024, 4, 6, 2 * DH, (d_out, lay * 4 + 4))
                act.wait_ge(g_logit, lay + 1)
                lg = scratch_b[:, 256:512]
                own.step(sc.activation(lg, bank(0)[:, 0:S], ACT.Abs))
                own.step(sc.activation(lg, lg, ACT.Exp, scale=-1.0))
                sc.activation(lg, lg, ACT.Ln, bias=1.0).then_inc(g_log, 1)
                act.wait_ge(g_cum, lay + 1)
                own.step(sc.activation(gT, bank(1)[:, 0:S], ACT.Copy))
                sc.activation(eg, bank(1)[:, 0:S], ACT.Exp)
                for c in range(4):
                    a, b = 64 * c, 64 * c + 64
                    e = sc.activation(kd[:, a:b], gT[:, a:b], ACT.Exp, scale=-1.0, bias=gT[:, b - 1:b])
                e.then_inc(g_exps, 1)
                act.wait_ge(g_keysT, lay + 1)
                sc.activation(kdt[0:64].rearrange("p c f -> p (c f)"), bank(2)[0:64], ACT.Copy).then_inc(g_keysC, 1)
                for v in range(8):
                    act.wait_ge(g_diff, lay * 8 + (v + 1))
                    own.step(sc.activation(pair_d[v % 2], pair_d[v % 2], ACT.Abs))
                    sc.activation(pair_d[v % 2], pair_d[v % 2], ACT.Exp, scale=-1.0).then_inc(g_dexp, 1)
                    if v % 2 == 1:
                        c = v // 2
                        act.wait_ge(g_pair, lay * 8 + (v + 1))
                        sc.activation(a_gla[0:64, 256 * c:256 * c + 256],
                                      bank(4 + c % 2)[0:64, 0:256], ACT.Copy).then_inc(g_acopy, 1)
                square_o(2, 512, 6, 3, DH, (g_out, lay + 1))
                square_x(lay * 2 + (MIN_X + 1), xT)
                act.wait_ge(t_logits, lay + 1)
                sc.activation(route[:, 0:64], bank(6)[:, 0:64], ACT.Exp, scale=-1.0).then_inc(t_exp, 1)
                act.wait_ge(t_rows, lay + 1)
                sc.activation(h2tok[:, 0, :], bank(0, 2), ACT.Copy)
                sc.activation(h2tok[:, 1, :], bank(2, 2), ACT.Copy).then_inc(t_rows_copied, 1)
                act.wait_ge(t_spread, lay + 1)
                sc.activation(dbc.rearrange("p j t -> p (j t)"), bank(4, 2), ACT.Copy).then_inc(t_spread_copied, 1)

                def gathered_copy(h, b):
                    act.wait_ge(gathered, b + 1)
                    sc.activation(xg[h].rearrange("p k s -> p (k s)"), bank(4), ACT.Copy).then_inc(xg_ready, 1)

                def expert(h, n, b, turns, last=False):
                    ring.wait_done(act, n + 1, turns)
                    sc.activation(eb, bank(5)[:, 0:256], ACT.Exp, scale=-1.0).then_inc(gate_e, 1)
                    if not last:
                        gathered_copy(1 - h, b + 1)
                    ring.wait_done(act, n + 2, turns)
                    sc.activation(ysb[64 * h:64 * h + 64, 0:512], bank(6)[64 * h:64 * h + 64], ACT.Copy
                                  ).then_inc(y_copied_a, 1)
                gathered_copy(0, lay * BLOCKS)
                with act.Fori(0, PAIRS) as i:
                    for h in range(2):
                        expert(h, MOE + 3 * h, lay * BLOCKS + i * 2 + h, lay * TURNS + i)
                expert(0, MOE + 6 * PAIRS, None, lay * TURNS, last=True)
                close(DEPTH)

    @block.vector
    def _(dve):
        ve = nc.vector
        own = Steps(dve, vec_step)
        dve.wait_ge(consts_in, 48 if first else 32)
        dve.wait_ge(x_in, 16)

        def norm(n, src, gain, shift=None):
            dve.wait_ge(x_root, n + 1)
            for k in range(KD):
                e = ve.scalar_tensor_tensor(out=h3[:, k, :], in0=src[:, k, :], scalar=gain[:, k:k + 1],
                                            in1=rstd, op0=ALU.mult, op1=ALU.mult)
            if shift is not None:
                own.step(e)
                for k in range(KD):
                    e = ve.tensor_scalar(h3[:, k, :], h3[:, k, :], shift[:, k:k + 1], None, ALU.add)
            e.then_inc(h_ready, 1)

        def rope(q, cos, sin, turned, ready):
            t = tmp_b.rearrange("p (k t) -> p k t", k=4)
            own.inc(ve.tensor_tensor(t, turned, sin.unsqueeze(1).broadcast_to([P, 4, S]), ALU.mult))
            own.step(ve.tensor_tensor(q, q, cos.unsqueeze(1).broadcast_to([P, 4, S]), ALU.mult))
            ve.tensor_tensor(q, q, t, ALU.add).then_inc(ready, 1)

        def mlp(l, n):
            def squared(j, i=0, more=0):
                dve.wait_ge(relu_ready, more + 8 * l + j + 1)
                if j >= 2:
                    ring.wait_done(dve, n + 2 * (j - 2), i)
                ve.tensor_tensor(act3[j % 3], tmp_a, tmp_a, ALU.mult).then_inc(act_ready, 1)
            squared(0)
            squared(1)
            with dve.Fori(0, 2) as i:
                for jj in range(3):
                    squared(2 + jj, i, i * 3)
            ring.wait_done(dve, n + 2 * NF - 1)
            ve.tensor_tensor(xT, xT, bank(0, 4), ALU.add).then_inc(x_ready, 1)

        if first:
            dve.wait_ge(xp_in, 16)
            norm(0, xp, par1("norm1")[:, 0:KD])
            with dve.Fori(0, GROUPS_A) as g:
                close = own.loop(g, 8)

                def part(s):
                    return qk[:, bass.ds(g, 1), s // 2, 4 * (s % 2):4 * (s % 2) + 4, :].rearrange(
                        "p g k t -> p (g k) t")

                def turn(s):
                    dve.wait_ge(q_turned, g * 4 + (s + 1))
                    rope(part(s), cos_a, sin_a, chunks(6, 4), q_ready)
                for s in range(4):
                    root_s = tmp_b
                    dve.wait_ge(q_root, g * 4 + (s + 1))
                    gcol = par1("gain_a").rearrange("p (g w) -> p g w", g=GROUPS_A)[:, bass.ds(g, 1), s // 2]
                    ve.scalar_tensor_tensor(
                        out=part(s), in0=chunks(2 * (s % 2), 4), scalar=gcol,
                        in1=root_s.rearrange("p (k t) -> p k t", k=4), op0=ALU.mult, op1=ALU.mult
                    ).then_inc(q_normed, 1)
                    dve.wait_ge(q_normed, g * 4 + (s + 1))
                    if s:
                        turn(s - 1)
                turn(3)
                close(GROUPS_A)

            with dve.Fori(0, KD) as c:
                close = own.loop(c, 4)

                def mask(u):
                    r, p = u // 2, u % 2
                    dve.wait_ge(scored, c * 4 + (u + 1))
                    if u >= 2:
                        dve.wait_ge(prob_turned, c * 4 + (u - 1))
                    dve.sem_inc(held, 1)
                    ve.tensor_tensor_reduce(att_s[p], bank(p), mask_a[:, r, :], 1.0, -3e38, ALU.add, ALU.max,
                                            small[:, p:p + 1]).then_inc(masked, 1)
                    dve.wait_ge(masked, c * 4 + (u + 1))
                    ve.tensor_scalar(small[:, 2 + p:3 + p], small[:, p:p + 1], -QK_SCALE, None, ALU.mult
                                     ).then_inc(max_ready, 1)

                def scale_o(u):
                    r, p = u // 2, u % 2
                    dve.wait_ge(pv_done, c * 4 + (u + 1))
                    own.step(ve.reciprocal(small[:, 6 + p:7 + p], small[:, 4 + p:5 + p]))
                    if p == 0:
                        dve.wait_ge(o_turned, c * 2 + r)
                    ve.tensor_scalar(o_rows[:, 64 * p:64 * p + 64], bank(o_bank[u])[:, 0:64],
                                     small[:, 6 + p:7 + p], None, ALU.mult).then_inc(o_scaled, 1)
                mask(0)
                mask(1)
                scale_o(0)
                mask(2)
                scale_o(1)
                mask(3)
                scale_o(2)
                scale_o(3)
                close(KD)

            for k in range(KD):
                if k % 4 == 0:
                    ring.wait_done(dve, A_WO + k // 4)
                nat = x3[:, k, :].rearrange("p (m b a) -> p a b m", b=4, a=4)
                e = ve.tensor_tensor(nat, nat, chunks(0, 8)[:, k, :].rearrange("p (a b m) -> p a b m", a=4, b=4),
                                     ALU.add)
            e.then_inc(x_ready, 1)
            dve.wait_ge(x_ready, 1)
            norm(1, x3, par1("norm2")[:, 0:KD])
            mlp(0, MLP0)
            dve.wait_ge(x_ready, 2)
            norm(2, x3, par1("norm1")[:, KD:2 * KD])
            conv = par1("conv")
            for s in range(2):
                ring.wait_done(dve, B_WIN + 3 * s + 1)
                dve.wait_ge(c_copied, s + 1)
                ve.tensor_tensor(conv_u.rearrange("p k t -> p (k t)"), tmp_a, bank(2, 2), ALU.mult).then_inc(u_ready, 1)
                dve.wait_ge(u_ready, s + 1)

                def tap(w, k):
                    return conv[:, w * KD + 4 * s + k:w * KD + 4 * s + k + 1]
                for k in range(4):
                    e = ve.tensor_scalar(conv_y[:, k, :], conv_u[:, k, :], tap(1, k), None, ALU.mult)
                own.step(e)
                for k in range(4):
                    e = ve.scalar_tensor_tensor(out=conv_y[:, k, 1:S], in0=conv_u[:, k, 0:S - 1], scalar=tap(0, k),
                                                in1=conv_y[:, k, 1:S], op0=ALU.mult, op1=ALU.add)
                own.step(e)
                for k in range(4):
                    e = ve.scalar_tensor_tensor(out=conv_y[:, k, 0:S - 1], in0=conv_u[:, k, 1:S], scalar=tap(2, k),
                                                in1=conv_y[:, k, 0:S - 1], op0=ALU.mult, op1=ALU.add)
                own.step(e)
                ring.wait_done(dve, B_WIN + 3 * s + 2)
                ve.tensor_tensor(mixB[:, 4 * s:4 * s + 4, :], conv_y, chunks(4, 4), ALU.mult).then_inc(y_ready, 1)
            ring.wait_done(dve, B_WOUT + 1)
            ve.tensor_tensor(xT, xT, bank(0, 4), ALU.add).then_inc(x_ready, 1)
            dve.wait_ge(x_ready, 3)
            norm(3, x3, par1("norm2")[:, KD:2 * KD])
            mlp(1, MLP1)
            dve.wait_ge(x_ready, 4)

        if second:
            dve.wait_ge(const2_in, 32)
            dve.wait_ge(pos_in, 16)
            own.inc(ve.memset(zeros, 0.0))
            pos = scratch[:, S:2 * S]
            own.step(ve.tensor_copy(pos, scratch[:, 0:S].bitcast(I32)))
            ang, turns_, wrap = scratch_b[:, 0:S], scratch_b[:, S:2 * S], scratch_b[:, 2 * S:3 * S]
            for n, inv in enumerate(("inv_r", "inv_d")):
                own.step(ve.tensor_scalar(ang, pos, con2(inv), None, ALU.mult))
                own.step(ve.tensor_scalar(turns_, ang, 1.0 / TWO_PI, None, ALU.mult))
                own.step(ve.tensor_scalar(turns_, turns_, MAGIC, None, ALU.add))
                own.step(ve.tensor_scalar(turns_, turns_, MAGIC, None, ALU.subtract))
                for part in (PI_1, PI_2, PI_3):
                    own.step(ve.scalar_tensor_tensor(out=ang, in0=turns_, scalar=-part, in1=ang, op0=ALU.mult,
                                                     op1=ALU.add))
                cos_arg = scratch[:, (2 + 2 * n) * S:(3 + 2 * n) * S]
                sin_arg = scratch[:, (3 + 2 * n) * S:(4 + 2 * n) * S]
                own.step(ve.tensor_scalar(cos_arg, ang, np.pi / 2, None, ALU.add))
                own.step(ve.tensor_scalar(wrap, cos_arg, np.pi, None, ALU.is_gt))
                own.step(ve.scalar_tensor_tensor(out=cos_arg, in0=wrap, scalar=-TWO_PI, in1=cos_arg, op0=ALU.mult,
                                                 op1=ALU.add))
                ve.tensor_scalar(cos_arg, cos_arg, 3.1415925, -3.1415925, ALU.min, ALU.max).then_inc(angle_ready, 1)
                ve.tensor_scalar(sin_arg, ang, 3.1415925, -3.1415925, ALU.min, ALU.max).then_inc(angle_ready, 1)
                dve.wait_ge(angle_ready, 2 * n + 2)
            dve.wait_ge(sin_ready, 4)
            cos_r, sin_r, cos_d, sin_d = [tables[:, n, :] for n in range(4)]
            dve.wait_ge(c_exp, 1)
            own.step(ve.tensor_scalar(small[:, 16:24], small[:, 16:24], 1.0, None, ALU.add))
            own.step(ve.reciprocal(small[:, 16:24], small[:, 16:24]))
            ve.tensor_tensor(small[:, 16:24], small[:, 16:24], parr("c"), ALU.mult).then_inc(tables_ready, 1)

            with dve.Fori(0, DEPTH) as lay:
                close = own.loop(lay, VEC_STEPS)
                dve.wait_ge(param2_in, lay * 16 + 16)
                lam = par2("lam").rearrange("p (n d) -> p n d", n=4)
                own.inc(ve.tensor_tensor_reduce(kvm[:, 0:64], lam[:, 0, :], lam[:, 1, :], 1.0, 0.0, ALU.mult, ALU.add,
                                                small[:, 24:25]))
                own.settle()
                ve.tensor_tensor_reduce(kvm[:, 0:64], lam[:, 2, :], lam[:, 3, :], 1.0, 0.0, ALU.mult, ALU.add,
                                        small[:, 25:26]).then_inc(lam_ready, 1)
                dve.wait_ge(lam_exp, lay + 1)
                own.step(ve.tensor_tensor(small[:, 28:29], small[:, 27:28], small[:, 26:27], ALU.subtract))
                own.step(ve.tensor_tensor(small[:, 28:29], small[:, 28:29], par2("neg_lam"), ALU.add))
                ve.tensor_tensor(small[:, 29:30], par2("gain_d"), par2("one_minus_lam"), ALU.mult).then_inc(lam_ready, 1)
                dve.wait_ge(lam_ready, lay * 2 + 2)
                ring.wait_done(dve, MOD + 11, lay * TURNS)
                own.step(ve.tensor_tensor(md, bank(6)[:, 0:48], par2("bmod"), ALU.add))
                for n in range(2):
                    e = ve.scalar_tensor_tensor(out=gains[:, n * KD:(n + 1) * KD], in0=md[:, 24 * n + 8:24 * n + 16],
                                                scalar=1.0, in1=par2(f"norm{n + 1}"), op0=ALU.add, op1=ALU.mult)
                own.step(e)
                dve.wait_ge(x_ready, lay * 2 + MIN_X)
                norm(lay * 2 + MIN_X, x3, gains[:, 0:KD], md[:, 0:8])
                dve.wait_ge(qk_product, lay * 5 + 1)
                dve.wait_ge(win_copied, lay * 7 + 1)
                rope(rqk, cos_r, sin_r, chunks(6, 4), qk_ready)
                for w in range(2):
                    part = dqk[:, 4 * w:4 * w + 4, :]
                    dve.wait_ge(qk_root, lay * 2 + (w + 1))
                    dve.wait_ge(win_copied, lay * 7 + (3 + w))
                    ve.scalar_tensor_tensor(out=part, in0=part, scalar=par2(("gain_q", "gain_k")[w]),
                                            in1=tmp_b.rearrange("p (k t) -> p k t", k=4), op0=ALU.mult,
                                            op1=ALU.mult).then_inc(qk_ready, 1)
                    dve.wait_ge(qk_ready, lay * 5 + (2 + 2 * w))
                    dve.wait_ge(qk_product, lay * 5 + (3 + 2 * w))
                    rope(part, cos_d, sin_d, chunks(6, 4), qk_ready)
                dve.wait_ge(gate_exp, lay + 1)
                gt = scratch[:, 0:1024]
                own.step(ve.tensor_scalar(gt, gt, 1.0, None, ALU.add))
                own.step(ve.reciprocal(gt, gt))
                flat = gates.rearrange("p k t -> p (k t)")
                ve.tensor_tensor(flat, flat, gt, ALU.mult).then_inc(gate_ready, 1)
                dve.wait_ge(gate_ready, lay + 1)
                mix = h3

                def norm_o(n, b, gain, k0, k1, gate):
                    width = (k1 - k0) * S
                    dve.wait_ge(o_root, lay * 3 + (n + 1))
                    o = ve.scalar_tensor_tensor(out=mix[:, k0:k1, :], in0=chunks(b, k1 - k0), scalar=gain,
                                                in1=tmp_b[:, 0:width].rearrange("p (k t) -> p k t", t=S),
                                                op0=ALU.mult, op1=ALU.mult)
                    if gate is None:
                        o.then_inc(mix_ready, 1)
                    else:
                        own.step(o)
                        ve.tensor_tensor(mix[:, k0:k1, :], mix[:, k0:k1, :], gate, ALU.mult).then_inc(mix_ready, 1)
                for h in range(4):
                    dve.wait_ge(r_scored, lay * 4 + (h + 1))
                    if h >= 2:
                        dve.wait_ge(r_used, lay * 4 + (h - 1))
                    ve.tensor_tensor(aT[h % 2], bank(h % 2).rearrange("p (r t) -> p r t", r=NT), decay[:, h],
                                     ALU.mult).then_inc(r_decayed, 1)
                norm_o(0, 2, par2("gain_r"), 0, 2, gates[:, 0:2, :])
                def d_mask(u):
                    r, p = u % 2, u % 2
                    dve.wait_ge(d_scored, lay * 8 + (u + 1))
                    if u >= 2:
                        dve.wait_ge(d_turned, lay * 8 + (u - 1))
                    dve.sem_inc(held, 1)
                    for w in range(2):
                        e = ve.tensor_tensor_reduce(att_d[p][:, w, :], bank(2 * p + w)[:, 0:S], mask_d[:, r, :],
                                                    1.0, -3e38, ALU.add, ALU.max, small[:, 30 + w:31 + w])
                    own.step(e)
                    ve.tensor_scalar(small[:, 32 + 2 * p:34 + 2 * p], small[:, 30:32], -QK_SCALE, None, ALU.mult
                                     ).then_inc(d_max, 1)
                    dve.wait_ge(d_max, lay * 8 + (u + 1))

                def d_sub(u):
                    p = u % 2
                    dve.wait_ge(d_exp, lay * 8 + (u + 1))
                    own.step(ve.reciprocal(small[:, 40:42], small[:, 36 + 2 * p:38 + 2 * p]))
                    own.inc(ve.tensor_scalar(small[:, 41:42], small[:, 41:42], small[:, 28:29], None, ALU.mult))
                    own.step(ve.tensor_scalar(att_d[p][:, 0, :], att_d[p][:, 0, :], small[:, 40:41], None, ALU.mult))
                    ve.scalar_tensor_tensor(out=att_d[p][:, 0, :], in0=att_d[p][:, 1, :], scalar=small[:, 41:42],
                                            in1=att_d[p][:, 0, :], op0=ALU.mult, op1=ALU.add).then_inc(d_diff, 1)
                    dve.wait_ge(d_diff, lay * 8 + (u + 1))
                dve.wait_ge(r_used, lay * 4 + 4)
                for u in range(8):
                    d_mask(u)
                    if u:
                        d_sub(u - 1)
                d_sub(7)
                dve.wait_ge(mix_ready, lay * 3 + 1)
                norm_o(1, 4, small[:, 29:30], 2, 6, None)
                logit = bank(0)[:, 0:S]
                dve.wait_ge(g_log, lay + 1)
                ve.scalar_tensor_tensor(out=la.rearrange("p r f -> p (r f)"), in0=logit, scalar=0.0,
                                        in1=scratch_b[:, 256:512], op0=ALU.min, op1=ALU.subtract).then_inc(g_la, 1)
                dve.wait_ge(g_exps, lay + 1)
                own.inc(ve.tensor_tensor(qe, gqk[:, 0, :], eg, ALU.mult))
                own.inc(ve.tensor_tensor(qsel, gqk[:, 0, :].unsqueeze(2).broadcast_to([P, S, 4]),
                                         con2("hsel").unsqueeze(1).broadcast_to([P, S, 4]), ALU.mult))
                own.inc(ve.memset(state, 0.0))
                ve.tensor_tensor(kd, kd, gqk[:, 1, :], ALU.mult).then_inc(g_keys, 1)

                def g_sub(v):
                    c, a = v // 2, 64 * (v // 2) + 32 * (v % 2)
                    if v >= 2:
                        dve.wait_ge(g_pair, lay * 8 + (v - 1))
                    ve.tensor_tensor(pair_d[v % 2], gT[:, a:a + 32].unsqueeze(2).broadcast_to([P, 32, 64]),
                                     gT[:, 64 * c:64 * c + 64].unsqueeze(1).broadcast_to([P, 32, 64]),
                                     ALU.subtract).then_inc(g_diff, 1)

                def g_mul(v):
                    c = v // 2
                    dve.wait_ge(g_dexp, lay * 8 + (v + 1))
                    ve.tensor_tensor(pair_d[v % 2], pair_d[v % 2],
                                     gqk[:, 1, 64 * c:64 * c + 64].unsqueeze(1).broadcast_to([P, 32, 64]),
                                     ALU.mult).then_inc(g_dk, 1)

                dve.wait_ge(g_log, lay + 1)
                dve.wait_ge(g_la, lay + 1)
                for v in range(8):
                    g_sub(v)
                    if v:
                        g_mul(v - 1)
                g_mul(7)
                for c in range(3):
                    dve.wait_ge(g_kv, lay * 3 + (c + 1))
                    own.step(ve.tensor_tensor(kvm, bank(7)[:, 0:256], con2("bdmask"), ALU.mult))
                    ve.scalar_tensor_tensor(out=state, in0=state, scalar=eg[:, 64 * c + 63:64 * c + 64], in1=kvm,
                                            op0=ALU.mult, op1=ALU.add).then_inc(g_state, 1)
                    dve.wait_ge(g_state, lay * 3 + (c + 1))
                dve.wait_ge(mix_ready, lay * 3 + 2)
                norm_o(2, 6, par2("gain_g"), 6, 8, gates[:, 2:4, :])
                for k in range(KD):
                    if k % 4 == 0:
                        ring.wait_done(dve, WOUT + k // 4, lay * TURNS)
                    e = ve.scalar_tensor_tensor(out=x3[:, k, :], in0=chunks(0, 8)[:, k, :], scalar=md[:, 16 + k:17 + k],
                                                in1=x3[:, k, :], op0=ALU.mult, op1=ALU.add)
                e.then_inc(x_ready, 1)
                dve.wait_ge(x_ready, lay * 2 + (MIN_X + 1))
                norm(lay * 2 + (MIN_X + 1), x3, gains[:, KD:2 * KD], md[:, 24:32])
                at = [64]

                def t(n):
                    at[0] += n
                    return route[:, at[0] - n:at[0]]
                score = route[:, 0:64].rearrange("p (r e) -> p r e", r=NT)
                biased, work = [t(64).rearrange("p (r e) -> p r e", r=NT) for _ in range(2)]
                oh = [t(64).rearrange("p (r e) -> p r e", r=NT) for _ in range(2)]
                both = t(64).rearrange("p (r e) -> p r e", r=NT)
                hi, lo = t(32).rearrange("p (g e) -> p g e", e=2), t(32).rearrange("p (g e) -> p g e", e=2)
                top, second_, gsum = [t(16) for _ in range(3)]
                best = t(2)
                wts = t(4).rearrange("p (r j) -> p r j", r=NT)
                wsum = t(2)
                dest = t(8).rearrange("p (r j) -> p r j", r=NT)
                cnt, nblk, incl, one32, startb = [t(32) for _ in range(5)]
                dcur = t(4).rearrange("p (r j) -> p r j", r=NT)
                slotcol = t(1)
                iota32 = con2("iota32").unsqueeze(1).broadcast_to([P, NT, E])

                dve.wait_ge(t_exp, lay + 1)
                own.step(ve.tensor_scalar(score, score, 1.0, None, ALU.add))
                own.step(ve.reciprocal(score, score))
                own.step(ve.tensor_tensor(biased, score, parr("router_b").unsqueeze(1).broadcast_to([P, NT, E]), ALU.add))
                quads = biased.rearrange("p r (g e) -> p (r g) e", e=EG)
                own.inc(ve.tensor_tensor(hi, quads[:, :, 0:2], quads[:, :, 2:4], ALU.max))
                own.step(ve.tensor_tensor(lo, quads[:, :, 0:2], quads[:, :, 2:4], ALU.min))
                own.inc(ve.tensor_tensor(top, hi[:, :, 0], hi[:, :, 1], ALU.max))
                own.inc(ve.tensor_tensor(second_, hi[:, :, 0], hi[:, :, 1], ALU.min))
                own.step(ve.tensor_tensor(gsum, lo[:, :, 0], lo[:, :, 1], ALU.max))
                own.step(ve.tensor_tensor(second_, second_, gsum, ALU.max))
                own.step(ve.tensor_tensor(gsum, top, second_, ALU.add))

                def first_best(values, out, iota, n):
                    own.step(ve.tensor_reduce(best, values, AX, ALU.max))
                    own.step(ve.tensor_tensor(out, values, best.unsqueeze(2).broadcast_to([P, NT, n]), ALU.is_equal))
                    own.step(ve.scalar_tensor_tensor(out=out, in0=out, scalar=-100.0, in1=iota, op0=ALU.mult, op1=ALU.add))
                    own.step(ve.tensor_reduce(best, out, AX, ALU.min))
                    own.step(ve.tensor_tensor(out, out, best.unsqueeze(2).broadcast_to([P, NT, n]), ALU.is_equal))
                g2 = gsum.rearrange("p (r g) -> p r g", r=NT)
                s2 = second_.rearrange("p (r g) -> p r g", r=NT)
                first_best(g2, s2, con2("iota8").unsqueeze(1).broadcast_to([P, NT, NG]), NG)
                own.step(ve.tensor_scalar(second_, second_, -NEG, NEG, ALU.mult, ALU.add))
                own.step(ve.tensor_tensor(quads, quads, second_.unsqueeze(2).broadcast_to([P, NT * NG, EG]), ALU.add))
                first_best(biased, oh[0], iota32, E)
                own.step(ve.scalar_tensor_tensor(out=biased, in0=oh[0], scalar=3 * NEG, in1=biased, op0=ALU.mult, op1=ALU.add))
                first_best(biased, oh[1], iota32, E)
                ve.tensor_tensor(both, oh[0], oh[1], ALU.add).then_inc(t_mask, 1)
                for j in range(2):
                    own.step(ve.tensor_tensor(work, score, oh[j], ALU.mult))
                    own.step(ve.tensor_reduce(wts[:, :, j], work, AX, ALU.add))
                own.step(ve.tensor_tensor(wsum, wts[:, :, 0], wts[:, :, 1], ALU.add))
                own.step(ve.reciprocal(wsum, wsum))
                own.step(ve.tensor_tensor(dest[:, :, 2:4], wts, wsum.unsqueeze(2).broadcast_to([P, NT, 2]), ALU.mult))
                dve.wait_ge(t_ranks, lay + 1)
                own.inc(ve.memset(one32, 1.0))
                own.step(ve.tensor_copy(cnt, bank(7)[:, 64:96]))
                own.step(ve.tensor_scalar(nblk, cnt, 0.0, None, ALU.is_gt))
                for j in range(1, S // SB):
                    own.step(ve.scalar_tensor_tensor(out=nblk, in0=cnt, scalar=float(SB * j), in1=nblk,
                                                     op0=ALU.is_gt, op1=ALU.add))
                own.step(ve.tensor_tensor_scan(incl, one32, nblk, 0.0, ALU.mult, ALU.add))
                own.step(ve.tensor_tensor(startb, incl, nblk, ALU.subtract))
                own.step(ve.tensor_scalar(startb, startb, float(SB), None, ALU.mult))
                own.step(ve.tensor_tensor(biased, bank(7)[:, 0:64].rearrange("p (r e) -> p r e", r=NT),
                                          startb.unsqueeze(1).broadcast_to([P, NT, E]), ALU.add))
                big = ends[0:1].rearrange("p (b e) -> p b e", b=BLOCKS)
                own.step(ve.tensor_tensor(big, incl[0:1].unsqueeze(1).broadcast_to([1, BLOCKS, E]),
                                          con2("iotab")[0:1].unsqueeze(2).broadcast_to([1, BLOCKS, E]), ALU.is_le))
                own.step(ve.tensor_reduce(passed[0:1], big, AX, ALU.add))
                ve.tensor_scalar(btab[0:1, :], passed[0:1], float(E - 1), None, ALU.min).then_inc(t_table, 1)
                for j in range(2):
                    own.step(ve.tensor_tensor(work, biased, oh[j], ALU.mult))
                    own.step(ve.tensor_reduce(dest[:, :, j], work, AX, ALU.add))
                for r in range(NT):
                    for j in range(4):
                        e = ve.tensor_scalar(diag[:, r, j, :], com("ident"), dest[:, r, j:j + 1], None, ALU.mult)
                e.then_inc(t_diag, 1)
                own.inc(ve.tensor_copy(dcur, dest[:, :, 0:2]))
                own.inc(ve.tensor_copy(slotcol, con2("slot0")))
                own.inc(ve.memset(ysb, 0.0))
                ve.memset(selT, 0.0).then_inc(selT_ready, 1)
                own.settle()

                def select(h, b, move):
                    if move:
                        dve.wait_ge(gathered, b - 1)
                        dve.wait_ge(sel_ready, b)
                        own.step(ve.tensor_scalar(dcur, dcur, -float(SB), None, ALU.add))
                    for r in range(NT):
                        e = ve.tensor_scalar(sel[h][:, r, :], con2("iota64"), dcur[:, r, 0:1], None, ALU.is_equal)
                    own.step(e)
                    for r in range(NT):
                        e = ve.scalar_tensor_tensor(out=sel[h][:, r, :], in0=con2("iota64"), scalar=dcur[:, r, 1:2],
                                                    in1=sel[h][:, r, :], op0=ALU.is_equal, op1=ALU.add)
                    e.then_inc(sel_ready, 1)

                def expert(h, n, b, turns, pair, last=False):
                    if not last:
                        select(1 - h, b + 1, True)
                    dve.wait_ge(gate_e, b + 1)
                    own.step(ve.tensor_scalar(sg, eb, 1.0, None, ALU.add))
                    own.step(ve.reciprocal(sg, sg))
                    own.step(ve.tensor_tensor(sg, sg, bank(5)[:, 0:256], ALU.mult))
                    ve.tensor_tensor(ue, sg, bank(5)[:, 256:512], ALU.mult).then_inc(ue_ready, 1)
                    if h == 0:
                        dve.wait_ge(scattered, pair + 1)
                        own.inc(ve.scalar_tensor_tensor(out=selT_b, in0=dbc[:, 0, :], scalar=slotcol, in1=dbc[:, 2, :],
                                                        op0=ALU.is_equal, op1=ALU.mult))
                        own.step(ve.scalar_tensor_tensor(out=selT, in0=dbc[:, 1, :], scalar=slotcol, in1=dbc[:, 3, :],
                                                         op0=ALU.is_equal, op1=ALU.mult))
                        ve.tensor_tensor(selT, selT, selT_b, ALU.add).then_inc(selT_ready, 1)
                        own.step(ve.tensor_scalar(slotcol, slotcol, float(2 * SB), None, ALU.add))
                    ring.wait_done(dve, n + 2, turns)
                    ve.tensor_copy(ysb[64 * h:64 * h + 64, 512:1024], bank(7)[64 * h:64 * h + 64]).then_inc(y_copied_v, 1)
                dve.wait_ge(t_spread_copied, lay + 1)
                select(0, None, False)
                with dve.Fori(0, PAIRS) as i:
                    close_i = own.loop(i, 13)
                    for h in range(2):
                        expert(h, MOE + 3 * h, lay * BLOCKS + i * 2 + h, lay * TURNS + i, lay * (PAIRS + 2) + i)
                    close_i(PAIRS)
                expert(0, MOE + 6 * PAIRS, lay * BLOCKS + (BLOCKS - 1), lay * TURNS, lay * (PAIRS + 2) + PAIRS, last=True)
                dve.wait_ge(scattered, lay * (PAIRS + 2) + (PAIRS + 2))
                for k in range(KD):
                    e = ve.scalar_tensor_tensor(out=x3[:, k, :], in0=chunks(0, 8)[:, k, :], scalar=md[:, 40 + k:41 + k],
                                                in1=x3[:, k, :], op0=ALU.mult, op1=ALU.add)
                e.then_inc(x_ready, 1)
                close(DEPTH)

    @block.tensor
    def _(pe):
        te = nc.tensor
        pe.wait_ge(consts_in, 48 if first else 32)

        def sum_x(n):
            pe.wait_ge(x_squared, n + 1)
            t3 = tmp.rearrange("p (k t) -> p k t", k=KD)
            for k in range(KD):
                e = te.matmul(bank(7)[:, 0:S], com("ones"), t3[:, k, :], start=(k == 0), stop=(k == KD - 1))
            e.then_inc(x_summed, 1)

        def feature_major(n, out, width, src, cols=512, c0=0, signal=True, turns=0):
            w = wcols(n, cols)
            for j in range(width):
                for k in range(KD):
                    e = te.matmul(out[:, j, :], w[:, k, c0 + 128 * j:c0 + 128 * j + 128], src[:, k, :],
                                  start=(k == 0), stop=(k == KD - 1))
            if signal:
                e.then_inc(slab_done, 1)

        def token_major(n, b, width, cols=512, c0=0, rows=P):
            w = wcols(n, cols)
            for r in range(S // rows):
                out = bank(b, 2)[0:rows, r * width:(r + 1) * width]
                for k in range(KD):
                    e = te.matmul(out, h3[:, k, r * rows:(r + 1) * rows], w[:, k, c0:c0 + width],
                                  start=(k == 0), stop=(k == KD - 1))
            return e

        def project_out(n, src, turns=0):
            for s in range(2):
                ring.wait_landed(pe, n + s, turns)
                feature_major(n + s, chunks(2 * s, 4), 4, src)

        def mlp(l, n):
            u3 = [a.rearrange("p (k t) -> p k t", k=4) for a in act3]

            def hidden(j, slab, turns=0, more=0):
                ring.wait_landed(pe, slab, turns)
                pe.wait_ge(relu_ready, more + 8 * l + j)
                feature_major(slab, chunks(4, 4), 4, h3)

            def down(j, slab, turns=0, more=0, start=False):
                ring.wait_landed(pe, slab, turns)
                pe.wait_ge(act_ready, more + 8 * l + j + 1)
                w = wrows(slab)
                for o in range(KD):
                    for k in range(4):
                        e = te.matmul(chunks(0, 8)[:, o, :], w[:, k, 128 * o:128 * o + 128], u3[j % 3][:, k, :],
                                      start=(start and k == 0 and o % 2 == 0), stop=False, skip_group_check=True)
                e.then_inc(slab_done, 1)
            pe.wait_ge(h_ready, 2 * l + 2)
            hidden(0, n)
            hidden(1, n + 1)
            down(0, n + 2, start=True)
            with pe.Fori(0, 2) as i:
                for jj in range(3):
                    hidden(2 + jj, n + 3 + 2 * jj, i, i * 3)
                    down(1 + jj, n + 4 + 2 * jj, i, i * 3)
            down(NF - 1, n + 2 * NF - 1)

        if first:
            sum_x(0)
            pe.wait_ge(h_ready, 1)
            with pe.Fori(0, GROUPS_A) as g:
                def proj(s):
                    n = A_QKV + s
                    ring.wait_landed(pe, n, g)
                    if s == 1:
                        pe.wait_ge(v_ready, g * 2)
                    elif s >= 2:
                        pe.wait_ge(q_normed, g * 4 + (s - 1))
                    if s < 4:
                        feature_major(n, chunks(2 * (s % 2), 4), 4, h3)
                    else:
                        token_major(n, 2 * (s % 2), 512).then_inc(slab_done, 1)

                def sums(s):
                    pe.wait_ge(q_squared, g * 4 + (s + 1))
                    pe.wait_ge(q_root, g * 4 + s)
                    for j in range(2):
                        e = te.matmul(bank(4 + j), com("bd64"), tmp_a[:, 512 * j:512 * j + 512], start=True, stop=True)
                    e.then_inc(q_summed, 1)

                def turn(s):
                    pe.wait_ge(q_normed, g * 4 + (s + 1))
                    pe.wait_ge(q_ready, g * 4 + s)
                    src = qk[:, bass.ds(g, 1), s // 2, 4 * (s % 2):4 * (s % 2) + 4, :].rearrange("p g k t -> p (g k t)")
                    for j in range(2):
                        e = te.matmul(bank(6 + j), com("rot16"), src[:, 512 * j:512 * j + 512], start=True, stop=True)
                    e.then_inc(q_turned, 1)
                proj(0)
                proj(1)
                sums(0)
                proj(2)
                sums(1)
                turn(0)
                proj(3)
                sums(2)
                turn(1)
                proj(4)
                sums(3)
                turn(2)
                proj(5)
                turn(3)
                pe.wait_ge(v_ready, g * 2 + 1)
            pe.wait_ge(v_ready, 2 * GROUPS_A)
            pe.wait_ge(q_ready, 4 * GROUPS_A)
            with pe.Fori(0, KD) as c:
                def scores(u):
                    r, h = u // 2, u % 2
                    pe.wait_ge(heads_staged, c + 1)
                    if u >= 2:
                        pe.wait_ge(masked, c * 4 + (u - 1))
                    rows = slice(64 * h, 64 * h + 64)
                    q = slice(r * P, (r + 1) * P)
                    te.matmul(bank(h)[:, 0:256], heads_now[rows, 0, 0, q], heads_now[rows, 0, 1, :], start=True, stop=True)
                    for g in (1, 2):
                        e = te.matmul(bank(h)[:, 128 + 128 * g:256 + 128 * g], heads_now[rows, g, 0, q],
                                      heads_now[rows, g, 1, q], start=True, stop=True)
                    e.then_inc(scored, 1)

                def turn_p(u):
                    pe.wait_ge(prob_ready, c * 4 + (u + 1))
                    for j in range(4):
                        e = te.transpose(bank(2)[:, 128 * j:128 * j + 128], att_s[u % 2][:, 128 * j:128 * j + 128],
                                         com("ident"))
                    e.then_inc(prob_turned, 1)

                def pv(u):
                    r, h = u // 2, u % 2
                    pe.wait_ge(prob_copied, c * 4 + (u + 1))
                    for j, (g, tile) in enumerate(((0, 0), (0, 1), (1, r), (2, r))):
                        v = vA[:, g, tile, bass.ds(c * P + 64 * h, 64)]
                        e = te.matmul(bank(o_bank[u])[:, 0:64], att_t[:, j, :], v, start=(j == 0), stop=(j == 3))
                    e.then_inc(pv_done, 1)

                def turn_o(r):
                    pe.wait_ge(o_scaled, c * 4 + (2 * r + 2))
                    pe.wait_ge(o_copied, c * 2 + r)
                    te.transpose(bank(6)[:, 0:P], o_rows, com("ident")).then_inc(o_turned, 1)
                scores(0)
                scores(1)
                turn_p(0)
                pv(0)
                scores(2)
                turn_p(1)
                pv(1)
                scores(3)
                turn_o(0)
                turn_p(2)
                pv(2)
                turn_p(3)
                pv(3)
                turn_o(1)
                pe.wait_ge(masked, c * 4 + 4)
            pe.wait_ge(o_copied, 2 * KD)
            project_out(A_WO, h3)
            sum_x(1)
            mlp(0, MLP0)
            sum_x(2)
            pe.wait_ge(h_ready, 3)
            for s in range(2):
                for j, (b, sm) in enumerate(((0, c_copied), (2, u_ready), (4, y_ready))):
                    ring.wait_landed(pe, B_WIN + 3 * s + j)
                    if s:
                        pe.wait_ge(sm, s)
                    feature_major(B_WIN + 3 * s + j, chunks(b, 4), 4, h3)
            pe.wait_ge(y_ready, 2)
            project_out(B_WOUT, mixB)
            sum_x(3)
            mlp(1, MLP1)

        if second:
            if not first:
                for _ in range(SLOTS):
                    te.matmul(bank(0)[:, 0:1], com("ones"), com("ones")[:, 0:1], start=True, stop=True).then_inc(slab_done, 1)
            pe.wait_ge(tables_ready, 1)
            with pe.Fori(0, DEPTH) as lay:
                turns = lay * TURNS
                pe.wait_ge(x_ready, lay * 2 + MIN_X)
                sum_x(lay * 2 + MIN_X)
                with pe.Fori(0, 2) as i:
                    for s in range(6):
                        ring.wait_landed(pe, MOD + s, lay * TURNS + i)
                        w = wcols(MOD + s)
                        for j in range(4):
                            out = bank(6)[:, bass.ds(i * 24 + (4 * s + j), 1)]
                            for k in range(KD):
                                e = te.matmul(out, w[:, k, 128 * j:128 * j + 128], small[:, 16 + k:17 + k],
                                              start=(k == 0), stop=(k == KD - 1))
                        e.then_inc(slab_done, 1)
                pe.wait_ge(h_ready, lay * 2 + (MIN_X + 1))

                def win(s):
                    b = (0, 3)[s % 2]
                    n = WIN + s
                    ring.wait_landed(pe, n, turns)
                    if s >= 2:
                        pe.wait_ge(win_copied, lay * 7 + (s - 1))
                    if s == 0 or s == 2 or s == 3:
                        feature_major(n, chunks(b, 4), 4, h3)
                    elif s == 1:
                        token_major(n, b, 256)
                        feature_major(n, chunks(b + 1, 2), 2, h3, c0=256)
                    elif s == 4:
                        token_major(n, b, 512).then_inc(slab_done, 1)
                    elif s == 5:
                        feature_major(n, chunks(b, 2), 2, h3, signal=False)
                        token_major(n, b + 1, 256, c0=256, rows=64).then_inc(slab_done, 1)
                    else:
                        cols = IN_WIDTH - 6 * 512
                        w = wcols(n, cols)
                        for k in range(KD):
                            te.matmul(bank(b)[0:16, 0:S], w[:, k, 0:16], h3[:, k, :], start=(k == 0), stop=(k == KD - 1))
                        feature_major(n, chunks(b + 1, 2), 2, h3, cols=cols, c0=16)

                def qk_mm(name, src):
                    src = src.rearrange("p k t -> p (k t)") if len(src.shape) == 3 else src
                    m = con2(name) if name == "rot64" else com(name)
                    for j in range(2):
                        e = te.matmul(bank(6 + j), m, src[:, 512 * j:512 * j + 512], start=True, stop=True)
                    e.then_inc(qk_product, 1)
                win(0)
                win(1)
                pe.wait_ge(win_copied, lay * 7 + 1)
                qk_mm("rot64", rqk)
                win(2)
                win(3)
                pe.wait_ge(dq_squared, lay * 2 + 1)
                pe.wait_ge(qk_ready, lay * 5 + 1)
                qk_mm("bd64", tmp_a)
                win(4)
                pe.wait_ge(qk_ready, lay * 5 + 2)
                qk_mm("rot16", dqk[:, 0:4, :])
                win(5)
                pe.wait_ge(dq_squared, lay * 2 + 2)
                pe.wait_ge(qk_ready, lay * 5 + 3)
                qk_mm("bd64", scratch_b[:, 0:1024])
                win(6)
                pe.wait_ge(qk_ready, lay * 5 + 4)
                qk_mm("rot16", dqk[:, 4:8, :])

                def sum_o(n, width, m, b):
                    pe.wait_ge(o_squared, lay * 3 + (n + 1))
                    for j in range(width // 512):
                        e = te.matmul(bank(b + j), com(m), tmp_a[:, 512 * j:512 * j + 512], start=True, stop=True)
                    e.then_inc(o_summed, 1)
                pe.wait_ge(win_copied, lay * 7 + 7)

                def r_scores(h):
                    rows = slice(64 * (h % 2), 64 * (h % 2) + 64)
                    if h >= 2:
                        pe.wait_ge(r_decayed, lay * 4 + (h - 1))
                    for r in range(NT):
                        e = te.matmul(bank(h % 2)[:, r * S:(r + 1) * S], rqk[rows, 2 + h // 2, r * P:(r + 1) * P],
                                      rqk[rows, h // 2, :], start=True, stop=True)
                    e.then_inc(r_scored, 1)

                def r_values(h):
                    pe.wait_ge(r_decayed, lay * 4 + (h + 1))
                    out = bank(2)[64 * (h % 2):64 * (h % 2) + 64, S * (h // 2):S * (h // 2) + S]
                    for r in range(NT):
                        e = te.matmul(out, rv[:, r, 64 * h:64 * h + 64], aT[h % 2][:, r, :], start=(r == 0),
                                      stop=(r == NT - 1))
                    e.then_inc(r_used, 1)
                r_scores(0)
                for h in range(1, 4):
                    r_scores(h)
                    r_values(h - 1)
                r_values(3)
                sum_o(0, 512, "bd64", 3)
                pe.wait_ge(mix_ready, lay * 3 + 1)
                pe.wait_ge(qk_ready, lay * 5 + 5)

                def d_scores(u):
                    h, r = u // 2, u % 2
                    if u >= 2:
                        pe.wait_ge(d_max, lay * 8 + (u - 1))
                    for w in range(2):
                        rows = slice(64 * w, 64 * w + 64)
                        e = te.matmul(bank(2 * (u % 2) + w)[:, 0:S], dqk[rows, h, r * P:(r + 1) * P],
                                      dqk[rows, 4 + h, :], start=True, stop=True)
                    e.then_inc(d_scored, 1)

                def d_turn(u):
                    pe.wait_ge(d_diff, lay * 8 + (u + 1))
                    if u >= 2:
                        pe.wait_ge(d_copied, lay * 8 + (u - 1))
                    for k in range(NT):
                        e = te.transpose(bank(6 + u % 2)[:, k * P:(k + 1) * P], att_d[u % 2][:, 0, k * P:(k + 1) * P],
                                         com("ident"))
                    e.then_inc(d_turned, 1)

                def d_values(h):
                    pe.wait_ge(d_copied, lay * 8 + (2 * h + 2))
                    for k in range(NT):
                        e = te.matmul(chunks(4, 4)[:, h, :], dv[:, k, 128 * h:128 * h + 128], aTd[h % 2][:, k, :],
                                      start=(k == 0), stop=(k == NT - 1))
                    e.then_inc(d_out, 1)
                d_scores(0)
                for u in range(8):
                    if u < 7:
                        d_scores(u + 1)
                    d_turn(u)
                    if u >= 2 and u % 2 == 0:
                        d_values(u // 2 - 1)
                d_values(3)
                sum_o(1, 1024, "ones", 6)
                for r in range(NT):
                    out = bank(0)[:, r * P:(r + 1) * P]
                    te.matmul(out, ga[0:16, r * P:(r + 1) * P], par2("wa2")[0:16], start=True, stop=False)
                    e = te.matmul(out, com("ones")[0:1, :], par2("ba")[0:1], start=False, stop=True)
                e.then_inc(g_logit, 1)
                pe.wait_ge(g_la, lay + 1)
                for r in range(NT):
                    e = te.matmul(bank(1)[:, r * P:(r + 1) * P], la[:, r, :], con2("tri"), start=True, stop=True)
                e.then_inc(g_cum, 1)
                pe.wait_ge(g_keys, lay + 1)
                pe.sem_inc(held, 1)
                for c in range(4):
                    e = te.transpose(bank(2)[0:64, c * P:(c + 1) * P], kd[:, 64 * c:64 * c + 64], com("ident"))
                e.then_inc(g_keysT, 1)
                pe.wait_ge(mix_ready, lay * 3 + 2)
                for v in range(8):
                    t0 = 32 * v
                    pe.wait_ge(g_dk, lay * 8 + (v + 1))
                    c = v // 2
                    if v % 2 == 0 and c >= 2:
                        pe.wait_ge(g_acopy, lay * 4 + (c - 1))
                    for i in range(32):
                        at = 4 * (32 * (v % 2) + i)
                        e = te.matmul(bank(4 + c % 2)[0:64, at:at + 4], pair_d[v % 2][:, i, :],
                                      qsel[:, t0 + i, :], start=True, stop=True)
                    e.then_inc(g_pair, 1)
                pe.wait_ge(g_keysC, lay + 1)
                for c in range(4):
                    t = slice(64 * c, 64 * c + 64)
                    pe.wait_ge(g_acopy, lay * 4 + (c + 1))
                    pe.wait_ge(g_state, lay * 3 + c)
                    a_c = a_gla[0:64, 256 * c:256 * c + 256].rearrange("p (t h) -> p h t", h=4)
                    for j in range(2):
                        out = chunks(6, 2)[:, j, t]
                        te.matmul(out, state[:, 128 * j:128 * j + 128], qe[:, t], start=True, stop=False,
                                  skip_group_check=True)
                        for w in range(2):
                            h = 2 * j + w
                            e = te.matmul(chunks(6, 2)[64 * w:64 * w + 64, j, t], gv[0:64, c, 64 * h:64 * h + 64],
                                          a_c[:, h, :], start=False, stop=True, skip_group_check=True)
                    if c == 3:
                        e.then_inc(g_out, 1)
                    else:
                        te.matmul(bank(7)[:, 0:256], kdt[0:64, c, :], gv[0:64, c, :], start=True, stop=True
                                  ).then_inc(g_kv, 1)
                sum_o(2, 512, "bd64", 3)
                pe.wait_ge(mix_ready, lay * 3 + 3)
                project_out(WOUT, h3, turns)
                sum_x(lay * 2 + (MIN_X + 1))
                pe.wait_ge(h_ready, lay * 2 + (MIN_X + 2))
                for r in range(NT):
                    for k in range(KD):
                        e = te.matmul(bank(6)[:, r * E:(r + 1) * E], h3[:, k, r * P:(r + 1) * P], router[:, k, :],
                                      start=(k == 0), stop=(k == KD - 1))
                e.then_inc(t_logits, 1)
                for r in range(NT):
                    for k in range(KD):
                        e = te.transpose(bank(2 * r, 2)[:, k * P:(k + 1) * P], h3[:, k, r * P:(r + 1) * P], com("ident"))
                e.then_inc(t_rows, 1)
                pe.wait_ge(t_mask, lay + 1)
                both = route[:, 64 + 4 * 64:64 + 5 * 64].rearrange("p (r e) -> p r e", r=NT)
                te.matmul(bank(7)[:, 0:32], con2("before"), both[:, 0, :], start=True, stop=True)
                te.matmul(bank(7)[:, 32:64], con2("before"), both[:, 1, :], start=True, stop=False)
                te.matmul(bank(7)[:, 32:64], com("ones"), both[:, 0, :], start=False, stop=True)
                te.matmul(bank(7)[:, 64:96], com("ones"), both[:, 0, :], start=True, stop=False)
                te.matmul(bank(7)[:, 64:96], com("ones"), both[:, 1, :], start=False, stop=True).then_inc(t_ranks, 1)
                pe.wait_ge(t_diag, lay + 1)
                for j in range(4):
                    for r in range(NT):
                        e = te.matmul(chunks(4, 4)[:, j, r * P:(r + 1) * P], com("ones"), diag[:, r, j, :], start=True,
                                      stop=True)
                e.then_inc(t_spread, 1)
                pe.wait_ge(t_rows_copied, lay + 1)
                pe.wait_ge(t_spread_copied, lay + 1)
                for j in range(4):
                    te.matmul(bank(j), zeros, hT[:, 0:512], start=True, stop=False, skip_group_check=True)

                def gather(h, b):
                    pe.wait_ge(sel_ready, b + 1)
                    pe.wait_ge(xg_ready, b)
                    for k in range(KD):
                        for r in range(NT):
                            e = te.matmul(bank(4)[:, SB * k:SB * k + SB], h2tok[:, r, k * P:(k + 1) * P], sel[h][:, r, :],
                                          start=(r == 0), stop=(r == NT - 1))
                    e.then_inc(gathered, 1)

                def scatter(pair, slots, b):
                    pe.wait_ge(selT_ready, pair + 1)
                    pe.wait_ge(y_copied_a, b)
                    pe.wait_ge(y_copied_v, b)
                    for k in range(KD):
                        e = te.matmul(chunks(0, 8)[:, k, :], ysb[0:slots, k * P:(k + 1) * P], selT[0:slots, :],
                                      start=False, stop=False, skip_group_check=True)
                    e.then_inc(scattered, 1)

                def expert(h, n, b, turns, pair, last=False):
                    pe.wait_ge(xg_ready, b + 1)
                    pe.wait_ge(ue_ready, b)
                    for m in range(2):
                        ring.wait_landed(pe, n + m, turns)
                        w = wcols(n + m)
                        for j in range(4):
                            out = bank(5)[:, 256 * m + 64 * j:256 * m + 64 * j + 64]
                            for k in range(KD):
                                e = te.matmul(out, w[:, k, 128 * j:128 * j + 128], xg[h][:, k, :], start=(k == 0),
                                              stop=(k == KD - 1))
                        e.then_inc(slab_done, 1)
                    if h == 0:
                        scatter(pair, 2 * SB, b)
                    if not last:
                        gather(1 - h, b + 1)
                    pe.wait_ge(ue_ready, b + 1)
                    pe.wait_ge(y_copied_a, b)
                    pe.wait_ge(y_copied_v, b)
                    ring.wait_landed(pe, n + 2, turns)
                    w = wrows(n + 2)
                    for o in range(2):
                        for k in range(4):
                            e = te.matmul(bank(6 + o)[64 * h:64 * h + 64], ue[:, SB * k:SB * k + SB],
                                          w[:, k, 512 * o:512 * o + 512], start=(k == 0), stop=(k == 3))
                    e.then_inc(slab_done, 1)
                gather(0, lay * BLOCKS)
                with pe.Fori(0, PAIRS) as i:
                    for h in range(2):
                        expert(h, MOE + 3 * h, lay * BLOCKS + i * 2 + h, lay * TURNS + i, lay * (PAIRS + 2) + i)
                expert(0, MOE + 6 * PAIRS, lay * BLOCKS + (BLOCKS - 1), lay * TURNS, lay * (PAIRS + 2) + PAIRS, last=True)
                scatter(lay * (PAIRS + 2) + (PAIRS + 1), SB, lay * BLOCKS + BLOCKS)

    ctx.close()


def constants():
    f = np.float32
    p = np.arange(P)
    ident = np.eye(P, dtype=f)
    bd64 = (p[:, None] // DH == p[None, :] // DH).astype(f)

    def rot(half):
        m = np.zeros((P, P), f)
        for head in range(0, P, DH):
            for j in range(half):
                m[head + j + half, head + j] = -1
                m[head + j, head + j + half] = 1
        return m
    common = np.concatenate([ident, np.ones((P, P), f), bd64, rot(8)], 1)

    order = np.array([16 * m + 4 * b + a for a in range(4) for b in range(4) for m in range(16)])
    inv = (500000.0 ** (-np.arange(0, 16, 2, dtype=np.float64) / 16)).astype(f)
    ang = (np.arange(S, dtype=f)[order][None, :] * inv[:, None]).astype(f)
    cos_a, sin_a = np.ones((P, S), f), np.zeros((P, S), f)
    for head in range(0, P, DH):
        for half in range(2):
            cos_a[head + 8 * half:head + 8 * half + 8] = np.cos(ang)
            sin_a[head + 8 * half:head + 8 * half + 8] = np.sin(ang)
    mask_a = np.zeros((P, NT, 512), f)
    for r in range(NT):
        q = order[r * P:(r + 1) * P]
        at = 0
        for dil, k in zip(DILATIONS, (order, q, q)):
            far = np.abs(q[:, None] - k[None, :])
            ok = (far % dil == 0) & (far <= RADIUS * dil)
            mask_a[:, r, at:at + len(k)] = np.where(ok, 0, NEG)
            at += len(k)
    const_a = np.concatenate([cos_a, sin_a, mask_a.reshape(P, -1)], 1)

    same = p[:, None] // CHUNK == p[None, :] // CHUNK
    tri = (same & (p[:, None] <= p[None, :])).astype(f) / 16
    before = (p[:, None] < p[None, :]).astype(f)
    bdmask = (p[:, None] // GLA_DK == np.arange(256)[None, :] // 64).astype(f)
    hsel = (p[:, None] // GLA_DK == np.arange(4)[None, :]).astype(f)

    def inverse(half, theta):
        power = np.power(theta, np.arange(half, dtype=np.float64) / half).astype(f)
        return (f(1) / power).astype(f)
    inv_r, inv_d = np.zeros((P, 1), f), np.zeros((P, 1), f)
    for head in range(0, P, DH):
        for half in range(2):
            inv_r[head + 32 * half:head + 32 * half + 32, 0] = inverse(32, 10000.0)
            inv_d[head + 8 * half:head + 8 * half + 8, 0] = inverse(8, 500000.0)
    t = np.arange(S)
    decay = np.zeros((P, 4, NT, S), f)
    for h in range(4):
        g = 1.0 - 2.0 ** (-5.0 - h)
        full = g ** np.abs(t[:, None] - t[None, :]).astype(np.float64) * SCALE
        full = np.where(t[:, None] // CHUNK <= t[None, :] // CHUNK, full, 0)
        decay[:, h] = full.reshape(NT, P, S).transpose(1, 0, 2)
    mask_d = np.where(t[None, :] // CHUNK <= t[:, None] // CHUNK, 0, NEG).astype(f)
    mask_d = mask_d.reshape(NT, P, S).transpose(1, 0, 2)

    def row(n):
        return np.broadcast_to(np.arange(n, dtype=f), (P, n))
    const_2 = np.concatenate([
        rot(32), tri, before, bdmask, hsel, inv_r, inv_d, decay.reshape(P, -1), mask_d.reshape(P, -1),
        row(SB), row(E), row(NG), row(BLOCKS), p[:, None].astype(f)], 1)
    return [np.ascontiguousarray(a, f) for a in (common, const_a, const_2)] + [order]


def by_partition(v):
    return np.asarray(v).reshape(-1, P).T


def kernel(**inputs):
    import concourse.bacc as bacc
    from concourse.bass_utils import run_bass_kernel_spmd

    i = {k: np.asarray(v) for k, v in inputs.items()}
    f = np.float32
    common, const_a, const_2, order = constants()
    x = i["x"][0]
    twice = lambda v: np.tile(v, P // v.shape[0])[:, None]
    param_1 = np.concatenate(
        [by_partition(i["norm1"].reshape(-1)), by_partition(i["norm2"].reshape(-1))]
        + [twice(i[n][0, g]) for g in range(GROUPS_A) for n in ("a_q_gain", "a_k_gain")]
        + [by_partition(i["b_conv"].reshape(-1))], 1)
    param_2 = []
    for l in range(DEPTH):
        lam = np.stack([i[n + "_2"][l] for n in ("lam_q1", "lam_k1", "lam_q2", "lam_k2")]).reshape(1, -1)
        wa2 = np.zeros((P, P), f)
        wa2[:16] = i["gla_w_a2_2"][l]
        param_2.append(np.concatenate([
            by_partition(i["b_mod_2"][l]), by_partition(i["norm1_g_2"][l]), by_partition(i["norm2_g_2"][l]),
            twice(i["ret_norm_g_2"][l]), twice(i["diff_q_g_2"][l]), twice(i["diff_k_g_2"][l]),
            twice(i["diff_sub_g_2"][l]), twice(i["gla_norm_g_2"][l]),
            np.full((P, 1), 1.0 - LAM_INIT[l], f), np.full((P, 1), -LAM_INIT[l], f),
            np.broadcast_to(lam, (P, 4 * DH)), wa2, np.broadcast_to(i["gla_b_a_2"][l], (P, P))], 1))
    param_r = np.concatenate([
        i["router_w_2"].reshape(KD, P, E).transpose(1, 0, 2).reshape(P, -1),
        np.broadcast_to(i["router_b_2"], (P, E)), by_partition(i["c_2"][0])], 1)
    feature_major = lambda a: a.T.reshape(KD, P, S).transpose(1, 0, 2).reshape(P, -1)
    arrays = {
        "x_t": feature_major(x), "x_by_residue": feature_major(x[order]),
        "common": common, "const_a": const_a, "const_2": const_2,
        "param_1": param_1, "param_2": np.stack(param_2), "param_r": param_r,
        "positions": np.broadcast_to(i["positions_2"], (P, S)),
        "a_wqkv": i["a_wqkv"], "a_wo": i["a_wo"], "b_win": i["b_win"], "b_wout": i["b_wout"],
        "mlp_w1": i["mlp_w1"], "mlp_w2": i["mlp_w2"], "w_mod": i["w_mod_2"], "w_in": i["w_in_2"],
        "w_out": i["w_out_2"], "w_gate": i["w_gate_2"], "w_up": i["w_up_2"], "w_down": i["w_down_2"],
    }
    nc = bacc.Bacc("TRN2", target_bir_lowering=False, num_devices=1)
    arrays = {f"in_{k}": np.ascontiguousarray(a) for k, a in arrays.items()}
    args = [nc.dram_tensor(k, a.shape, mybir.dt.from_np(a.dtype), kind="ExternalInput").ap() for k, a in arrays.items()]
    out = nc.dram_tensor("out", (P, KD * S), F32, kind="ExternalOutput").ap()
    program(nc, *args, out, **FLAGS)
    r = run_bass_kernel_spmd(nc, [arrays], core_ids=[0])
    got = np.asarray(r.results[0]["out"])
    return got.reshape(P, KD, S).transpose(2, 1, 0).reshape(1, S, D)


FLAGS = {}
```

```python
from contextlib import ExitStack

import numpy as np

import concourse.bass as bass
from concourse import mybir

F32 = mybir.dt.float32
I32 = mybir.dt.int32
ALU = mybir.AluOpType
ACT = mybir.ActivationFunctionType
AX = mybir.AxisListType.X

P = 128
D = 1024
KD = D // P
S = 256
NT = S // P
EPS = 1e-6
SLOTS = 6
SLAB = 4096
HEADS = 16
DH = 64
GROUPS_A = 3
DILATIONS = (1, 4, 16)
RADIUS = 64
FF = 4096
NF = FF // 512
CHUNK = 64
DEPTH = 2
E = 32
EG = 4
NG = E // EG
FE = 512
SB = 64
HOME_PAIRS = E // 2
OVER = (2 * S - E) // SB
OVER_PAIRS = OVER // 2
BLOCKS = E + OVER
PAIRS = BLOCKS // 2
IN_WIDTH = 3344
NEG = -1e30
SCALE = DH ** -0.5
QK_SCALE = SCALE * DH
GLA_HEADS, GLA_DK = 4, 32
LAM_INIT = [0.8 - 0.6 * float(np.exp(-0.3 * l)) for l in range(DEPTH)]

A_QKV = 0
A_WO = A_QKV + 6 * GROUPS_A
MLP0 = A_WO + 2
MLP_SLABS = 2 * NF + 12
B_WIN = MLP0 + MLP_SLABS
B_WOUT = B_WIN + 6
MLP1 = B_WOUT + 2
WIN = MLP1 + MLP_SLABS
WOUT = WIN + 7
MOE = WOUT + 2
OVERS = MOE + 6 * HOME_PAIRS
TURNS = (7 + 2 + 3 * BLOCKS) // SLOTS
assert TURNS * SLOTS == 7 + 2 + 3 * BLOCKS and BLOCKS % 2 == 1

COMMON = {"ident": 128, "ones": 128, "bd64": 128, "rot16": 128}
COND = KD
CONST_A = {"cos_a": S, "sin_a": S, "mask_a": NT * 512}
CONST_2 = {"rot64": 128, "tri": 128, "before": 128, "bdmask": 256, "hsel": 4, "inv_r": 1, "inv_d": 1,
           "decay": 4 * NT * S, "mask_d": NT * S, "iota128": 2 * SB, "iota32": 32, "iota8": 8,
           "iotab": OVER, "slot0": 1}
PARAM_1 = {"norm1": 2 * KD, "norm2": 2 * KD, "gain_a": 2 * GROUPS_A, "conv": 3 * KD}
PARAM_2 = {"bmod": 48, "norm1": KD, "norm2": KD, "gain_r": 1, "gain_q": 1, "gain_k": 1, "gain_d": 1,
           "gain_g": 1, "one_minus_lam": 1, "neg_lam": 1, "lam": 4 * DH, "wa2": 128, "ba": 128}
PARAM_R = {"router": KD * E, "router_b": E}


def columns(table):
    at, out = 0, {}
    for name, n in table.items():
        out[name] = (at, at + n)
        at += n
    return out, at


def round_bits(x, bits):
    m, e = np.frexp(x)
    return float(np.ldexp(np.round(m * 2 ** bits), e - bits))


TWO_PI = 2 * np.pi
PI_1 = round_bits(TWO_PI, 8)
PI_2 = round_bits(TWO_PI - PI_1, 8)
PI_3 = TWO_PI - PI_1 - PI_2
MAGIC = 1.5 * 2.0 ** 23

VEC_STEPS = 272
ACT_STEPS = 26


class Ring:

    def __init__(self, slots, landed, done):
        self.slots, self.landed, self.done = slots, landed, done

    def tile(self, n):
        return self.slots[:, n % SLOTS, :]

    def wait_landed(self, eng, n, turns=0):
        eng.wait_ge(self.landed[n % SLOTS], (turns + (n // SLOTS + 1)) * 16)

    def wait_done(self, eng, n, turns=0):
        eng.wait_ge(self.done, turns * SLOTS + (n + 1))


class Steps:

    def __init__(self, eng, sem):
        self.eng, self.sem, self.n, self.turns = eng, sem, 0, 0

    def inc(self, ins):
        ins.then_inc(self.sem, 1)
        self.n += 1

    def settle(self):
        self.eng.wait_ge(self.sem, self.turns + self.n)

    def step(self, ins):
        self.inc(ins)
        self.settle()

    def loop(self, i, per):
        outer, start = self.turns, self.n
        self.turns = outer + i * per

        def end(times):
            assert self.n - start == per, (self.n - start, per)
            self.turns, self.n = outer, start + per * times
        return end


def program(nc, x_d, xp_d, common_d, const_a_d, const_2_d, param_1_d, param_2_d, param_r_d, pos_d,
            a_wqkv, a_wo, b_win, b_wout, mlp_w1, mlp_w2, w_mod, w_in, w_out, w_gate, w_up, w_down,
            out_d):
    ctx = ExitStack()
    enter = ctx.enter_context

    def sb(name, n, dt=F32):
        return enter(nc.sbuf_tensor(name, [P, n], dt))[:, :]

    def sem(name):
        return enter(nc.semaphore(name))

    ring_sb = enter(nc.sbuf_tensor("ring", [P, SLOTS, SLAB], F32))
    xT = sb("xT", KD * S)
    hT = sb("hT", KD * S)
    tmp = sb("tmp", 2048)
    rstd = sb("rstd", S)
    small = sb("small", 64)
    com_c, com_n = columns(COMMON)
    common = sb("common", com_n + COND)
    cond = common[:, com_n:com_n + COND]
    p1_c, p1_n = columns(PARAM_1)
    param_1 = sb("param_1", p1_n)
    ARENA = 21504
    arena = sb("arena", ARENA)
    x3 = xT.rearrange("p (k t) -> p k t", k=KD)
    h3 = hT.rearrange("p (k t) -> p k t", k=KD)
    tmp_a, tmp_b = tmp[:, 0:1024], tmp[:, 1024:2048]

    def com(name):
        a, b = com_c[name]
        return common[:, a:b]

    def par1(name):
        a, b = p1_c[name]
        return param_1[:, a:b]

    def carve():
        at = [0]

        def take(n):
            at[0] += n
            assert at[0] <= ARENA, at
            return arena[:, at[0] - n:at[0]]
        return take

    take = carve()
    qk = take(GROUPS_A * 2 * KD * S).rearrange("p (g w k t) -> p g w k t", g=GROUPS_A, w=2, k=KD)
    vA = take(GROUPS_A * NT * D).rearrange("p (g r f) -> p g r f", g=GROUPS_A, r=NT)
    xp = vA[:, :, :, :].rearrange("p g r f -> p (g r f)")[:, 0:KD * S].rearrange("p (k t) -> p k t", k=KD)
    ca_c, ca_n = columns(CONST_A)
    const_a = take(ca_n)
    heads_now = take(GROUPS_A * 2 * S).rearrange("p (g w t) -> p g w t", g=GROUPS_A, w=2)
    o_rows = rstd[:, 0:P]
    att_s = [tmp[:, 0:512], tmp[:, 512:1024]]
    att_t = tmp[:, 1024:1536].rearrange("p (j q) -> p j q", j=4)
    o_bank = (3, 4, 5, 7)
    cos_a = const_a[:, ca_c["cos_a"][0]:ca_c["cos_a"][1]]
    sin_a = const_a[:, ca_c["sin_a"][0]:ca_c["sin_a"][1]]
    mask_a = const_a[:, ca_c["mask_a"][0]:ca_c["mask_a"][1]].rearrange("p (r n) -> p r n", r=NT)

    modcols = arena[:, ARENA - 96:ARENA].rearrange("p (l n) -> p l n", l=DEPTH)
    take = carve()
    c2_c, c2_n = columns(CONST_2)
    const_2 = take(c2_n)
    p2_c, p2_n = columns(PARAM_2)
    param_2 = take(p2_n)
    pr_c, pr_n = columns(PARAM_R)
    param_r = take(pr_n)
    tables = take(4 * S).rearrange("p (n t) -> p n t", n=4)
    md = take(48)
    gains = take(2 * KD)
    zeros = take(P)
    base2 = c2_n + p2_n + pr_n + 4 * S + 48 + 2 * KD + P

    def carve2():
        at = [base2]

        def take(n):
            at[0] += n
            assert at[0] <= ARENA - 96, (at, ARENA)
            return arena[:, at[0] - n:at[0]]
        return take

    take = carve2()
    act3 = [take(1024) for _ in range(3)]
    conv_u = take(1024).rearrange("p (k t) -> p k t", k=4)
    conv_y = take(1024).rearrange("p (k t) -> p k t", k=4)
    mixB = take(KD * S).rearrange("p (k t) -> p k t", k=KD)
    mod_rows = take(512)
    cond32 = take(KD * 32).rearrange("p (k c) -> p k c", k=KD)
    angles = take(4 * S).rearrange("p (n t) -> p n t", n=4)
    pos_i, pos_f, ang, turns_, wrap = [take(S) for _ in range(5)]
    pos_i = pos_i.bitcast(I32)

    take = carve2()
    rqk = take(4 * S).rearrange("p (k t) -> p k t", k=4)
    gates = take(4 * S).rearrange("p (k t) -> p k t", k=4)
    dqk = take(8 * S).rearrange("p (k t) -> p k t", k=8)
    rv = take(NT * 256).rearrange("p (r f) -> p r f", r=NT)
    dv = take(NT * 512).rearrange("p (r f) -> p r f", r=NT)
    gv = take(4 * 256).rearrange("p (c f) -> p c f", c=4)
    gqk = take(2 * S).rearrange("p (k t) -> p k t", k=2)
    ga = take(S)
    gT, eg, qe, kd = take(S), take(S), take(S), take(S)
    qsel = take(4 * S).rearrange("p (t h) -> p t h", h=4)
    a_gla = rqk.rearrange("p k t -> p (k t)")
    state = take(256)
    kvm = take(256)
    scratch, scratch_b = take(2048), take(2048)
    pair_d = [a[:, n:n + 16 * CHUNK].rearrange("p (t s) -> p t s", t=16) for a in (scratch, scratch_b)
              for n in (0, 16 * CHUNK)]
    kdt = rv.rearrange("p r f -> p (r f)").rearrange("p (c f) -> p c f", c=4)
    la = take(NT * P).rearrange("p (r f) -> p r f", r=NT)
    aT = [take(512).rearrange("p (r t) -> p r t", r=NT) for _ in range(2)]
    att_d = aT
    aTd = [kdt.rearrange("p c f -> p (c f)"), a_gla[:, 0:512]]
    aTd = [a.rearrange("p (r t) -> p r t", r=NT) for a in aTd]

    take = carve2()
    h2tok = take(NT * D).rearrange("p (r f) -> p r f", r=NT)
    sel = take(NT * 2 * SB).rearrange("p (r s) -> p r s", r=NT)
    selT = take(S)
    selT_b = take(S)
    xg = take(KD * 2 * SB)
    eb, ue = take(FE), take(FE)
    ueT = take(4 * 2 * SB)
    ysb = take(D)
    dbc = take(4 * S).rearrange("p (j t) -> p j t", j=4)
    route = take(1400)
    ends, passed = take(OVER * E), take(OVER + 1)
    diag = take(8 * P).rearrange("p (r j t) -> p r j t", r=NT, j=4)
    btab = enter(nc.sbuf_tensor("block_experts", [P, OVER + 1], I32))

    def con2(name):
        a, b = c2_c[name]
        return const_2[:, a:b]

    def par2(name):
        a, b = p2_c[name]
        return param_2[:, a:b]

    def parr(name):
        a, b = pr_c[name]
        return param_r[:, a:b]

    decay = con2("decay").rearrange("p (h r t) -> p h r t", h=4, r=NT)
    mask_d = con2("mask_d").rearrange("p (r t) -> p r t", r=NT)
    router = parr("router").rearrange("p (k e) -> p k e", k=KD)

    ps = enter(nc.psum_tensor("ps", [P, 8, 512], F32))

    def bank(b, n=1):
        return ps[:, b:b + n, :].rearrange("p b n -> p (b n)")

    def chunks(b, n):
        return bank(b, (n + 1) // 2)[:, 0:n * S].rearrange("p (k t) -> p k t", k=n)

    landed = [sem(f"slab_landed_{i}") for i in range(SLOTS)]
    slab_done = sem("slab_done")
    ring = Ring(ring_sb, landed, slab_done)
    consts_in, x_in, xp_in, const2_in, pos_in, param2_in, out_sent = [
        sem(n) for n in ("consts_in", "x_in", "xp_in", "const2_in", "pos_in", "param2_in", "out_sent")]
    vec_step, act_step = sem("vec_step"), sem("act_step")
    held = sem("held")
    x_squared, x_summed, x_root, h_ready, x_ready = [
        sem(n) for n in ("x_squared", "x_summed", "x_root", "h_ready", "x_ready")]
    q_squared, q_summed, q_normed, q_root, q_turned, q_ready, v_ready = [
        sem(n) for n in ("q_squared", "q_summed", "q_normed", "q_root", "q_turned", "q_ready", "v_ready")]
    heads_staged, scored, masked, max_ready, prob_ready, prob_turned, prob_copied, pv_done, o_scaled, \
        o_turned, o_copied = [sem("a_" + n) for n in (
            "heads_staged", "scored", "masked", "max_ready", "prob_ready", "prob_turned", "prob_copied",
            "pv_done", "o_scaled", "o_turned", "o_copied")]
    relu_ready, act_ready = sem("relu_ready"), sem("act_ready")
    c_copied, u_ready, y_ready = sem("c_copied"), sem("u_ready"), sem("y_ready")
    angle_ready, sin_ready, c_exp, cond_ready, mod_rows_copied, mod_done = [sem(n) for n in (
        "angle_ready", "sin_ready", "c_exp", "cond_ready", "mod_rows_copied", "mod_done")]
    win_copied, dq_squared, qk_product, qk_root, qk_ready = [
        sem(n) for n in ("win_copied", "dq_squared", "qk_product", "qk_root", "qk_ready")]
    gate_exp, gate_ready, lam_exp, lam_ready = [sem(n) for n in ("gate_exp", "gate_ready", "lam_exp", "lam_ready")]
    r_scored, r_decayed, r_used = [sem(n) for n in ("r_scored", "r_decayed", "r_used")]
    d_scored, d_max, d_exp, d_diff, d_turned, d_copied, d_out = [
        sem("d_" + n) for n in ("scored", "max", "exp", "diff", "turned", "copied", "out")]
    o_squared, o_summed, o_root, mix_ready = [
        sem(n) for n in ("o_squared", "o_summed", "o_root", "mix_ready")]
    g_logit, g_log, g_la, g_cum, g_exps, g_keys, g_keysT, g_keysC, g_diff, g_dexp, g_dk, g_pair, \
        g_acopy, g_kv, g_state, g_out = [sem("g_" + n) for n in (
            "logit", "log", "la", "cum", "exps", "keys", "keysT", "keysC", "diff", "dexp", "dk",
            "pair", "acopy", "kv", "state", "out")]
    t_logits, t_exp, t_rows, t_rows_copied, t_mask, t_ranks, t_table, t_diag, t_spread, t_spread_copied, \
        t_cleared = [sem("t_" + n) for n in (
            "logits", "exp", "rows", "rows_copied", "mask", "ranks", "table", "diag", "spread",
            "spread_copied", "cleared")]
    sel_ready, gathered, xg_copied_a, xg_copied_v, gate_e, ue_ready, ue_turned, ue_copied, y_copied_a, \
        y_copied_v, selT_ready, scattered = [sem("e_" + n) for n in (
            "sel_ready", "gathered", "xg_copied_a", "xg_copied_v", "gate_e", "ue_ready", "ue_turned",
            "ue_copied", "y_copied_a", "y_copied_v", "selT_ready", "scattered")]

    def cols_of(w, n0, cols=512):
        return w[:, n0:n0 + cols].rearrange("(k p) n -> p k n", p=P)

    def rows_of(w, r0):
        return w[r0:r0 + 512, :].rearrange("(k p) n -> p k n", p=P)

    def wcols(n, cols=512):
        return ring.tile(n)[:, 0:KD * cols].rearrange("p (k n) -> p k n", k=KD)

    def wrows(n):
        return ring.tile(n).rearrange("p (k n) -> p k n", k=4)

    def more_blocks(eng):
        return eng.value_load(btab[0:1, OVER:OVER + 1], min_val=0, max_val=OVER)

    block = enter(nc.Block())
    MIN_X = 4

    credited = (q_ready, q_root, q_summed, v_ready, scored, pv_done, o_turned, o_copied, mix_ready, g_state,
                ue_ready, ue_copied, y_copied_a, y_copied_v)

    @block.gpsimd
    def _(pool):
        for s in credited:
            pool.sem_inc(s, 1)

    @block.sync
    def _(sp):
        def load(n, dst, src, turns=0):
            if n >= SLOTS:
                sp.wait_ge(slab_done, turns * SLOTS + (n - SLOTS + 1))
            sp.dma_start(dst, src).then_inc(landed[n % SLOTS], 16)

        def load_cols(n, w, n0, cols=512, turns=0):
            load(n, wcols(n, cols), cols_of(w, n0, cols), turns)

        def load_rows(n, w, r0, turns=0):
            load(n, wrows(n), rows_of(w, r0), turns)

        sp.dma_start(common[:, :], common_d).then_inc(consts_in, 16)
        sp.dma_start(param_1[:, :], param_1_d).then_inc(consts_in, 16)
        sp.dma_start(xp.rearrange("p k t -> p (k t)"), xp_d).then_inc(xp_in, 16)

        def mlp(n, w1, w2, wm):
            load_cols(n, w1, 0)
            load_cols(n + 1, w1, 512)
            load_rows(n + 2, w2, 0)
            for j in range(6):
                load_cols(n + 3 + 4 * j, w1, 512 * (j + 2))
                load_cols(n + 4 + 4 * j, wm, 512 * (2 * j))
                load_rows(n + 5 + 4 * j, w2, 512 * (j + 1))
                load_cols(n + 6 + 4 * j, wm, 512 * (2 * j + 1))
            load_rows(n + MLP_SLABS - 1, w2, 512 * (NF - 1))

        for g in range(GROUPS_A):
            for s in range(6):
                load_cols(A_QKV + 6 * g + s, a_wqkv[0], (6 * g + s) * 512)
        for s in range(2):
            load_cols(A_WO + s, a_wo[0], 512 * s)
        mlp(MLP0, mlp_w1[0], mlp_w2[0], w_mod[0])
        for s in range(2):
            for j, part in enumerate((1, 2, 0)):
                load_cols(B_WIN + 3 * s + j, b_win[0], part * D + 512 * s)
        for s in range(2):
            load_cols(B_WOUT + s, b_wout[0], 512 * s)
        mlp(MLP1, mlp_w1[1], mlp_w2[1], w_mod[1])
        wi = w_in.rearrange("l (k p) n -> l p k n", p=P)
        wo = w_out.rearrange("l (k p) n -> l p k n", p=P)
        wg = w_gate.rearrange("l e (k p) f -> (l e) p k f", p=P)
        wu = w_up.rearrange("l e (k p) f -> (l e) p k f", p=P)
        wd = w_down.rearrange("l e (k p) n -> (l e) p k n", p=P)

        def pick(w, i):
            return w[bass.ds(i, 1)].rearrange("o p k n -> p (o k) n")

        with sp.Fori(0, DEPTH) as lay:
            for s in range(7):
                cols = min(512, IN_WIDTH - 512 * s)
                src = wi[bass.ds(lay, 1), :, :, 512 * s:512 * s + cols].rearrange("o p k n -> p (o k) n")
                load(WIN + s, wcols(WIN + s, cols), src, lay * TURNS)
            for s in range(2):
                src = wo[bass.ds(lay, 1), :, :, 512 * s:512 * s + 512].rearrange("o p k n -> p (o k) n")
                load(WOUT + s, wcols(WOUT + s), src, lay * TURNS)

            def pair(n, experts, turns):
                for part, w in enumerate((wg, wu, wd)):
                    for m, e in enumerate(experts):
                        slab = n + len(experts) * part + m
                        load(slab, (wrows if part == 2 else wcols)(slab), pick(w, e), turns)

            def expert_of(b):
                row = btab[0:1, b:b + 1] if isinstance(b, int) else btab[0:1, bass.ds(b, 1)]
                e = sp.value_load(row, min_val=0, max_val=E - 1)
                return sp.snap(e + lay * E, min_val=0, max_val=DEPTH * E - 1)
            with sp.Fori(0, HOME_PAIRS) as i:
                pair(MOE, [sp.snap(lay * E + i * 2 + m, min_val=0, max_val=DEPTH * E - 1) for m in range(2)],
                     lay * TURNS + i)
            sp.wait_ge(t_table, lay + 1)
            sp.sem_inc(held, 1)
            with sp.If(more_blocks(sp) > 0):
                with sp.Fori(0, OVER_PAIRS) as i:
                    pair(OVERS, [expert_of(sp.snap(i * 2)), expert_of(sp.snap(i * 2 + 1))],
                         lay * TURNS + i)
                pair(OVERS + 6 * OVER_PAIRS, [expert_of(OVER - 1)], lay * TURNS)
            with sp.Else():
                for n in range(OVERS - SLOTS, OVERS):
                    ring.wait_landed(sp, n, lay * TURNS)
                for slot in range(SLOTS):
                    missing = sum(n % SLOTS == slot for n in range(OVERS, OVERS + 3 * OVER))
                    sp.sem_inc(landed[slot], 16 * missing)
        sp.wait_ge(x_ready, MIN_X + 2 * DEPTH)
        sp.dma_start(out_d, xT).then_inc(out_sent, 16)
        sp.wait_ge(out_sent, 16)

    @block.scalar
    def _(act):
        sc = nc.scalar
        own = Steps(act, act_step)
        act.dma_start(xT, x_d).then_inc(x_in, 16)
        act.dma_start(const_a[:, :], const_a_d).then_inc(consts_in, 16)
        act.wait_ge(consts_in, 48)
        sc.activation(small[:, 16:24], cond, ACT.Exp, scale=-1.0).then_inc(c_exp, 1)

        def root(dst, src, scale, eps, ready):
            own.step(sc.activation(dst, src, ACT.Ln, bias=eps, scale=scale))
            sc.activation(dst, dst, ACT.Exp, scale=-0.5).then_inc(ready, 1)

        def square_x(n, src):
            if isinstance(n, int) and n == 0:
                act.wait_ge(xp_in, 16)
            else:
                act.wait_ge(x_ready, n)
            sc.activation(tmp, src, ACT.Square).then_inc(x_squared, 1)
            act.wait_ge(x_summed, n + 1)
            root(rstd, bank(7)[:, 0:S], 1.0 / D, EPS, x_root)

        def mlp(l, n):
            def relu(j, slab, turns=0, i=0):
                ring.wait_done(act, slab, turns)
                act.wait_ge(act_ready, i + 8 * l + j)
                sc.activation(tmp_a, bank(4, 2), ACT.Relu).then_inc(relu_ready, 1)
            def rows(slab, turns):
                ring.wait_done(act, slab, turns)
                sc.activation(mod_rows, bank(6), ACT.Copy).then_inc(mod_rows_copied, 1)
            relu(0, n)
            relu(1, n + 1)
            with act.Fori(0, 2) as i:
                for jj in range(3):
                    relu(2 + jj, n + 3 + 4 * jj, i * 2, i * 3)
                    rows(n + 4 + 4 * jj, i * 2)
                    rows(n + 6 + 4 * jj, i * 2)

        def load_second():
            act.dma_start(const_2[:, :], const_2_d).then_inc(const2_in, 16)
            act.dma_start(param_r[:, :], param_r_d).then_inc(const2_in, 16)
            act.dma_start(pos_i, pos_d).then_inc(pos_in, 16)
            act.dma_start(param_2[:, :], param_2_d[0]).then_inc(param2_in, 16)

        def sines():
            act.wait_ge(angle_ready, 4)
            sc.activation(tables, angles, ACT.Sin).then_inc(sin_ready, 1)

        square_x(0, xp.rearrange("p k t -> p (k t)"))
        with act.Fori(0, GROUPS_A) as g:
            close = own.loop(g, 4)
            for s in range(4):
                ring.wait_done(act, A_QKV + s, g)
                act.wait_ge(q_summed, g * 4 + (s + 1))
                sc.activation(tmp_a, bank(2 * (s % 2), 2), ACT.Square).then_inc(q_squared, 1)
                act.wait_ge(q_summed, g * 4 + (s + 2))
                act.wait_ge(q_ready, g * 4 + (max(s - 1, 0) + 1))
                root(tmp_b, bank(4, 2), 1.0, DH * EPS, q_root)
            close(GROUPS_A)
            for s in range(2):
                ring.wait_done(act, A_QKV + 4 + s, g)
                dst = vA[:, bass.ds(g, 1), :, 512 * s:512 * s + 512].rearrange("p g r f -> p (g r) f")
                sc.activation(dst, bank(2 * s, 2).rearrange("p (r f) -> p r f", r=NT),
                              ACT.Copy).then_inc(v_ready, 1)
        act.wait_ge(q_ready, 4 * GROUPS_A + 1)
        with act.Fori(0, KD) as c:
            act.wait_ge(scored, c * 4 + 1)
            src = qk[:, :, :, bass.ds(c, 1), :].rearrange("p g w c t -> p (g w c) t")
            sc.activation(heads_now.rearrange("p g w t -> p (g w) t"), src, ACT.Copy).then_inc(heads_staged, 1)

            def o_copy(r):
                act.wait_ge(o_turned, c * 2 + (r + 2))
                dst = h3[:, bass.ds(c, 1), r * P:(r + 1) * P].rearrange("p c t -> p (c t)")
                sc.activation(dst, bank(6)[:, 0:P], ACT.Copy).then_inc(o_copied, 1)
            for u in range(4):
                act.wait_ge(max_ready, c * 4 + (u + 1))
                sc.activation(att_s[u % 2], att_s[u % 2], ACT.Exp, bias=small[:, 2 + u % 2:3 + u % 2],
                              scale=QK_SCALE, accum_out=small[:, 4 + u % 2:5 + u % 2]).then_inc(prob_ready, 1)
                act.wait_ge(prob_turned, c * 4 + (u + 1))
                act.wait_ge(pv_done, c * 4 + (u + 1))
                sc.activation(att_t.rearrange("p j q -> p (j q)"), bank(2), ACT.Copy).then_inc(prob_copied, 1)
                if u == 2:
                    o_copy(0)
            o_copy(1)
        square_x(1, xT)
        load_second()
        mlp(0, MLP0)
        sines()
        square_x(2, xT)
        for s in range(2):
            ring.wait_done(act, B_WIN + 3 * s)
            if s:
                act.wait_ge(u_ready, s)
            sc.activation(tmp_a, bank(0, 2), ACT.Copy).then_inc(c_copied, 1)
        square_x(3, xT)
        mlp(1, MLP1)

        with act.Fori(0, DEPTH) as lay:
            close = own.loop(lay, ACT_STEPS)
            square_x(lay * 2 + MIN_X, xT)
            act.wait_ge(lam_ready, lay * 2 + 1)
            sc.activation(small[:, 26:28], small[:, 24:26], ACT.Exp).then_inc(lam_exp, 1)
            pair = (0, 3)

            def slab(s):
                ring.wait_done(act, WIN + s, lay * TURNS)
                return pair[s % 2]

            def qk_roots(w):
                act.wait_ge(qk_product, lay * 5 + (2 + 2 * w))
                act.wait_ge(qk_ready, lay * 5 + (1 + 2 * w))
                root(tmp_b, bank(6, 2), 1.0, DH * EPS, qk_root)
            b = slab(0)
            sc.activation(rqk, chunks(b, 4), ACT.Copy).then_inc(win_copied, 1)
            b = slab(1)
            sc.activation(rv, bank(b).rearrange("p (r f) -> p r f", r=NT), ACT.Copy)
            sc.activation(gates[:, 0:2, :], chunks(b + 1, 2), ACT.Copy).then_inc(win_copied, 1)
            b = slab(2)
            sc.activation(tmp_a, bank(b, 2), ACT.Square).then_inc(dq_squared, 1)
            sc.activation(dqk[:, 0:4, :], chunks(b, 4), ACT.Copy).then_inc(win_copied, 1)
            b = slab(3)
            sc.activation(scratch_b[:, 0:1024], bank(b, 2), ACT.Square).then_inc(dq_squared, 1)
            sc.activation(dqk[:, 4:8, :], chunks(b, 4), ACT.Copy).then_inc(win_copied, 1)
            qk_roots(0)
            b = slab(4)
            sc.activation(dv, bank(b, 2).rearrange("p (r f) -> p r f", r=NT), ACT.Copy).then_inc(win_copied, 1)
            b = slab(5)
            sc.activation(gqk[:, 0, :], chunks(b, 2)[:, 0, :], ACT.Copy, scale=GLA_DK ** -0.5)
            sc.activation(gqk[:, 1, :], chunks(b, 2)[:, 1, :], ACT.Copy)
            sc.activation(gv[0:64].rearrange("p c f -> p (c f)"), bank(b + 1, 2)[0:64], ACT.Copy).then_inc(win_copied, 1)
            qk_roots(1)
            b = slab(6)
            sc.activation(ga[0:16, :], bank(b)[0:16, 0:S], ACT.Copy)
            sc.activation(gates[:, 2:4, :], chunks(b + 1, 2), ACT.Copy).then_inc(win_copied, 1)
            act.wait_ge(win_copied, lay * 7 + 7)
            sc.activation(scratch[:, 0:1024], gates.rearrange("p k t -> p (k t)"), ACT.Exp, scale=-1.0
                          ).then_inc(gate_exp, 1)

            def square_o(n, width, b, sums, dim, ready):
                act.wait_ge(*ready)
                act.wait_ge(qk_ready, lay * 5 + 5)
                if n:
                    act.wait_ge(o_summed, lay * 3 + n)
                sc.activation(tmp_a[:, 0:width], bank(b, width // 512), ACT.Square).then_inc(o_squared, 1)
                act.wait_ge(o_summed, lay * 3 + (n + 1))
                act.wait_ge(mix_ready, lay * 3 + (n + 1))
                root(tmp_b[:, 0:width], bank(sums, width // 512), 1.0 / dim, EPS, o_root)
            square_o(0, 512, 2, 3, DH, (r_used, lay * 4 + 4))
            def d_copy(u):
                h, r = u // 2, u % 2
                act.wait_ge(d_turned, lay * 8 + (u + 1))
                if h >= 2:
                    act.wait_ge(d_out, lay * 4 + (h - 1))
                src = bank(6 + u % 2)[:, 0:S].rearrange("p (k q) -> p k q", k=NT)
                sc.activation(aTd[h % 2][:, :, r * P:(r + 1) * P], src, ACT.Copy).then_inc(d_copied, 1)
            for u in range(8):
                act.wait_ge(d_max, lay * 8 + (u + 1))
                for w in range(2):
                    e = sc.activation(att_d[u % 2][:, w, :], att_d[u % 2][:, w, :], ACT.Exp,
                                      bias=small[:, 32 + 2 * (u % 2) + w:33 + 2 * (u % 2) + w],
                                      scale=QK_SCALE,
                                      accum_out=small[:, 36 + 2 * (u % 2) + w:37 + 2 * (u % 2) + w])
                e.then_inc(d_exp, 1)
                if u:
                    d_copy(u - 1)
            d_copy(7)
            square_o(1, 1024, 4, 6, 2 * DH, (d_out, lay * 4 + 4))
            act.wait_ge(g_logit, lay + 1)
            lg = scratch_b[:, 256:512]
            own.step(sc.activation(lg, bank(0)[:, 0:S], ACT.Abs))
            own.step(sc.activation(lg, lg, ACT.Exp, scale=-1.0))
            sc.activation(lg, lg, ACT.Ln, bias=1.0).then_inc(g_log, 1)
            act.wait_ge(g_cum, lay + 1)
            own.step(sc.activation(gT, bank(1)[:, 0:S], ACT.Copy))
            sc.activation(eg, bank(1)[:, 0:S], ACT.Exp)
            for c in range(4):
                a, b = 64 * c, 64 * c + 64
                e = sc.activation(kd[:, a:b], gT[:, a:b], ACT.Exp, scale=-1.0, bias=gT[:, b - 1:b])
            e.then_inc(g_exps, 1)
            act.wait_ge(g_keysT, lay + 1)
            sc.activation(kdt[0:64].rearrange("p c f -> p (c f)"), bank(2)[0:64], ACT.Copy).then_inc(g_keysC, 1)

            def g_copy(c):
                act.wait_ge(g_pair, lay * 16 + (4 * c + 4))
                sc.activation(a_gla[0:64, 256 * c:256 * c + 256],
                              bank(4 + c % 2)[0:64, 0:256], ACT.Copy).then_inc(g_acopy, 1)
            for v in range(16):
                act.wait_ge(g_diff, lay * 16 + (v + 1))
                own.step(sc.activation(pair_d[v % 4], pair_d[v % 4], ACT.Abs))
                sc.activation(pair_d[v % 4], pair_d[v % 4], ACT.Exp, scale=-1.0).then_inc(g_dexp, 1)
                if v % 4 == 2 and v > 2:
                    g_copy(v // 4 - 1)
            g_copy(3)
            square_o(2, 512, 6, 3, DH, (g_out, lay + 1))
            act.wait_ge(mix_ready, lay * 3 + 4)
            act.dma_start(param_2[:, :], param_2_d[bass.ds(1 - lay, 1)].rearrange("o p n -> p (o n)")
                          ).then_inc(param2_in, 16)
            square_x(lay * 2 + (MIN_X + 1), xT)
            act.wait_ge(t_logits, lay + 1)
            sc.activation(route[:, 0:64], bank(6)[:, 0:64], ACT.Exp, scale=-1.0).then_inc(t_exp, 1)
            act.wait_ge(t_rows, lay + 1)
            sc.activation(h2tok[:, 0, :], bank(0, 2), ACT.Copy)
            sc.activation(h2tok[:, 1, :], bank(2, 2), ACT.Copy).then_inc(t_rows_copied, 1)
            act.wait_ge(t_spread, lay + 1)
            sc.activation(dbc.rearrange("p j t -> p (j t)"), bank(4, 2), ACT.Copy).then_inc(t_spread_copied, 1)

            def gathered_copy(pair):
                act.wait_ge(gathered, pair + 1)
                sc.activation(xg[:, 0:512], bank(6), ACT.Copy).then_inc(xg_copied_a, 1)

            def expert_pair(n, pair, turns, m=2):
                ring.wait_done(act, n + m - 1, turns)
                act.wait_ge(ue_ready, pair + 1)
                sc.activation(eb, bank(4), ACT.Exp, scale=-1.0).then_inc(gate_e, 1)
                if m == 2:
                    gathered_copy(pair + 1)
                act.wait_ge(ue_turned, pair + 1)
                sc.activation(ueT, bank(4), ACT.Copy).then_inc(ue_copied, 1)
                ring.wait_done(act, n + 3 * m - 1, turns)
                sc.activation(ysb[0:SB * m, 0:512], bank(6)[0:SB * m], ACT.Copy).then_inc(y_copied_a, 1)
            base = lay * (PAIRS + 1)
            gathered_copy(base)
            with act.Fori(0, HOME_PAIRS) as i:
                expert_pair(MOE, base + i, lay * TURNS + i)
            act.wait_ge(t_table, lay + 1)
            act.sem_inc(held, 1)
            with act.If(more_blocks(act) > 0):
                with act.Fori(0, OVER_PAIRS) as i:
                    expert_pair(OVERS, base + HOME_PAIRS + i, lay * TURNS + i)
                expert_pair(OVERS + 6 * OVER_PAIRS, base + PAIRS, lay * TURNS, 1)
            with act.Else():
                act.sem_inc(xg_copied_a, OVER_PAIRS)
                for s in (gate_e, ue_copied, y_copied_a):
                    act.sem_inc(s, OVER_PAIRS + 1)
            close(DEPTH)
        act.wait_ge(param2_in, (DEPTH + 1) * 16)

    @block.vector
    def _(dve):
        ve = nc.vector
        own = Steps(dve, vec_step)
        dve.wait_ge(consts_in, 48)
        dve.wait_ge(c_exp, 1)
        own.step(ve.tensor_scalar(small[:, 16:24], small[:, 16:24], 1.0, None, ALU.add))
        own.step(ve.reciprocal(small[:, 16:24], small[:, 16:24]))
        own.step(ve.tensor_tensor(small[:, 16:24], small[:, 16:24], cond, ALU.mult))
        dve.wait_ge(x_in, 16)

        def rotary_angles():
            own.step(ve.memset(cond32, 0.0))
            own.inc(ve.tensor_copy(cond32[:, :, 0], small[:, 16:24]))
            ve.memset(zeros, 0.0).then_inc(cond_ready, 1)
            dve.wait_ge(const2_in, 32)
            dve.wait_ge(pos_in, 16)
            own.step(ve.tensor_copy(pos_f, pos_i))
            for n, inv in enumerate(("inv_r", "inv_d")):
                own.step(ve.tensor_scalar(ang, pos_f, con2(inv), None, ALU.mult))
                own.step(ve.tensor_scalar(turns_, ang, 1.0 / TWO_PI, None, ALU.mult))
                own.step(ve.tensor_scalar(turns_, turns_, MAGIC, None, ALU.add))
                own.step(ve.tensor_scalar(turns_, turns_, MAGIC, None, ALU.subtract))
                for part in (PI_1, PI_2, PI_3):
                    own.step(ve.scalar_tensor_tensor(out=ang, in0=turns_, scalar=-part, in1=ang, op0=ALU.mult,
                                                     op1=ALU.add))
                quarter, plain = angles[:, 2 * n, :], angles[:, 2 * n + 1, :]
                own.step(ve.tensor_scalar(quarter, ang, np.pi / 2, None, ALU.add))
                own.step(ve.tensor_scalar(wrap, quarter, np.pi, None, ALU.is_gt))
                own.step(ve.scalar_tensor_tensor(out=quarter, in0=wrap, scalar=-TWO_PI, in1=quarter, op0=ALU.mult,
                                                 op1=ALU.add))
                ve.tensor_scalar(quarter, quarter, 3.1415925, -3.1415925, ALU.min, ALU.max).then_inc(angle_ready, 1)
                ve.tensor_scalar(plain, ang, 3.1415925, -3.1415925, ALU.min, ALU.max).then_inc(angle_ready, 1)
                dve.wait_ge(angle_ready, 2 * n + 2)

        def norm(n, src, gain, shift=None):
            dve.wait_ge(x_root, n + 1)
            for k in range(KD):
                e = ve.scalar_tensor_tensor(out=h3[:, k, :], in0=src[:, k, :], scalar=gain[:, k:k + 1],
                                            in1=rstd, op0=ALU.mult, op1=ALU.mult)
            if shift is not None:
                own.step(e)
                for k in range(KD):
                    e = ve.tensor_scalar(h3[:, k, :], h3[:, k, :], shift[:, k:k + 1], None, ALU.add)
            e.then_inc(h_ready, 1)

        def rope(q, cos, sin, turned, ready):
            t = tmp_b.rearrange("p (k t) -> p k t", k=4)
            own.inc(ve.tensor_tensor(t, turned, sin.unsqueeze(1).broadcast_to([P, 4, S]), ALU.mult))
            own.step(ve.tensor_tensor(q, q, cos.unsqueeze(1).broadcast_to([P, 4, S]), ALU.mult))
            ve.tensor_tensor(q, q, t, ALU.add).then_inc(ready, 1)

        def mlp(l, n):
            def squared(j, i=0, more=0):
                dve.wait_ge(relu_ready, more + 8 * l + j + 1)
                if j >= 2:
                    ring.wait_done(dve, n + 4 * (j - 2) - (2 if j > 2 else 0), i)
                ve.tensor_tensor(act3[j % 3], tmp_a, tmp_a, ALU.mult).then_inc(act_ready, 1)
            squared(0)
            squared(1)
            with dve.Fori(0, 2) as i:
                for jj in range(3):
                    squared(2 + jj, i * 2, i * 3)
            dve.wait_ge(mod_done, l + 1)
            ve.tensor_copy(modcols[:, l, :], bank(7)[:, 0:48])
            ring.wait_done(dve, n + MLP_SLABS - 1)
            ve.tensor_tensor(xT, xT, bank(0, 4), ALU.add).then_inc(x_ready, 1)

        dve.wait_ge(xp_in, 16)
        norm(0, xp, par1("norm1")[:, 0:KD])
        with dve.Fori(0, GROUPS_A) as g:
            close = own.loop(g, 8)

            def part(s):
                return qk[:, bass.ds(g, 1), s // 2, 4 * (s % 2):4 * (s % 2) + 4, :].rearrange(
                    "p g k t -> p (g k) t")

            def turn(s):
                dve.wait_ge(q_turned, g * 4 + (s + 1))
                rope(part(s), cos_a, sin_a, chunks(6, 4), q_ready)
            for s in range(4):
                root_s = tmp_b
                dve.wait_ge(q_root, g * 4 + (s + 2))
                gcol = par1("gain_a").rearrange("p (g w) -> p g w", g=GROUPS_A)[:, bass.ds(g, 1), s // 2]
                ve.scalar_tensor_tensor(
                    out=part(s), in0=chunks(2 * (s % 2), 4), scalar=gcol,
                    in1=root_s.rearrange("p (k t) -> p k t", k=4), op0=ALU.mult, op1=ALU.mult
                ).then_inc(q_normed, 1)
                dve.wait_ge(q_normed, g * 4 + (s + 1))
                if s:
                    turn(s - 1)
            turn(3)
            close(GROUPS_A)

        with dve.Fori(0, KD) as c:
            close = own.loop(c, 4)

            def mask(u):
                r, p = u // 2, u % 2
                dve.wait_ge(scored, c * 4 + (u + 2))
                if u >= 2:
                    dve.wait_ge(prob_turned, c * 4 + (u - 1))
                dve.sem_inc(held, 1)
                ve.tensor_tensor_reduce(att_s[p], bank(p), mask_a[:, r, :], 1.0, -3e38, ALU.add, ALU.max,
                                        small[:, p:p + 1]).then_inc(masked, 1)
                dve.wait_ge(masked, c * 4 + (u + 1))
                ve.tensor_scalar(small[:, 2 + p:3 + p], small[:, p:p + 1], -QK_SCALE, None, ALU.mult
                                 ).then_inc(max_ready, 1)

            def scale_o(u):
                r, p = u // 2, u % 2
                dve.wait_ge(pv_done, c * 4 + (u + 2))
                own.step(ve.reciprocal(small[:, 6 + p:7 + p], small[:, 4 + p:5 + p]))
                if p == 0:
                    dve.wait_ge(o_turned, c * 2 + (r + 1))
                ve.tensor_scalar(o_rows[:, 64 * p:64 * p + 64], bank(o_bank[u])[:, 0:64],
                                 small[:, 6 + p:7 + p], None, ALU.mult).then_inc(o_scaled, 1)
            mask(0)
            mask(1)
            scale_o(0)
            mask(2)
            scale_o(1)
            mask(3)
            scale_o(2)
            scale_o(3)
            close(KD)

        for k in range(KD):
            if k % 4 == 0:
                ring.wait_done(dve, A_WO + k // 4)
            nat = x3[:, k, :].rearrange("p (m b a) -> p a b m", b=4, a=4)
            e = ve.tensor_tensor(nat, nat, chunks(0, 8)[:, k, :].rearrange("p (a b m) -> p a b m", a=4, b=4),
                                 ALU.add)
        e.then_inc(x_ready, 1)
        dve.wait_ge(x_ready, 1)
        norm(1, x3, par1("norm2")[:, 0:KD])
        rotary_angles()
        mlp(0, MLP0)
        dve.wait_ge(x_ready, 2)
        norm(2, x3, par1("norm1")[:, KD:2 * KD])
        conv = par1("conv")
        for s in range(2):
            ring.wait_done(dve, B_WIN + 3 * s + 1)
            dve.wait_ge(c_copied, s + 1)
            ve.tensor_tensor(conv_u.rearrange("p k t -> p (k t)"), tmp_a, bank(2, 2), ALU.mult).then_inc(u_ready, 1)
            dve.wait_ge(u_ready, s + 1)

            def tap(w, k):
                return conv[:, w * KD + 4 * s + k:w * KD + 4 * s + k + 1]
            for k in range(4):
                e = ve.tensor_scalar(conv_y[:, k, :], conv_u[:, k, :], tap(1, k), None, ALU.mult)
            own.step(e)
            for k in range(4):
                e = ve.scalar_tensor_tensor(out=conv_y[:, k, 1:S], in0=conv_u[:, k, 0:S - 1], scalar=tap(0, k),
                                            in1=conv_y[:, k, 1:S], op0=ALU.mult, op1=ALU.add)
            own.step(e)
            for k in range(4):
                e = ve.scalar_tensor_tensor(out=conv_y[:, k, 0:S - 1], in0=conv_u[:, k, 1:S], scalar=tap(2, k),
                                            in1=conv_y[:, k, 0:S - 1], op0=ALU.mult, op1=ALU.add)
            own.step(e)
            ring.wait_done(dve, B_WIN + 3 * s + 2)
            ve.tensor_tensor(mixB[:, 4 * s:4 * s + 4, :], conv_y, chunks(4, 4), ALU.mult).then_inc(y_ready, 1)
        ring.wait_done(dve, B_WOUT + 1)
        ve.tensor_tensor(xT, xT, bank(0, 4), ALU.add).then_inc(x_ready, 1)
        dve.wait_ge(x_ready, 3)
        norm(3, x3, par1("norm2")[:, KD:2 * KD])
        mlp(1, MLP1)
        dve.wait_ge(x_ready, 4)

        dve.wait_ge(sin_ready, 1)
        cos_r, sin_r, cos_d, sin_d = [tables[:, n, :] for n in range(4)]
        with dve.Fori(0, DEPTH) as lay:
            close = own.loop(lay, VEC_STEPS)
            dve.wait_ge(param2_in, lay * 16 + 16)
            lam = par2("lam").rearrange("p (n d) -> p n d", n=4)
            own.inc(ve.tensor_tensor_reduce(kvm[:, 0:64], lam[:, 0, :], lam[:, 1, :], 1.0, 0.0, ALU.mult, ALU.add,
                                            small[:, 24:25]))
            own.settle()
            ve.tensor_tensor_reduce(kvm[:, 0:64], lam[:, 2, :], lam[:, 3, :], 1.0, 0.0, ALU.mult, ALU.add,
                                    small[:, 25:26]).then_inc(lam_ready, 1)
            dve.wait_ge(lam_exp, lay + 1)
            own.step(ve.tensor_tensor(small[:, 28:29], small[:, 27:28], small[:, 26:27], ALU.subtract))
            own.step(ve.tensor_tensor(small[:, 28:29], small[:, 28:29], par2("neg_lam"), ALU.add))
            ve.tensor_tensor(small[:, 29:30], par2("gain_d"), par2("one_minus_lam"), ALU.mult).then_inc(lam_ready, 1)
            dve.wait_ge(lam_ready, lay * 2 + 2)
            own.step(ve.tensor_tensor(md, modcols[:, bass.ds(lay, 1), :].rearrange("p l n -> p (l n)"),
                                      par2("bmod"), ALU.add))
            for n in range(2):
                e = ve.scalar_tensor_tensor(out=gains[:, n * KD:(n + 1) * KD], in0=md[:, 24 * n + 8:24 * n + 16],
                                            scalar=1.0, in1=par2(f"norm{n + 1}"), op0=ALU.add, op1=ALU.mult)
            own.step(e)
            dve.wait_ge(x_ready, lay * 2 + MIN_X)
            norm(lay * 2 + MIN_X, x3, gains[:, 0:KD], md[:, 0:8])
            dve.wait_ge(qk_product, lay * 5 + 1)
            dve.wait_ge(win_copied, lay * 7 + 1)
            rope(rqk, cos_r, sin_r, chunks(6, 4), qk_ready)
            for w in range(2):
                part = dqk[:, 4 * w:4 * w + 4, :]
                dve.wait_ge(qk_root, lay * 2 + (w + 1))
                dve.wait_ge(win_copied, lay * 7 + (3 + w))
                ve.scalar_tensor_tensor(out=part, in0=part, scalar=par2(("gain_q", "gain_k")[w]),
                                        in1=tmp_b.rearrange("p (k t) -> p k t", k=4), op0=ALU.mult,
                                        op1=ALU.mult).then_inc(qk_ready, 1)
                dve.wait_ge(qk_ready, lay * 5 + (2 + 2 * w))
                dve.wait_ge(qk_product, lay * 5 + (3 + 2 * w))
                rope(part, cos_d, sin_d, chunks(6, 4), qk_ready)
            dve.wait_ge(gate_exp, lay + 1)
            gt = scratch[:, 0:1024]
            own.step(ve.tensor_scalar(gt, gt, 1.0, None, ALU.add))
            own.step(ve.reciprocal(gt, gt))
            flat = gates.rearrange("p k t -> p (k t)")
            ve.tensor_tensor(flat, flat, gt, ALU.mult).then_inc(gate_ready, 1)
            dve.wait_ge(gate_ready, lay + 1)
            mix = h3

            def norm_o(n, b, gain, k0, k1, gate):
                width = (k1 - k0) * S
                dve.wait_ge(o_root, lay * 3 + (n + 1))
                o = ve.scalar_tensor_tensor(out=mix[:, k0:k1, :], in0=chunks(b, k1 - k0), scalar=gain,
                                            in1=tmp_b[:, 0:width].rearrange("p (k t) -> p k t", t=S),
                                            op0=ALU.mult, op1=ALU.mult)
                if gate is None:
                    o.then_inc(mix_ready, 1)
                else:
                    own.step(o)
                    ve.tensor_tensor(mix[:, k0:k1, :], mix[:, k0:k1, :], gate, ALU.mult).then_inc(mix_ready, 1)
            for h in range(4):
                dve.wait_ge(r_scored, lay * 4 + (h + 1))
                if h >= 2:
                    dve.wait_ge(r_used, lay * 4 + (h - 1))
                ve.tensor_tensor(aT[h % 2], bank(h % 2).rearrange("p (r t) -> p r t", r=NT), decay[:, h],
                                 ALU.mult).then_inc(r_decayed, 1)
            norm_o(0, 2, par2("gain_r"), 0, 2, gates[:, 0:2, :])
            def d_mask(u):
                r, p = u % 2, u % 2
                dve.wait_ge(d_scored, lay * 8 + (u + 1))
                if u >= 2:
                    dve.wait_ge(d_turned, lay * 8 + (u - 1))
                dve.sem_inc(held, 1)
                for w in range(2):
                    e = ve.tensor_tensor_reduce(att_d[p][:, w, :], bank(2 * p + w)[:, 0:S], mask_d[:, r, :],
                                                1.0, -3e38, ALU.add, ALU.max, small[:, 30 + w:31 + w])
                own.step(e)
                ve.tensor_scalar(small[:, 32 + 2 * p:34 + 2 * p], small[:, 30:32], -QK_SCALE, None, ALU.mult
                                 ).then_inc(d_max, 1)
                dve.wait_ge(d_max, lay * 8 + (u + 1))

            def d_sub(u):
                p = u % 2
                dve.wait_ge(d_exp, lay * 8 + (u + 1))
                own.step(ve.reciprocal(small[:, 40:42], small[:, 36 + 2 * p:38 + 2 * p]))
                own.inc(ve.tensor_scalar(small[:, 41:42], small[:, 41:42], small[:, 28:29], None, ALU.mult))
                own.step(ve.tensor_scalar(att_d[p][:, 0, :], att_d[p][:, 0, :], small[:, 40:41], None, ALU.mult))
                ve.scalar_tensor_tensor(out=att_d[p][:, 0, :], in0=att_d[p][:, 1, :], scalar=small[:, 41:42],
                                        in1=att_d[p][:, 0, :], op0=ALU.mult, op1=ALU.add).then_inc(d_diff, 1)
                dve.wait_ge(d_diff, lay * 8 + (u + 1))
            dve.wait_ge(r_used, lay * 4 + 4)
            for u in range(8):
                d_mask(u)
                if u:
                    d_sub(u - 1)
            d_sub(7)
            dve.wait_ge(mix_ready, lay * 3 + 2)
            norm_o(1, 4, small[:, 29:30], 2, 6, None)
            logit = bank(0)[:, 0:S]
            dve.wait_ge(g_log, lay + 1)
            ve.scalar_tensor_tensor(out=la.rearrange("p r f -> p (r f)"), in0=logit, scalar=0.0,
                                    in1=scratch_b[:, 256:512], op0=ALU.min, op1=ALU.subtract).then_inc(g_la, 1)
            dve.wait_ge(g_exps, lay + 1)
            own.inc(ve.tensor_tensor(qe, gqk[:, 0, :], eg, ALU.mult))
            own.inc(ve.tensor_tensor(qsel, gqk[:, 0, :].unsqueeze(2).broadcast_to([P, S, 4]),
                                     con2("hsel").unsqueeze(1).broadcast_to([P, S, 4]), ALU.mult))
            own.inc(ve.memset(state, 0.0))
            ve.tensor_tensor(kd, kd, gqk[:, 1, :], ALU.mult).then_inc(g_keys, 1)

            def g_sub(v):
                c, a = v // 4, 16 * v
                if v >= 4:
                    dve.wait_ge(g_pair, lay * 16 + (v - 3))
                ve.tensor_tensor(pair_d[v % 4], gT[:, a:a + 16].unsqueeze(2).broadcast_to([P, 16, CHUNK]),
                                 gT[:, 64 * c:64 * c + 64].unsqueeze(1).broadcast_to([P, 16, CHUNK]),
                                 ALU.subtract).then_inc(g_diff, 1)

            def g_mul(v):
                c = v // 4
                dve.wait_ge(g_dexp, lay * 16 + (v + 1))
                ve.tensor_tensor(pair_d[v % 4], pair_d[v % 4],
                                 gqk[:, 1, 64 * c:64 * c + 64].unsqueeze(1).broadcast_to([P, 16, CHUNK]),
                                 ALU.mult).then_inc(g_dk, 1)

            for v in range(18):
                if v >= 2:
                    g_mul(v - 2)
                if v < 16:
                    g_sub(v)
            for c in range(3):
                dve.wait_ge(g_kv, lay * 3 + (c + 1))
                own.step(ve.tensor_tensor(kvm, bank(7)[:, 0:256], con2("bdmask"), ALU.mult))
                ve.scalar_tensor_tensor(out=state, in0=state, scalar=eg[:, 64 * c + 63:64 * c + 64], in1=kvm,
                                        op0=ALU.mult, op1=ALU.add).then_inc(g_state, 1)
                dve.wait_ge(g_state, lay * 3 + (c + 2))
            dve.wait_ge(mix_ready, lay * 3 + 3)
            norm_o(2, 6, par2("gain_g"), 6, 8, gates[:, 2:4, :])
            for k in range(KD):
                if k % 4 == 0:
                    ring.wait_done(dve, WOUT + k // 4, lay * TURNS)
                e = ve.scalar_tensor_tensor(out=x3[:, k, :], in0=chunks(0, 8)[:, k, :], scalar=md[:, 16 + k:17 + k],
                                            in1=x3[:, k, :], op0=ALU.mult, op1=ALU.add)
            e.then_inc(x_ready, 1)
            dve.wait_ge(x_ready, lay * 2 + (MIN_X + 1))
            norm(lay * 2 + (MIN_X + 1), x3, gains[:, KD:2 * KD], md[:, 24:32])
            at = [64]

            def t(n):
                at[0] += n
                return route[:, at[0] - n:at[0]]
            score = route[:, 0:64].rearrange("p (r e) -> p r e", r=NT)
            biased, work = [t(64).rearrange("p (r e) -> p r e", r=NT) for _ in range(2)]
            oh = [t(64).rearrange("p (r e) -> p r e", r=NT) for _ in range(2)]
            both = t(64).rearrange("p (r e) -> p r e", r=NT)
            hi, lo = t(32).rearrange("p (g e) -> p g e", e=2), t(32).rearrange("p (g e) -> p g e", e=2)
            top, second_, gsum = [t(16) for _ in range(3)]
            best = t(2)
            wts = t(4).rearrange("p (r j) -> p r j", r=NT)
            wsum = t(2)
            dest = t(8).rearrange("p (r j) -> p r j", r=NT)
            cnt, nblk, incl, one32, startb, home = [t(32) for _ in range(6)]
            dcur = t(4).rearrange("p (r j) -> p r j", r=NT)
            slotcol = t(1)
            iota32 = con2("iota32").unsqueeze(1).broadcast_to([P, NT, E])

            dve.wait_ge(t_exp, lay + 1)
            own.step(ve.tensor_scalar(score, score, 1.0, None, ALU.add))
            own.step(ve.reciprocal(score, score))
            own.step(ve.tensor_tensor(biased, score, parr("router_b").unsqueeze(1).broadcast_to([P, NT, E]), ALU.add))
            quads = biased.rearrange("p r (g e) -> p (r g) e", e=EG)
            own.inc(ve.tensor_tensor(hi, quads[:, :, 0:2], quads[:, :, 2:4], ALU.max))
            own.step(ve.tensor_tensor(lo, quads[:, :, 0:2], quads[:, :, 2:4], ALU.min))
            own.inc(ve.tensor_tensor(top, hi[:, :, 0], hi[:, :, 1], ALU.max))
            own.inc(ve.tensor_tensor(second_, hi[:, :, 0], hi[:, :, 1], ALU.min))
            own.step(ve.tensor_tensor(gsum, lo[:, :, 0], lo[:, :, 1], ALU.max))
            own.step(ve.tensor_tensor(second_, second_, gsum, ALU.max))
            own.step(ve.tensor_tensor(gsum, top, second_, ALU.add))

            def first_best(values, out, iota, n):
                own.step(ve.tensor_reduce(best, values, AX, ALU.max))
                own.step(ve.tensor_tensor(out, values, best.unsqueeze(2).broadcast_to([P, NT, n]), ALU.is_equal))
                own.step(ve.scalar_tensor_tensor(out=out, in0=out, scalar=-100.0, in1=iota, op0=ALU.mult, op1=ALU.add))
                own.step(ve.tensor_reduce(best, out, AX, ALU.min))
                own.step(ve.tensor_tensor(out, out, best.unsqueeze(2).broadcast_to([P, NT, n]), ALU.is_equal))
            g2 = gsum.rearrange("p (r g) -> p r g", r=NT)
            s2 = second_.rearrange("p (r g) -> p r g", r=NT)
            first_best(g2, s2, con2("iota8").unsqueeze(1).broadcast_to([P, NT, NG]), NG)
            own.step(ve.tensor_scalar(second_, second_, -NEG, NEG, ALU.mult, ALU.add))
            own.step(ve.tensor_tensor(quads, quads, second_.unsqueeze(2).broadcast_to([P, NT * NG, EG]), ALU.add))
            first_best(biased, oh[0], iota32, E)
            own.step(ve.scalar_tensor_tensor(out=biased, in0=oh[0], scalar=3 * NEG, in1=biased, op0=ALU.mult, op1=ALU.add))
            first_best(biased, oh[1], iota32, E)
            ve.tensor_tensor(both, oh[0], oh[1], ALU.add).then_inc(t_mask, 1)
            for j in range(2):
                own.step(ve.tensor_tensor(work, score, oh[j], ALU.mult))
                own.step(ve.tensor_reduce(wts[:, :, j], work, AX, ALU.add))
            own.step(ve.tensor_tensor(wsum, wts[:, :, 0], wts[:, :, 1], ALU.add))
            own.step(ve.reciprocal(wsum, wsum))
            own.step(ve.tensor_tensor(dest[:, :, 2:4], wts, wsum.unsqueeze(2).broadcast_to([P, NT, 2]), ALU.mult))
            dve.wait_ge(t_ranks, lay + 1)
            own.inc(ve.memset(one32, 1.0))
            own.step(ve.tensor_copy(cnt, bank(7)[:, 64:96]))
            own.step(ve.tensor_scalar(home, con2("iota32"), float(SB), None, ALU.mult))
            own.step(ve.tensor_scalar(nblk, cnt, float(SB), None, ALU.is_gt))
            for j in range(2, S // SB):
                own.step(ve.scalar_tensor_tensor(out=nblk, in0=cnt, scalar=float(SB * j), in1=nblk,
                                                 op0=ALU.is_gt, op1=ALU.add))
            own.step(ve.tensor_tensor_scan(incl, one32, nblk, 0.0, ALU.mult, ALU.add))
            own.step(ve.tensor_tensor(startb, incl, nblk, ALU.subtract))
            own.step(ve.tensor_scalar(startb, startb, float(SB), float(SB * (E - 1)), ALU.mult, ALU.add))
            own.step(ve.tensor_tensor(startb, startb, home, ALU.subtract))
            rank = bank(7)[:, 0:64].rearrange("p (r e) -> p r e", r=NT)
            own.inc(ve.tensor_tensor(biased, rank, home.unsqueeze(1).broadcast_to([P, NT, E]), ALU.add))
            own.step(ve.scalar_tensor_tensor(out=work, in0=rank, scalar=float(SB),
                                             in1=startb.unsqueeze(1).broadcast_to([P, NT, E]), op0=ALU.is_ge,
                                             op1=ALU.mult))
            own.step(ve.tensor_tensor(biased, biased, work, ALU.add))
            big = ends[0:1].rearrange("p (b e) -> p b e", b=OVER)
            own.inc(ve.tensor_copy(passed[0:1, OVER:OVER + 1], incl[0:1, E - 1:E]))
            own.step(ve.tensor_tensor(big, incl[0:1].unsqueeze(1).broadcast_to([1, OVER, E]),
                                      con2("iotab")[0:1].unsqueeze(2).broadcast_to([1, OVER, E]), ALU.is_le))
            own.step(ve.tensor_reduce(passed[0:1, 0:OVER], big, AX, ALU.add))
            ve.tensor_scalar(btab[0:1, :], passed[0:1], float(E - 1), None, ALU.min).then_inc(t_table, 1)
            for j in range(2):
                own.step(ve.tensor_tensor(work, biased, oh[j], ALU.mult))
                own.step(ve.tensor_reduce(dest[:, :, j], work, AX, ALU.add))
            for r in range(NT):
                for j in range(4):
                    e = ve.tensor_scalar(diag[:, r, j, :], com("ident"), dest[:, r, j:j + 1], None, ALU.mult)
            e.then_inc(t_diag, 1)
            own.inc(ve.tensor_copy(dcur, dest[:, :, 0:2]))
            own.inc(ve.tensor_copy(slotcol, con2("slot0")))
            own.inc(ve.memset(ysb, 0.0))
            ve.memset(selT, 0.0).then_inc(selT_ready, 1)
            own.settle()

            def select(pair, move=True):
                if move:
                    dve.wait_ge(gathered, pair)
                    dve.wait_ge(sel_ready, pair)
                    own.step(ve.tensor_scalar(dcur, dcur, -2.0 * SB, None, ALU.add))
                for r in range(NT):
                    e = ve.tensor_scalar(sel[:, r, :], con2("iota128"), dcur[:, r, 0:1], None, ALU.is_equal)
                own.step(e)
                for r in range(NT):
                    e = ve.scalar_tensor_tensor(out=sel[:, r, :], in0=con2("iota128"), scalar=dcur[:, r, 1:2],
                                                in1=sel[:, r, :], op0=ALU.is_equal, op1=ALU.add)
                e.then_inc(sel_ready, 1)

            def gathered_copy(pair):
                dve.wait_ge(gathered, pair + 1)
                ve.tensor_copy(xg[:, 512:1024], bank(7)).then_inc(xg_copied_v, 1)

            def expert_pair(n, pair, turns, m=2):
                if m == 2:
                    select(pair + 1)
                dve.wait_ge(gate_e, pair + 1)
                own.step(ve.tensor_scalar(eb, eb, 1.0, None, ALU.add))
                own.step(ve.reciprocal(eb, eb))
                own.step(ve.tensor_tensor(eb, bank(4), eb, ALU.mult))
                ring.wait_done(dve, n + 2 * m - 1, turns)
                ve.tensor_tensor(ue, eb, bank(5), ALU.mult).then_inc(ue_ready, 1)
                if m == 2:
                    gathered_copy(pair + 1)
                dve.wait_ge(scattered, pair + (lay + 1))
                own.inc(ve.scalar_tensor_tensor(out=selT_b, in0=dbc[:, 0, :], scalar=slotcol, in1=dbc[:, 2, :],
                                                op0=ALU.is_equal, op1=ALU.mult))
                own.step(ve.scalar_tensor_tensor(out=selT, in0=dbc[:, 1, :], scalar=slotcol, in1=dbc[:, 3, :],
                                                 op0=ALU.is_equal, op1=ALU.mult))
                ve.tensor_tensor(selT, selT, selT_b, ALU.add).then_inc(selT_ready, 1)
                own.step(ve.tensor_scalar(slotcol, slotcol, 2.0 * SB, None, ALU.add))
                ring.wait_done(dve, n + 3 * m - 1, turns)
                ve.tensor_copy(ysb[0:SB * m, 512:1024], bank(7)[0:SB * m]).then_inc(y_copied_v, 1)
            base = lay * (PAIRS + 1)
            dve.wait_ge(t_spread_copied, lay + 1)
            select(base, move=False)
            gathered_copy(base)
            with dve.Fori(0, HOME_PAIRS) as i:
                close_i = own.loop(i, 8)
                expert_pair(MOE, base + i, lay * TURNS + i)
                close_i(HOME_PAIRS)
            before = own.n
            dve.wait_ge(t_table, lay + 1)
            dve.sem_inc(held, 1)
            with dve.If(more_blocks(dve) > 0):
                with dve.Fori(0, OVER_PAIRS) as i:
                    close_i = own.loop(i, 8)
                    expert_pair(OVERS, base + HOME_PAIRS + i, lay * TURNS + i)
                    close_i(OVER_PAIRS)
                expert_pair(OVERS + 6 * OVER_PAIRS, base + PAIRS, lay * TURNS, 1)
            with dve.Else():
                for s in (sel_ready, xg_copied_v):
                    dve.sem_inc(s, OVER_PAIRS)
                for s in (ue_ready, selT_ready, y_copied_v):
                    dve.sem_inc(s, OVER_PAIRS + 1)
                dve.sem_inc(vec_step, own.n - before)
            dve.wait_ge(scattered, lay * (PAIRS + 2) + (PAIRS + 2))
            for k in range(KD):
                e = ve.scalar_tensor_tensor(out=x3[:, k, :], in0=chunks(0, 8)[:, k, :], scalar=md[:, 40 + k:41 + k],
                                            in1=x3[:, k, :], op0=ALU.mult, op1=ALU.add)
            e.then_inc(x_ready, 1)
            close(DEPTH)

    @block.tensor
    def _(pe):
        te = nc.tensor
        pe.wait_ge(consts_in, 48)

        def sum_x(n):
            pe.wait_ge(x_squared, n + 1)
            t3 = tmp.rearrange("p (k t) -> p k t", k=KD)
            for k in range(KD):
                e = te.matmul(bank(7)[:, 0:S], com("ones"), t3[:, k, :], start=(k == 0), stop=(k == KD - 1))
            e.then_inc(x_summed, 1)

        def feature_major(n, out, width, src, cols=512, c0=0, signal=True, turns=0):
            w = wcols(n, cols)
            for j in range(width):
                for k in range(KD):
                    e = te.matmul(out[:, j, :], w[:, k, c0 + 128 * j:c0 + 128 * j + 128], src[:, k, :],
                                  start=(k == 0), stop=(k == KD - 1))
            if signal:
                e.then_inc(slab_done, 1)

        def token_major(n, b, width, cols=512, c0=0, rows=P):
            w = wcols(n, cols)
            for r in range(S // rows):
                out = bank(b, 2)[0:rows, r * width:(r + 1) * width]
                for k in range(KD):
                    e = te.matmul(out, h3[:, k, r * rows:(r + 1) * rows], w[:, k, c0:c0 + width],
                                  start=(k == 0), stop=(k == KD - 1))
            return e

        def project_out(n, src, turns=0):
            for s in range(2):
                ring.wait_landed(pe, n + s, turns)
                feature_major(n + s, chunks(2 * s, 4), 4, src)

        def mlp(l, n):
            u3 = [a.rearrange("p (k t) -> p k t", k=4) for a in act3]

            def hidden(j, slab, turns=0, more=0):
                ring.wait_landed(pe, slab, turns)
                pe.wait_ge(relu_ready, more + 8 * l + j)
                feature_major(slab, chunks(4, 4), 4, h3)

            def down(j, slab, turns=0, more=0, start=False):
                ring.wait_landed(pe, slab, turns)
                pe.wait_ge(act_ready, more + 8 * l + j + 1)
                w = wrows(slab)
                for o in range(KD):
                    for k in range(4):
                        e = te.matmul(chunks(0, 8)[:, o, :], w[:, k, 128 * o:128 * o + 128], u3[j % 3][:, k, :],
                                      start=(start and k == 0 and o % 2 == 0), stop=False, skip_group_check=True)
                e.then_inc(slab_done, 1)

            def mod_products(s, slab, turns):
                ring.wait_landed(pe, slab, turns)
                w = wcols(slab)
                for k in range(KD):
                    g = 32 * (k % 4)
                    e = te.matmul(bank(6)[g:g + 32], cond32[:, k, :], w[:, k, :], start=(k < 4), stop=(k >= 4),
                                  skip_group_check=True)
                e.then_inc(slab_done, 1)

            def mod_columns(s, i):
                pe.wait_ge(mod_rows_copied, i * 6 + (12 * l + s + 1))
                for j in range(4):
                    e = te.matmul(bank(7)[:, bass.ds(i * 24 + (4 * s + j), 1)], mod_rows[:, 128 * j:128 * j + 128],
                                  com("ones")[:, 0:1], start=True, stop=True)
                return e
            pe.wait_ge(h_ready, 2 * l + 2)
            hidden(0, n)
            hidden(1, n + 1)
            down(0, n + 2, start=True)
            pe.wait_ge(cond_ready, 1)
            with pe.Fori(0, 2) as i:
                for jj in range(3):
                    hidden(2 + jj, n + 3 + 4 * jj, i * 2, i * 3)
                    if jj:
                        mod_columns(2 * jj - 1, i)
                    mod_products(2 * jj, n + 4 + 4 * jj, i * 2)
                    down(1 + jj, n + 5 + 4 * jj, i * 2, i * 3)
                    mod_columns(2 * jj, i)
                    mod_products(2 * jj + 1, n + 6 + 4 * jj, i * 2)
                mod_columns(5, i)
            te.matmul(bank(6)[:, 0:1], zeros, com("ones")[:, 0:1], start=True, stop=True).then_inc(mod_done, 1)
            down(NF - 1, n + MLP_SLABS - 1)

        sum_x(0)
        pe.wait_ge(h_ready, 1)
        with pe.Fori(0, GROUPS_A) as g:
            def proj(s):
                n = A_QKV + s
                ring.wait_landed(pe, n, g)
                if s == 1:
                    pe.wait_ge(v_ready, g * 2 + 1)
                elif s >= 2:
                    pe.wait_ge(q_normed, g * 4 + (s - 1))
                if s < 4:
                    feature_major(n, chunks(2 * (s % 2), 4), 4, h3)
                else:
                    token_major(n, 2 * (s % 2), 512).then_inc(slab_done, 1)

            def sums(s):
                pe.wait_ge(q_squared, g * 4 + (s + 1))
                pe.wait_ge(q_root, g * 4 + (s + 1))
                for j in range(2):
                    e = te.matmul(bank(4 + j), com("bd64"), tmp_a[:, 512 * j:512 * j + 512], start=True, stop=True)
                e.then_inc(q_summed, 1)

            def turn(s):
                pe.wait_ge(q_normed, g * 4 + (s + 1))
                pe.wait_ge(q_ready, g * 4 + (s + 1))
                src = qk[:, bass.ds(g, 1), s // 2, 4 * (s % 2):4 * (s % 2) + 4, :].rearrange("p g k t -> p (g k t)")
                for j in range(2):
                    e = te.matmul(bank(6 + j), com("rot16"), src[:, 512 * j:512 * j + 512], start=True, stop=True)
                e.then_inc(q_turned, 1)
            proj(0)
            proj(1)
            sums(0)
            proj(2)
            sums(1)
            turn(0)
            proj(3)
            sums(2)
            turn(1)
            proj(4)
            sums(3)
            turn(2)
            proj(5)
            turn(3)
            pe.wait_ge(v_ready, g * 2 + 2)
        pe.wait_ge(v_ready, 2 * GROUPS_A + 1)
        pe.wait_ge(q_ready, 4 * GROUPS_A + 1)
        with pe.Fori(0, KD) as c:
            def scores(u):
                r, h = u // 2, u % 2
                pe.wait_ge(heads_staged, c + 1)
                if u >= 2:
                    pe.wait_ge(masked, c * 4 + (u - 1))
                rows = slice(64 * h, 64 * h + 64)
                q = slice(r * P, (r + 1) * P)
                te.matmul(bank(h)[:, 0:256], heads_now[rows, 0, 0, q], heads_now[rows, 0, 1, :], start=True, stop=True)
                for g in (1, 2):
                    e = te.matmul(bank(h)[:, 128 + 128 * g:256 + 128 * g], heads_now[rows, g, 0, q],
                                  heads_now[rows, g, 1, q], start=True, stop=True)
                e.then_inc(scored, 1)

            def turn_p(u):
                pe.wait_ge(prob_ready, c * 4 + (u + 1))
                for j in range(4):
                    e = te.transpose(bank(2)[:, 128 * j:128 * j + 128], att_s[u % 2][:, 128 * j:128 * j + 128],
                                     com("ident"))
                e.then_inc(prob_turned, 1)

            def pv(u):
                r, h = u // 2, u % 2
                pe.wait_ge(prob_copied, c * 4 + (u + 1))
                for j, (g, tile) in enumerate(((0, 0), (0, 1), (1, r), (2, r))):
                    v = vA[:, g, tile, bass.ds(c * P + 64 * h, 64)]
                    e = te.matmul(bank(o_bank[u])[:, 0:64], att_t[:, j, :], v, start=(j == 0), stop=(j == 3))
                e.then_inc(pv_done, 1)

            def turn_o(r):
                pe.wait_ge(o_scaled, c * 4 + (2 * r + 2))
                pe.wait_ge(o_copied, c * 2 + (r + 1))
                te.transpose(bank(6)[:, 0:P], o_rows, com("ident")).then_inc(o_turned, 1)
            scores(0)
            scores(1)
            turn_p(0)
            pv(0)
            scores(2)
            turn_p(1)
            pv(1)
            scores(3)
            turn_o(0)
            turn_p(2)
            pv(2)
            turn_p(3)
            pv(3)
            turn_o(1)
            pe.wait_ge(masked, c * 4 + 4)
        pe.wait_ge(o_copied, 2 * KD + 1)
        project_out(A_WO, h3)
        sum_x(1)
        mlp(0, MLP0)
        sum_x(2)
        pe.wait_ge(h_ready, 3)
        for s in range(2):
            for j, (b, sm) in enumerate(((0, c_copied), (2, u_ready), (4, y_ready))):
                ring.wait_landed(pe, B_WIN + 3 * s + j)
                if s:
                    pe.wait_ge(sm, s)
                feature_major(B_WIN + 3 * s + j, chunks(b, 4), 4, h3)
        pe.wait_ge(y_ready, 2)
        project_out(B_WOUT, mixB)
        sum_x(3)
        mlp(1, MLP1)

        with pe.Fori(0, DEPTH) as lay:
            turns = lay * TURNS
            pe.wait_ge(x_ready, lay * 2 + MIN_X)
            sum_x(lay * 2 + MIN_X)
            pe.wait_ge(h_ready, lay * 2 + (MIN_X + 1))

            def win(s):
                b = (0, 3)[s % 2]
                n = WIN + s
                ring.wait_landed(pe, n, turns)
                if s >= 2:
                    pe.wait_ge(win_copied, lay * 7 + (s - 1))
                if s == 0 or s == 2 or s == 3:
                    feature_major(n, chunks(b, 4), 4, h3)
                elif s == 1:
                    token_major(n, b, 256)
                    feature_major(n, chunks(b + 1, 2), 2, h3, c0=256)
                elif s == 4:
                    token_major(n, b, 512).then_inc(slab_done, 1)
                elif s == 5:
                    feature_major(n, chunks(b, 2), 2, h3, signal=False)
                    token_major(n, b + 1, 256, c0=256, rows=64).then_inc(slab_done, 1)
                else:
                    cols = IN_WIDTH - 6 * 512
                    w = wcols(n, cols)
                    for k in range(KD):
                        te.matmul(bank(b)[0:16, 0:S], w[:, k, 0:16], h3[:, k, :], start=(k == 0), stop=(k == KD - 1))
                    feature_major(n, chunks(b + 1, 2), 2, h3, cols=cols, c0=16)

            def qk_mm(name, src):
                src = src.rearrange("p k t -> p (k t)") if len(src.shape) == 3 else src
                m = con2(name) if name == "rot64" else com(name)
                for j in range(2):
                    e = te.matmul(bank(6 + j), m, src[:, 512 * j:512 * j + 512], start=True, stop=True)
                e.then_inc(qk_product, 1)
            win(0)
            win(1)
            pe.wait_ge(win_copied, lay * 7 + 1)
            qk_mm("rot64", rqk)
            win(2)
            win(3)
            pe.wait_ge(dq_squared, lay * 2 + 1)
            pe.wait_ge(qk_ready, lay * 5 + 1)
            qk_mm("bd64", tmp_a)
            win(4)
            pe.wait_ge(qk_ready, lay * 5 + 2)
            qk_mm("rot16", dqk[:, 0:4, :])
            win(5)
            pe.wait_ge(dq_squared, lay * 2 + 2)
            pe.wait_ge(qk_ready, lay * 5 + 3)
            qk_mm("bd64", scratch_b[:, 0:1024])
            win(6)
            pe.wait_ge(qk_ready, lay * 5 + 4)
            qk_mm("rot16", dqk[:, 4:8, :])

            def sum_o(n, width, m, b):
                pe.wait_ge(o_squared, lay * 3 + (n + 1))
                for j in range(width // 512):
                    e = te.matmul(bank(b + j), com(m), tmp_a[:, 512 * j:512 * j + 512], start=True, stop=True)
                e.then_inc(o_summed, 1)
            pe.wait_ge(win_copied, lay * 7 + 7)

            def r_scores(h):
                rows = slice(64 * (h % 2), 64 * (h % 2) + 64)
                if h >= 2:
                    pe.wait_ge(r_decayed, lay * 4 + (h - 1))
                for r in range(NT):
                    e = te.matmul(bank(h % 2)[:, r * S:(r + 1) * S], rqk[rows, 2 + h // 2, r * P:(r + 1) * P],
                                  rqk[rows, h // 2, :], start=True, stop=True)
                e.then_inc(r_scored, 1)

            def r_values(h):
                pe.wait_ge(r_decayed, lay * 4 + (h + 1))
                out = bank(2)[64 * (h % 2):64 * (h % 2) + 64, S * (h // 2):S * (h // 2) + S]
                for r in range(NT):
                    e = te.matmul(out, rv[:, r, 64 * h:64 * h + 64], aT[h % 2][:, r, :], start=(r == 0),
                                  stop=(r == NT - 1))
                e.then_inc(r_used, 1)
            r_scores(0)
            for h in range(1, 4):
                r_scores(h)
                r_values(h - 1)
            r_values(3)
            sum_o(0, 512, "bd64", 3)
            pe.wait_ge(mix_ready, lay * 3 + 2)
            pe.wait_ge(qk_ready, lay * 5 + 5)

            def d_scores(u):
                h, r = u // 2, u % 2
                if u >= 2:
                    pe.wait_ge(d_max, lay * 8 + (u - 1))
                for w in range(2):
                    rows = slice(64 * w, 64 * w + 64)
                    e = te.matmul(bank(2 * (u % 2) + w)[:, 0:S], dqk[rows, h, r * P:(r + 1) * P],
                                  dqk[rows, 4 + h, :], start=True, stop=True)
                e.then_inc(d_scored, 1)

            def d_turn(u):
                pe.wait_ge(d_diff, lay * 8 + (u + 1))
                if u >= 2:
                    pe.wait_ge(d_copied, lay * 8 + (u - 1))
                for k in range(NT):
                    e = te.transpose(bank(6 + u % 2)[:, k * P:(k + 1) * P], att_d[u % 2][:, 0, k * P:(k + 1) * P],
                                     com("ident"))
                e.then_inc(d_turned, 1)

            def d_values(h):
                pe.wait_ge(d_copied, lay * 8 + (2 * h + 2))
                for k in range(NT):
                    e = te.matmul(chunks(4, 4)[:, h, :], dv[:, k, 128 * h:128 * h + 128], aTd[h % 2][:, k, :],
                                  start=(k == 0), stop=(k == NT - 1))
                e.then_inc(d_out, 1)
            d_scores(0)
            for u in range(8):
                if u < 7:
                    d_scores(u + 1)
                d_turn(u)
                if u >= 2 and u % 2 == 0:
                    d_values(u // 2 - 1)
            d_values(3)
            sum_o(1, 1024, "ones", 6)
            for r in range(NT):
                out = bank(0)[:, r * P:(r + 1) * P]
                te.matmul(out, ga[0:16, r * P:(r + 1) * P], par2("wa2")[0:16], start=True, stop=False)
                e = te.matmul(out, com("ones")[0:1, :], par2("ba")[0:1], start=False, stop=True)
            e.then_inc(g_logit, 1)
            pe.wait_ge(g_la, lay + 1)
            for r in range(NT):
                e = te.matmul(bank(1)[:, r * P:(r + 1) * P], la[:, r, :], con2("tri"), start=True, stop=True)
            e.then_inc(g_cum, 1)
            pe.wait_ge(g_keys, lay + 1)
            pe.sem_inc(held, 1)
            for c in range(4):
                e = te.transpose(bank(2)[0:64, c * P:(c + 1) * P], kd[:, 64 * c:64 * c + 64], com("ident"))
            e.then_inc(g_keysT, 1)
            pe.wait_ge(mix_ready, lay * 3 + 3)
            for v in range(16):
                c, t0 = v // 4, 16 * v
                pe.wait_ge(g_dk, lay * 16 + (v + 1))
                if v % 4 == 0 and c >= 2:
                    pe.wait_ge(g_acopy, lay * 4 + (c - 1))
                for i in range(16):
                    at = 4 * (16 * (v % 4) + i)
                    e = te.matmul(bank(4 + c % 2)[0:64, at:at + 4], pair_d[v % 4][:, i, :],
                                  qsel[:, t0 + i, :], start=True, stop=True)
                e.then_inc(g_pair, 1)
            pe.wait_ge(g_keysC, lay + 1)
            for c in range(4):
                t = slice(64 * c, 64 * c + 64)
                pe.wait_ge(g_acopy, lay * 4 + (c + 1))
                pe.wait_ge(g_state, lay * 3 + (c + 1))
                a_c = a_gla[0:64, 256 * c:256 * c + 256].rearrange("p (t h) -> p h t", h=4)
                for j in range(2):
                    out = chunks(6, 2)[:, j, t]
                    te.matmul(out, state[:, 128 * j:128 * j + 128], qe[:, t], start=True, stop=False,
                              skip_group_check=True)
                    for w in range(2):
                        h = 2 * j + w
                        e = te.matmul(chunks(6, 2)[64 * w:64 * w + 64, j, t], gv[0:64, c, 64 * h:64 * h + 64],
                                      a_c[:, h, :], start=False, stop=True, skip_group_check=True)
                if c == 3:
                    e.then_inc(g_out, 1)
                else:
                    te.matmul(bank(7)[:, 0:256], kdt[0:64, c, :], gv[0:64, c, :], start=True, stop=True
                              ).then_inc(g_kv, 1)
            sum_o(2, 512, "bd64", 3)
            pe.wait_ge(mix_ready, lay * 3 + 4)
            project_out(WOUT, h3, turns)
            sum_x(lay * 2 + (MIN_X + 1))
            pe.wait_ge(h_ready, lay * 2 + (MIN_X + 2))
            for r in range(NT):
                for k in range(KD):
                    e = te.matmul(bank(6)[:, r * E:(r + 1) * E], h3[:, k, r * P:(r + 1) * P], router[:, k, :],
                                  start=(k == 0), stop=(k == KD - 1))
            e.then_inc(t_logits, 1)
            for r in range(NT):
                for k in range(KD):
                    e = te.transpose(bank(2 * r, 2)[:, k * P:(k + 1) * P], h3[:, k, r * P:(r + 1) * P], com("ident"))
            e.then_inc(t_rows, 1)
            pe.wait_ge(t_mask, lay + 1)
            both = route[:, 64 + 4 * 64:64 + 5 * 64].rearrange("p (r e) -> p r e", r=NT)
            te.matmul(bank(7)[:, 0:32], con2("before"), both[:, 0, :], start=True, stop=True)
            te.matmul(bank(7)[:, 32:64], con2("before"), both[:, 1, :], start=True, stop=False)
            te.matmul(bank(7)[:, 32:64], com("ones"), both[:, 0, :], start=False, stop=True)
            te.matmul(bank(7)[:, 64:96], com("ones"), both[:, 0, :], start=True, stop=False)
            te.matmul(bank(7)[:, 64:96], com("ones"), both[:, 1, :], start=False, stop=True).then_inc(t_ranks, 1)
            pe.wait_ge(t_diag, lay + 1)
            for j in range(4):
                for r in range(NT):
                    e = te.matmul(chunks(4, 4)[:, j, r * P:(r + 1) * P], com("ones"), diag[:, r, j, :], start=True,
                                  stop=True)
            e.then_inc(t_spread, 1)
            pe.wait_ge(t_rows_copied, lay + 1)
            pe.wait_ge(t_spread_copied, lay + 1)
            for j in range(4):
                te.matmul(bank(j), zeros, hT[:, 0:512], start=True, stop=False, skip_group_check=True)

            base = lay * (PAIRS + 1)

            def gather(pair):
                pe.wait_ge(sel_ready, pair + 1)
                for k in range(KD):
                    for r in range(NT):
                        e = te.matmul(bank(6, 2)[:, P * k:P * k + P], h2tok[:, r, k * P:(k + 1) * P], sel[:, r, :],
                                      start=(r == 0), stop=(r == NT - 1))
                e.then_inc(gathered, 1)

            def scatter(k_th, pair):
                pe.wait_ge(selT_ready, k_th + 1)
                pe.wait_ge(y_copied_a, pair + 1)
                pe.wait_ge(y_copied_v, pair + 1)
                for k in range(KD):
                    e = te.matmul(chunks(0, 8)[:, k, :], ysb[:, k * P:(k + 1) * P], selT,
                                  start=False, stop=False, skip_group_check=True)
                e.then_inc(scattered, 1)

            def expert_pair(n, pair, k_th, turns, m=2):
                pe.wait_ge(xg_copied_a, pair + 1)
                pe.wait_ge(xg_copied_v, pair + 1)
                pe.wait_ge(ue_copied, pair + 1)
                for part in range(2):
                    for h in range(m):
                        ring.wait_landed(pe, n + m * part + h, turns)
                    for k in range(KD):
                        for h in range(m):
                            e = te.matmul(bank(4 + part)[SB * h:SB * h + SB],
                                          xg[:, P * k + SB * h:P * k + SB * h + SB],
                                          wcols(n + m * part + h)[:, k, :], start=(k == 0), stop=(k == KD - 1),
                                          skip_group_check=True)
                            if k == KD - 1:
                                e.then_inc(slab_done, 1)
                scatter(k_th, pair)
                if m == 2:
                    gather(pair + 1)
                pe.wait_ge(ue_ready, pair + 2)
                for j in range(4):
                    e = te.transpose(bank(4)[:, P * j:P * j + P], ue[:, P * j:P * j + P], com("ident"))
                e.then_inc(ue_turned, 1)
                pe.wait_ge(ue_copied, pair + 2)
                if m == 2:
                    pe.wait_ge(xg_copied_a, pair + 2)
                    pe.wait_ge(xg_copied_v, pair + 2)
                for h in range(m):
                    ring.wait_landed(pe, n + 2 * m + h, turns)
                for o in range(2):
                    for k in range(4):
                        for h in range(m):
                            e = te.matmul(bank(6 + o)[SB * h:SB * h + SB],
                                          ueT[:, P * k + SB * h:P * k + SB * h + SB],
                                          wrows(n + 2 * m + h)[:, k, 512 * o:512 * o + 512], start=(k == 0),
                                          stop=(k == 3), skip_group_check=True)
                            if k == 3 and o == 1:
                                e.then_inc(slab_done, 1)
            gather(base)
            with pe.Fori(0, HOME_PAIRS) as i:
                expert_pair(MOE, base + i, lay * (PAIRS + 2) + i, lay * TURNS + i)
            pe.wait_ge(t_table, lay + 1)
            pe.sem_inc(held, 1)
            with pe.If(more_blocks(pe) > 0):
                with pe.Fori(0, OVER_PAIRS) as i:
                    expert_pair(OVERS, base + HOME_PAIRS + i, lay * (PAIRS + 2) + HOME_PAIRS + i,
                                lay * TURNS + i)
                expert_pair(OVERS + 6 * OVER_PAIRS, base + PAIRS, lay * (PAIRS + 2) + PAIRS, lay * TURNS, 1)
            with pe.Else():
                ring.wait_done(pe, OVERS - 1, lay * TURNS)
                pe.sem_inc(slab_done, 3 * OVER)
                pe.sem_inc(gathered, OVER_PAIRS)
                for s in (ue_turned, scattered):
                    pe.sem_inc(s, OVER_PAIRS + 1)
            scatter(lay * (PAIRS + 2) + (PAIRS + 1), base + (PAIRS + 1))

    ctx.close()


def constants():
    f = np.float32
    p = np.arange(P)
    ident = np.eye(P, dtype=f)
    bd64 = (p[:, None] // DH == p[None, :] // DH).astype(f)

    def rot(half):
        m = np.zeros((P, P), f)
        for head in range(0, P, DH):
            for j in range(half):
                m[head + j + half, head + j] = -1
                m[head + j, head + j + half] = 1
        return m
    common = np.concatenate([ident, np.ones((P, P), f), bd64, rot(8)], 1)

    order = np.array([16 * m + 4 * b + a for a in range(4) for b in range(4) for m in range(16)])
    inv = (500000.0 ** (-np.arange(0, 16, 2, dtype=np.float64) / 16)).astype(f)
    ang = (np.arange(S, dtype=f)[order][None, :] * inv[:, None]).astype(f)
    cos_a, sin_a = np.ones((P, S), f), np.zeros((P, S), f)
    for head in range(0, P, DH):
        for half in range(2):
            cos_a[head + 8 * half:head + 8 * half + 8] = np.cos(ang)
            sin_a[head + 8 * half:head + 8 * half + 8] = np.sin(ang)
    mask_a = np.zeros((P, NT, 512), f)
    for r in range(NT):
        q = order[r * P:(r + 1) * P]
        at = 0
        for dil, k in zip(DILATIONS, (order, q, q)):
            far = np.abs(q[:, None] - k[None, :])
            ok = (far % dil == 0) & (far <= RADIUS * dil)
            mask_a[:, r, at:at + len(k)] = np.where(ok, 0, NEG)
            at += len(k)
    const_a = np.concatenate([cos_a, sin_a, mask_a.reshape(P, -1)], 1)

    same = p[:, None] // CHUNK == p[None, :] // CHUNK
    tri = (same & (p[:, None] <= p[None, :])).astype(f) / 16
    before = (p[:, None] < p[None, :]).astype(f)
    bdmask = (p[:, None] // GLA_DK == np.arange(256)[None, :] // 64).astype(f)
    hsel = (p[:, None] // GLA_DK == np.arange(4)[None, :]).astype(f)

    def inverse(half, theta):
        power = np.power(theta, np.arange(half, dtype=np.float64) / half).astype(f)
        return (f(1) / power).astype(f)
    inv_r, inv_d = np.zeros((P, 1), f), np.zeros((P, 1), f)
    for head in range(0, P, DH):
        for half in range(2):
            inv_r[head + 32 * half:head + 32 * half + 32, 0] = inverse(32, 10000.0)
            inv_d[head + 8 * half:head + 8 * half + 8, 0] = inverse(8, 500000.0)
    t = np.arange(S)
    decay = np.zeros((P, 4, NT, S), f)
    for h in range(4):
        g = 1.0 - 2.0 ** (-5.0 - h)
        full = g ** np.abs(t[:, None] - t[None, :]).astype(np.float64) * SCALE
        full = np.where(t[:, None] // CHUNK <= t[None, :] // CHUNK, full, 0)
        decay[:, h] = full.reshape(NT, P, S).transpose(1, 0, 2)
    mask_d = np.where(t[None, :] // CHUNK <= t[:, None] // CHUNK, 0, NEG).astype(f)
    mask_d = mask_d.reshape(NT, P, S).transpose(1, 0, 2)

    def row(n):
        return np.broadcast_to(np.arange(n, dtype=f), (P, n))
    const_2 = np.concatenate([
        rot(32), tri, before, bdmask, hsel, inv_r, inv_d, decay.reshape(P, -1), mask_d.reshape(P, -1),
        row(2 * SB), row(E), row(NG), row(OVER), p[:, None].astype(f)], 1)
    return [np.ascontiguousarray(a, f) for a in (common, const_a, const_2)] + [order]


def by_partition(v):
    return np.asarray(v).reshape(-1, P).T


def kernel(**inputs):
    import concourse.bacc as bacc
    from concourse.bass_utils import run_bass_kernel_spmd

    i = {k: np.asarray(v) for k, v in inputs.items()}
    f = np.float32
    common, const_a, const_2, order = constants()
    x = i["x"][0]
    twice = lambda v: np.tile(v, P // v.shape[0])[:, None]
    param_1 = np.concatenate(
        [by_partition(i["norm1"].reshape(-1)), by_partition(i["norm2"].reshape(-1))]
        + [twice(i[n][0, g]) for g in range(GROUPS_A) for n in ("a_q_gain", "a_k_gain")]
        + [by_partition(i["b_conv"].reshape(-1))], 1)
    param_2 = []
    for l in range(DEPTH):
        lam = np.stack([i[n + "_2"][l] for n in ("lam_q1", "lam_k1", "lam_q2", "lam_k2")]).reshape(1, -1)
        wa2 = np.zeros((P, P), f)
        wa2[:16] = i["gla_w_a2_2"][l]
        param_2.append(np.concatenate([
            by_partition(i["b_mod_2"][l]), by_partition(i["norm1_g_2"][l]), by_partition(i["norm2_g_2"][l]),
            twice(i["ret_norm_g_2"][l]), twice(i["diff_q_g_2"][l]), twice(i["diff_k_g_2"][l]),
            twice(i["diff_sub_g_2"][l]), twice(i["gla_norm_g_2"][l]),
            np.full((P, 1), 1.0 - LAM_INIT[l], f), np.full((P, 1), -LAM_INIT[l], f),
            np.broadcast_to(lam, (P, 4 * DH)), wa2, np.broadcast_to(i["gla_b_a_2"][l], (P, P))], 1))
    param_r = np.concatenate([
        i["router_w_2"].reshape(KD, P, E).transpose(1, 0, 2).reshape(P, -1),
        np.broadcast_to(i["router_b_2"], (P, E))], 1)
    feature_major = lambda a: a.T.reshape(KD, P, S).transpose(1, 0, 2).reshape(P, -1)
    arrays = {
        "x_t": feature_major(x), "x_by_residue": feature_major(x[order]),
        "common": np.concatenate([common, by_partition(i["c_2"][0])], 1), "const_a": const_a, "const_2": const_2,
        "param_1": param_1, "param_2": np.stack(param_2), "param_r": param_r,
        "positions": np.broadcast_to(i["positions_2"], (P, S)),
        "a_wqkv": i["a_wqkv"], "a_wo": i["a_wo"], "b_win": i["b_win"], "b_wout": i["b_wout"],
        "mlp_w1": i["mlp_w1"], "mlp_w2": i["mlp_w2"], "w_mod": i["w_mod_2"], "w_in": i["w_in_2"],
        "w_out": i["w_out_2"], "w_gate": i["w_gate_2"], "w_up": i["w_up_2"], "w_down": i["w_down_2"],
    }
    nc = bacc.Bacc("TRN2", target_bir_lowering=False, num_devices=1)
    arrays = {f"in_{k}": np.ascontiguousarray(a) for k, a in arrays.items()}
    args = [nc.dram_tensor(k, a.shape, mybir.dt.from_np(a.dtype), kind="ExternalInput").ap() for k, a in arrays.items()]
    out = nc.dram_tensor("out", (P, KD * S), F32, kind="ExternalOutput").ap()
    program(nc, *args, out)
    r = run_bass_kernel_spmd(nc, [arrays], core_ids=[0])
    got = np.asarray(r.results[0]["out"])
    return got.reshape(P, KD, S).transpose(2, 1, 0).reshape(1, S, D)
```
